# Optimizing a Trainium2 kernel written in Bass

```python
import math
import jax, jax.numpy as jnp
from jax import lax
import numpy as np

D_MODEL = 1024
BATCH = 1
SEQ = 1024
DEPTH = 1

N_META = 16
D_INNER = 2 * D_MODEL
D_ATTN = D_INNER // 4
D_CONV = D_INNER // 4
D_SSM = D_INNER // 2
ATTN_HEADS = 4
ATTN_QK_DIM = D_ATTN // (2 * ATTN_HEADS)
ATTN_V_DIM = 2 * ATTN_QK_DIM
SCONV_WIDTH = 3
SSM_HEAD_DIM = 64
SSM_HEADS = D_SSM // SSM_HEAD_DIM
SSM_GROUPS = 4
SSM_STATE = 128
SSM_CONV_WIDTH = 4
SSM_CONV_DIM = D_SSM + 2 * SSM_GROUPS * SSM_STATE
CHUNK = 128
N_PAD = CHUNK - N_META
NORM_EPS = 1e-5
MASK_VALUE = -1e30
IN_SPLIT_SIZES = (D_ATTN, D_ATTN, D_ATTN, D_ATTN,
                  D_CONV, D_CONV, D_CONV, D_CONV,
                  D_SSM, SSM_CONV_DIM, SSM_HEADS)
N_IN = sum(IN_SPLIT_SIZES)
IN_SPLIT_POINTS = tuple(int(s) for s in np.cumsum(IN_SPLIT_SIZES)[:-1])

kernel_name = "hybrid_diffattn_shortconv_ssd_meta"

def rmsnorm(x, w):
    xf = x.astype(jnp.float32)
    y = xf * lax.rsqrt(jnp.mean(xf * xf, axis=-1, keepdims=True) + NORM_EPS)
    return (y * w.astype(jnp.float32)).astype(x.dtype)

def gated_group_rmsnorm(y, z, w):
    u = (y.astype(jnp.float32) * jax.nn.silu(z.astype(jnp.float32)))
    shp = u.shape
    u = u.reshape(shp[:-1] + (SSM_GROUPS, shp[-1] // SSM_GROUPS))
    u = u * lax.rsqrt(jnp.mean(u * u, axis=-1, keepdims=True) + NORM_EPS)
    return (u.reshape(shp) * w.astype(jnp.float32)).astype(z.dtype)

def causal_dwconv(u, w):
    k, c = w.shape
    return lax.conv_general_dilated(
        u, w[:, None, :].astype(u.dtype), window_strides=(1,), padding=[(k - 1, 0)],
        dimension_numbers=('NWC', 'WIO', 'NWC'), feature_group_count=c)

def pad_front(a):
    return jnp.pad(a, [(0, 0), (N_PAD, 0)] + [(0, 0)] * (a.ndim - 2))

def diff_attention(q, k, v, lam):
    b, lp = q.shape[:2]
    nblk = lp // CHUNK
    scale = ATTN_QK_DIM ** -0.5
    kpos = jnp.arange(lp)
    qb = q.reshape(b, nblk, CHUNK, ATTN_HEADS, 2, ATTN_QK_DIM).swapaxes(0, 1)
    starts = jnp.arange(nblk) * CHUNK

    def one_block(args):
        qi, s0 = args
        qpos = s0 + jnp.arange(CHUNK)
        mask = (kpos[None, :] <= qpos[:, None]) & (kpos[None, :] >= N_PAD)
        s = jnp.einsum('bqhmd,bkhmd->bhmqk', qi, k).astype(jnp.float32) * scale
        p = jax.nn.softmax(jnp.where(mask, s, MASK_VALUE), axis=-1)
        a = p[:, :, 0] - lam * p[:, :, 1]
        return jnp.einsum('bhqk,bkhe->bqhe', a.astype(v.dtype), v)

    o = lax.map(one_block, (qb, starts))
    return o.swapaxes(0, 1).reshape(b, lp, ATTN_HEADS, ATTN_V_DIM)

def diff_attention_branch(q, k, v, lam_params, sub_norm_w, layer):
    b, l = q.shape[:2]
    lam_init = 0.8 - 0.6 * math.exp(-0.3 * layer)
    lp = lam_params.astype(jnp.float32)
    lam = jnp.exp(jnp.sum(lp[0] * lp[1])) - jnp.exp(jnp.sum(lp[2] * lp[3])) + lam_init
    q = pad_front(q.reshape(b, l, ATTN_HEADS, 2, ATTN_QK_DIM))
    k = pad_front(k.reshape(b, l, ATTN_HEADS, 2, ATTN_QK_DIM))
    v = pad_front(v.reshape(b, l, ATTN_HEADS, ATTN_V_DIM))
    o = diff_attention(q, k, v, lam)[:, N_PAD:]
    o = rmsnorm(o, sub_norm_w) * (1.0 - lam_init)
    return o.reshape(b, l, D_ATTN)

def short_conv_branch(gate_b, gate_c, hin, conv_w):
    return gate_b * causal_dwconv(gate_c * hin, conv_w)

def ssd_scan(x, dt, a, bm, cm):
    b, lp, nh, p = x.shape
    g, n = bm.shape[-2:]
    r = nh // g
    c = lp // CHUNK
    xc = (x.astype(jnp.float32) * dt[..., None]).reshape(b, c, CHUNK, g, r, p)
    bc = bm.astype(jnp.float32).reshape(b, c, CHUNK, g, n)
    cc = cm.astype(jnp.float32).reshape(b, c, CHUNK, g, n)
    adt = jnp.transpose((a * dt).reshape(b, c, CHUNK, g, r), (0, 1, 3, 4, 2))
    acum = jnp.cumsum(adt, axis=-1)
    causal = jnp.tril(jnp.ones((CHUNK, CHUNK), dtype=bool))
    seg = acum[..., :, None] - acum[..., None, :]
    lmat = jnp.exp(jnp.where(causal, seg, -jnp.inf))
    cb = jnp.einsum('bclgn,bcsgn->bcgls', cc, bc)
    y_diag = jnp.einsum('bcgls,bcgrls,bcsgrp->bclgrp', cb, lmat, xc)
    decay_s = jnp.exp(acum[..., -1:] - acum)
    states = jnp.einsum('bclgn,bcgrl,bclgrp->bcgrpn', bc, decay_s, xc)
    chunk_decay = jnp.exp(acum[..., -1])

    def step(carry, inp):
        st, dec = inp
        return carry * dec[..., None, None] + st, carry

    init = jnp.zeros((b, g, r, p, n), jnp.float32)
    _, prev = lax.scan(step, init, (states.swapaxes(0, 1), chunk_decay.swapaxes(0, 1)))
    prev = prev.swapaxes(0, 1)
    y_off = jnp.einsum('bclgn,bcgrpn,bcgrl->bclgrp', cc, prev, jnp.exp(acum))
    return (y_diag + y_off).reshape(b, lp, nh, p)

def ssd_branch(z, xbc, dt_raw, conv_w, conv_b, a_log, dt_bias, d_skip, norm_w):
    b, l = z.shape[:2]
    xbc = jax.nn.silu(causal_dwconv(xbc, conv_w) + conv_b.astype(xbc.dtype))
    xs, bm, cm = jnp.split(xbc, [D_SSM, D_SSM + SSM_GROUPS * SSM_STATE], axis=-1)
    xs = xs.reshape(b, l, SSM_HEADS, SSM_HEAD_DIM)
    bm = bm.reshape(b, l, SSM_GROUPS, SSM_STATE)
    cm = cm.reshape(b, l, SSM_GROUPS, SSM_STATE)
    dt = jax.nn.softplus(dt_raw.astype(jnp.float32) + dt_bias.astype(jnp.float32))
    a = -jnp.exp(a_log.astype(jnp.float32))
    y = ssd_scan(pad_front(xs), pad_front(dt), a, pad_front(bm), pad_front(cm))[:, N_PAD:]
    y = y + xs.astype(jnp.float32) * d_skip.astype(jnp.float32)[:, None]
    return gated_group_rmsnorm(y.reshape(b, l, D_SSM), z, norm_w)

def setup_inputs(seed: int = 0) -> dict:
    key = jax.random.key(seed)
    ks = jax.random.split(key, 16)
    nrm = jax.random.normal
    dt0 = jnp.exp(jax.random.uniform(ks[11], (DEPTH, SSM_HEADS), minval=math.log(1e-3), maxval=math.log(1e-1)))
    return {
        "x": nrm(ks[0], (BATCH, SEQ, D_MODEL), jnp.float32),
        "meta_tokens": nrm(ks[1], (N_META, D_MODEL), jnp.float32),
        "norm_w": 1.0 + 0.02 * nrm(ks[2], (DEPTH, D_MODEL), jnp.float32),
        "w_in": nrm(ks[3], (DEPTH, D_MODEL, N_IN), jnp.float32) * D_MODEL ** -0.5,
        "w_out": nrm(ks[4], (DEPTH, D_INNER, D_MODEL), jnp.float32) * D_INNER ** -0.5,
        "attn_lambda": 0.1 * nrm(ks[5], (DEPTH, 4, ATTN_QK_DIM), jnp.float32),
        "attn_norm_w": 1.0 + 0.02 * nrm(ks[6], (DEPTH, ATTN_V_DIM), jnp.float32),
        "sconv_w": nrm(ks[7], (DEPTH, SCONV_WIDTH, D_CONV), jnp.float32) * SCONV_WIDTH ** -0.5,
        "ssm_conv_w": nrm(ks[8], (DEPTH, SSM_CONV_WIDTH, SSM_CONV_DIM), jnp.float32) * SSM_CONV_WIDTH ** -0.5,
        "ssm_conv_b": 0.02 * nrm(ks[9], (DEPTH, SSM_CONV_DIM), jnp.float32),
        "ssm_a_log": jnp.log(jax.random.uniform(ks[10], (DEPTH, SSM_HEADS), minval=1.0, maxval=16.0)),
        "ssm_dt_bias": dt0 + jnp.log(-jnp.expm1(-dt0)),
        "ssm_d": 1.0 + 0.02 * nrm(ks[12], (DEPTH, SSM_HEADS), jnp.float32),
        "ssm_norm_w": 1.0 + 0.02 * nrm(ks[13], (DEPTH, D_SSM), jnp.float32),
        "final_norm_w": 1.0 + 0.02 * nrm(ks[14], (D_MODEL,), jnp.float32),
    }

def reference(x, meta_tokens, norm_w, w_in, w_out, attn_lambda, attn_norm_w, sconv_w,
              ssm_conv_w, ssm_conv_b, ssm_a_log, ssm_dt_bias, ssm_d, ssm_norm_w, final_norm_w):
    b = x.shape[0]
    meta = jnp.broadcast_to(meta_tokens.astype(x.dtype)[None], (b, N_META, D_MODEL))
    h = jnp.concatenate([meta, x], axis=1)
    for layer in range(DEPTH):
        u = rmsnorm(h, norm_w[layer])
        proj = jnp.einsum('bld,de->ble', u, w_in[layer])
        (q, k, v, g_attn, c_b, c_c, c_h, g_conv, z, xbc, dt) = jnp.split(proj, IN_SPLIT_POINTS, axis=-1)
        y_attn = diff_attention_branch(q, k, v, attn_lambda[layer], attn_norm_w[layer], layer) * jax.nn.silu(g_attn)
        y_conv = short_conv_branch(c_b, c_c, c_h, sconv_w[layer]) * jax.nn.silu(g_conv)
        y_ssm = ssd_branch(z, xbc, dt, ssm_conv_w[layer], ssm_conv_b[layer], ssm_a_log[layer],
                           ssm_dt_bias[layer], ssm_d[layer], ssm_norm_w[layer])
        y = jnp.concatenate([y_attn, y_conv, y_ssm], axis=-1)
        h = h + jnp.einsum('ble,ed->bld', y, w_out[layer])
    return rmsnorm(h, final_norm_w)[:, N_META:]


_drawn_inputs = setup_inputs


def setup_inputs(seed=0):
    import zlib

    import numpy as np

    out = dict(_drawn_inputs(seed))
    spreads = {}
    factors = {'norm_w': 2.699,
     'attn_lambda': 23.9,
     'attn_norm_w': 64.0,
     'ssm_conv_b': 29.152,
     'ssm_d': 64.0,
     'ssm_norm_w': 39.976,
     'final_norm_w': 8.251}
    for name, (base, spread) in spreads.items():
        noise = np.random.default_rng([zlib.crc32(name.encode()), seed]).standard_normal(out[name].shape)
        drawn = base * np.exp(spread * noise) if base else spread * noise
        out[name] = __import__('jax').numpy.asarray(drawn.astype(out[name].dtype))
    for name, factor in factors.items():
        out[name] = (out[name] * factor).astype(out[name].dtype)
    return out
```

```python
import math
from contextlib import ExitStack

import numpy as np

import concourse.bass as bass
from concourse import mybir

F32 = mybir.dt.float32
F32R = mybir.dt.float32r
BF16 = mybir.dt.bfloat16
ALU = mybir.AluOpType
ACT = mybir.ActivationFunctionType
AX = mybir.AxisListType

P = 128
D = 1024
T = 1024
META = 16
L = META + T
PIECES = 3
PW = 348
LP = PIECES * PW
KD = D // P
N_IN = 7184
HEADS = 4
QK = 64
QB = T // P
CH = QB + 1
SH = 16
R = SH // HEADS
HD = 64
GW = R * HD
XT = D // P
KO = 2 * D // P
HALF = D // 2
EPS = 1e-5
LAM_INIT = 0.8 - 0.6 * math.exp(-0.3 * 0)
MASK = -1e30
O_TOP = 2.0 ** 64

C_Q, C_K, C_V, C_G, C_CB, C_CC, C_CH, C_GC = (512 * n for n in range(8))
C_Z, C_XS, C_B, C_C, C_DT = 4096, 5120, 6144, 6656, 7168

TILES = [(C_Q, P), (C_K, P), (C_V, P), (C_G, P), (C_XS, GW), (C_XS + P, GW), (C_B, P), (C_C, P),
         (C_CB, P), (C_CC, P), (C_CH, P), (C_GC, P), (C_Z, GW), (C_Z + P, GW)]
NT = len(TILES)
(TQ, TK, TV, TG, TXS0, TXS1, TB, TC, TCB, TCC, TCH, TGC, TZ0, TZ1) = range(NT)
NP = TZ0 * PIECES
PPI = NP + QB

R_CW, R_CB, R_SW, R_SN, R_NW, R_AN, R_END = 0, 64, 80, 92, 100, 108, 109


def schedule():
    out = [("load", 0), ("load", 1), ("split", 0), ("params", 0)]
    piece = iter(range(NP))

    def pieces(n):
        for _ in range(n):
            p = next(piece, None)
            if p is None:
                return
            t, tc = divmod(p, PIECES)
            if tc == 0:
                if t + 2 < NT:
                    out.append(("load", t + 2))
                out.append(("split", t + 1))
            out.append(("piece", p))
            if tc == PIECES - 1 and TXS0 <= t <= TC:
                out.append(("taps", t))
            if tc == 1 and TXS0 < t <= TC + 1:
                out.append(("gate_taps", t - 1))
            if p == TV * PIECES + 3:
                out.append(("turn_v", 0))

    pieces(TCB * PIECES)
    for s in range(QB + 1):
        if s < QB:
            out.append(("scores", (s, 0)))
        if s > 0:
            out.append(("turn", s - 1))
        pieces(1)
        if s < QB:
            out.append(("scores", (s, 1)))
            out.append(("mix", s))
        if s > 0:
            out.append(("values", s - 1))
        pieces(1 if s % 3 == 0 or s == QB else 0)
        if s > 0:
            out.append(("attn_out", s - 1))
    out += [("store_attn", 0), ("split", TZ1)] + [("decay", 1), ("chunk", 0)]
    for c in range(1, CH):
        if c + 1 < CH:
            out.append(("decay", c + 1))
        out += [("chunk", c), ("z", c), ("scan", c - 1)]
        if c == 1:
            out.append(("conv", 0))
        if c > 2:
            out.append(("ssm_out", c - 2))
    out += [("scan", CH - 1), ("ssm_out", CH - 2), ("ssm_out", CH - 1), ("store_ssm", 0)]
    return [s for n, s in enumerate(out) if s not in out[:n]]


STEPS = schedule()


class Chain:

    def __init__(self, sem, per):
        self.sem, self.per, self.base, self.n = sem, per, 0, 0

    def enter(self, i):
        self.base, self.n = self.n + i * self.per, 0

    def leave(self, base, iterations):
        assert self.n == self.per, (self.sem, self.n)
        self.base, self.n = 0, base + iterations * self.per

    def __call__(self, eng, ins):
        self.n += 1
        ins.then_inc(self.sem, 1)
        eng.wait_ge(self.sem, self.base + self.n)


def token_cols(c):
    return (0, META) if c == 0 else (META + P * (c - 1), META + P * c)


def build(nc, x, meta_tokens, norm_w, w_in, w_out, attn_lambda, attn_norm_w, sconv_w, ssm_conv_w,
          ssm_conv_b, ssm_a_log, ssm_dt_bias, ssm_d, ssm_norm_w, final_norm_w, out, y_dram, acum_dram):
    x_rows = x.rearrange("b t d -> (b t) d")
    out_rows = out.rearrange("b t d -> (b t) d")
    w_in_t = w_in.rearrange("a (k p) n -> p (a k) n", p=P)
    w_out_rows = w_out.rearrange("a k n -> (a k) n")

    with ExitStack() as ctx:
        def sb(name, shape, dt=F32):
            return ctx.enter_context(nc.sbuf_tensor(name, shape, dt))

        def sem(name):
            return ctx.enter_context(nc.semaphore(name))

        u_hi = sb("u_hi", [P, KD, LP], F32R)
        u_lo = sb("u_lo", [P, KD, LP], F32R)
        w_raw = sb("w_raw", [P, 2, KD, P])
        w_hi = sb("w_hi", [P, 2, KD, P], F32R)
        w_lo = sb("w_lo", [P, 2, KD, P], F32R)
        wd_raw, wd_hi, wd_lo = (w[:, 1, :, 0:SH] for w in (w_raw, w_hi, w_lo))

        work = sb("work", [P, 12528])
        taken = [0]

        def part(n):
            taken[0] += n
            return work[:, taken[0] - n:taken[0]]

        q_map = [part(LP), part(LP)]
        k_t = part(LP)
        v_t = part(LP)
        gate = part(LP)
        prob = [part(L), part(L)]
        xs_flat = part(2 * LP)
        xs = xs_flat.rearrange("p (t n) -> p t n", t=2)
        dt_row = xs_flat[0:SH, 0:CH * P]
        b_t = part(LP)
        c_t = part(LP)
        raw = part(3 + LP)
        h_res = work[:, 0:QB * D].rearrange("p (t d) -> p t d", t=QB)
        y_raw = work[:, QB * D:QB * D + 2 * T].rearrange("p (b n) -> p b n", b=2)
        w_fin = work[:, QB * D + 2 * T:QB * D + 2 * T + D]
        assert QB * D + 2 * T + D <= taken[0] <= 12528
        y_hi = u_hi[:, :, :].rearrange("p k n -> p (k n)")[:, 0:2 * T].rearrange("p (b n) -> p b n", b=2)
        y_lo = u_lo[:, :, :].rearrange("p k n -> p (k n)")[:, 0:2 * T].rearrange("p (b n) -> p b n", b=2)
        wo_raw = w_raw[:, :, :, :].rearrange("p b k n -> p b (k n)")[:, :, 0:HALF]
        wo_hi = w_hi[:, :, :, :].rearrange("p b k n -> p b (k n)")[:, :, 0:HALF]
        wo_lo = w_lo[:, :, :, :].rearrange("p b k n -> p b (k n)")[:, :, 0:HALF]

        th_tile = sb("th_tile", [P, LP])
        th_piece = sb("th_piece", [P, 2, PW])
        v_blk = sb("v_blk", [P, QB, P])
        a_t = sb("a_t", [P, QB, P])
        a_meta = th_tile[0:META, 512:512 + P]
        conv_b_s = sb("conv_b_s", [P, LP])
        conv_u = sb("conv_u", [P, 2 + LP])
        conv_g = sb("conv_g", [P, LP])
        conv_y = sb("conv_y", [P, T])
        acum_b = sb("acum_b", [P, 2, R, P])
        lmat = sb("lmat", [P, 2, R, P])
        xdt = sb("xdt", [P, 2, GW])
        xdd = sb("xdd", [P, 2, GW])
        xd = sb("xd", [P, 2, GW])
        b_n = sb("b_n", [P, 2, P])
        cbm = sb("cbm", [P, 2, P])
        state = sb("state", [P, GW])
        state_d = sb("state_d", [P, GW])
        y_a = sb("y_a", [P, GW])
        v_meta = y_a[0:META, 0:P]
        o_n = y_a[:, P:2 * P]
        y_n = sb("y_n", [P, 2, GW])
        z_n = sb("z_n", [P, 2, GW])
        ys = sb("ys", [P, 2, T])

        ident = sb("ident", [P, P])
        ident_b = sb("ident_b", [P, P], BF16)
        mask_b = sb("mask_b", [P, P], BF16)
        tri = sb("tri", [P, P])
        ones = sb("ones", [P, P])
        valid = sb("valid", [P, 1])
        m_half = sb("m_half", [P, 1])
        rows = conv_g[:, 0:P]
        par = sb("par", [P, R_END])
        par_cw = sb("par_cw", [P, 4, 4])
        par_cb = sb("par_cb", [P, 4])
        par_cbh = sb("par_cbh", [P, 4])
        par_sw = sb("par_sw", [P, 3])
        par_sn = sb("par_sn", [P, 2])
        a_norm = sb("a_norm", [P, 1])
        lam_in = conv_b_s[0:1, 0:4 * QK].rearrange("p (r d) -> p r d", r=4)
        lam_p = conv_b_s[0:1, 4 * QK:6 * QK].rearrange("p (r d) -> p r d", r=2)
        lam_s = sb("lam_s", [1, 8])
        n_lam = sb("n_lam", [P, 1])
        dt_bias = sb("dt_bias", [SH, 1])
        a_bc = sb("a_bc", [P, SH])
        d_bc = sb("d_bc", [P, SH])
        sp = conv_y[:, 0:6 * CH * SH].rearrange("p (s n) -> p s n", s=6)
        stat = sb("stat", [P, 5, CH, SH])
        sg = sb("sg", [P, 5, CH, R])
        small = sb("small", [P, 96])
        used = [0]

        def few(n):
            used[0] += n
            return small[:, used[0] - n:used[0]]

        dg = few(R)
        ss = few(2)
        ms = few(2)
        rs = few(2)
        mx = few(2)
        psum_e = few(4).rearrange("p (b m) -> p b m", b=2)
        rinv = few(4).rearrange("p (b m) -> p b m", b=2)
        cmix = few(1)
        o_ss = few(1)
        o_ms = few(1)
        o_fit = few(1)
        o_rs = few(1)
        z_ss = few(2)
        z_ms = few(2)
        z_rs = few(2)
        f_ss = few(QB)
        f_ms = few(QB)
        f_rs = few(QB)

        ps = ctx.enter_context(nc.psum_tensor("ps", [P, 8, 512], F32))
        pb = [ps[:, 0, :], ps[:, 1, :]]
        s_ps = ps[:, 2:5, :].rearrange("p b n -> p (b n)")
        t_ps = [ps[:, 5, :], ps[:, 6, :]]
        o_ps = ps[:, 7, :]
        x_ps = [ps[:, 2, :], ps[:, 3, :]]
        y_ps = [ps[:, 4, :], ps[:, 5, :]]
        st_ps = ps[:, 6, :]
        yt_ps = ps[:, 7, :]
        u_ps = [ps[:, 2:4, :].rearrange("p b n -> p (b n)"), ps[:, 5:7, :].rearrange("p b n -> p (b n)")]

        params_in = sem("params_in")
        x_in = [sem("x_in0"), sem("x_in1")]
        consts = sem("consts")
        x_sq = sem("x_sq")
        x_ms = sem("x_ms")
        x_rs = sem("x_rs")
        x_n = sem("x_n")
        x_tr = sem("x_tr")
        u_prod = sem("u_prod")
        u_hi_ok = sem("u_hi_ok")
        u_lo_ok = sem("u_lo_ok")
        par_tr = sem("par_tr")
        par_ok = sem("par_ok")
        lam_sum = sem("lam_sum")
        lam_exp = sem("lam_exp")
        lam_row = sem("lam_row")
        lam_pe = sem("lam_pe")
        lam_ok = sem("lam_ok")
        wd_in = sem("wd_in")
        dt_pe = sem("dt_pe")
        dt_row_ok = sem("dt_row_ok")
        dt_tr = sem("dt_tr")
        dt_x = sem("dt_x")
        dt_e = sem("dt_e")
        adt_ok = sem("adt_ok")
        cum_pe = sem("cum_pe")
        acum_ok = sem("acum_ok")
        acum_tr = sem("acum_tr")
        acum_row = sem("acum_row")
        acum_st = sem("acum_st")
        stat_x = sem("stat_x")
        stat_e = sem("stat_e")
        stat_ok = sem("stat_ok")
        w_in_ok = [sem("w_in_ok0"), sem("w_in_ok1")]
        w_hi_ok = sem("w_hi_ok")
        w_lo_ok = sem("w_lo_ok")
        piece_done = sem("piece_done")
        bank_free = [sem("bank_free0"), sem("bank_free1")]
        q_ok = sem("q_ok")
        k_ok = sem("k_ok")
        v_ok = sem("v_ok")
        th_ok = sem("th_ok")
        gate_ok = sem("gate_ok")
        raw_ok = sem("raw_ok")
        raw_free = sem("raw_free")
        thc_ok = sem("thc_ok")
        conv_ok = sem("conv_ok")
        v_tr = sem("v_tr")
        v_blk_ok = sem("v_blk_ok")
        v_meta_ok = sem("v_meta_ok")
        s_done = sem("s_done")
        max_ok = sem("max_ok")
        exp_ok = sem("exp_ok")
        mix_ok = sem("mix_ok")
        a_tr = sem("a_tr")
        a_t_ok = sem("a_t_ok")
        a_m_ok = sem("a_m_ok")
        o_done = sem("o_done")
        o_sq = sem("o_sq")
        o_c_ok = sem("o_c_ok")
        o_ms_ok = sem("o_ms_ok")
        o_rs_ok = sem("o_rs_ok")
        o_n_ok = sem("o_n_ok")
        o_tr = sem("o_tr")
        attn_ok = sem("attn_ok")
        attn_st = sem("attn_st")
        convg_ok = sem("convg_ok")
        convg_st = sem("convg_st")
        acum_in = [sem("acum_in0"), sem("acum_in1")]
        seg_ok = sem("seg_ok")
        l_ok = sem("l_ok")
        sg_ok = sem("sg_ok")
        x_done = sem("x_done")
        xdt_ok = sem("xdt_ok")
        x_free = sem("x_free")
        xdd_ok = sem("xdd_ok")
        g_ok = sem("g_ok")
        scan_done = sem("scan_done")
        sd_ok = sem("sd_ok")
        state_ok = sem("state_ok")
        zth_ok = sem("zth_ok")
        y_gated = sem("y_gated")
        z_sq = sem("z_sq")
        z_ms_ok = sem("z_ms_ok")
        z_rs_ok = sem("z_rs_ok")
        y_n_ok = sem("y_n_ok")
        y_tr = sem("y_tr")
        ys_ok = sem("ys_ok")
        ssm_st = sem("ssm_st")
        yw_in = [sem("yw_in0"), sem("yw_in1")]
        yw_hi = sem("yw_hi")
        y_lo_ok = sem("y_lo_ok")
        wo_lo_ok = sem("wo_lo_ok")
        out_k = sem("out_k")
        x_res = sem("x_res")
        out_bank = sem("out_bank")
        h_ok = sem("h_ok")
        f_sq = sem("f_sq")
        f_ms_ok = sem("f_ms_ok")
        f_rs_ok = sem("f_rs_ok")
        f_ok = sem("f_ok")
        out_st = sem("out_st")
        dve_own = Chain(sem("dve_own"), 89)
        act_own = Chain(sem("act_own"), 0)
        pool_own = Chain(sem("pool_own"), 0)


        primed = [a_m_ok, a_t_ok, a_tr, attn_ok, conv_ok, exp_ok, g_ok, mix_ok, o_ms_ok, o_sq, out_k, piece_done, raw_free, s_done, scan_done, seg_ok, state_ok, v_tr, w_lo_ok, wo_lo_ok, x_free, xdd_ok, y_gated, y_lo_ok, y_tr, ys_ok, z_ms_ok, *bank_free]
        primed_dma = [attn_st, convg_st, ssm_st]

        block = ctx.enter_context(nc.Block())

        @block.sync
        def _(eng):
            def load_x(r):
                if r >= 2:
                    eng.wait_ge(x_tr, r - 1)
                if r == 0:
                    eng.dma_start(prob[0][0:META, 0:D], meta_tokens).then_inc(x_in[0], 16)
                else:
                    eng.dma_start(prob[r % 2][:, 0:D], x_rows[(r - 1) * P:r * P, :]).then_inc(x_in[r % 2], 16)

            for guard in primed:
                eng.sem_inc(guard, 1)
            for guard in primed_dma:
                eng.sem_inc(guard, 16)
            load_x(0)
            load_x(1)
            eng.dma_start(rows[R_CW:R_CB, :], ssm_conv_w.rearrange("a j (t c) -> (a j t) c", c=P)).then_inc(params_in, 16)
            eng.dma_start(rows[R_CB:R_SW, :], ssm_conv_b.rearrange("a (t c) -> (a t) c", c=P)).then_inc(params_in, 16)
            eng.dma_start(rows[R_SW:R_SN, :], sconv_w.rearrange("a j (t c) -> (a j t) c", c=P)).then_inc(params_in, 16)
            eng.dma_start(rows[R_SN:R_NW, :], ssm_norm_w.rearrange("a (t c) -> (a t) c", c=P)).then_inc(params_in, 16)
            eng.dma_start(rows[R_NW:R_AN, :], norm_w.rearrange("a (t c) -> (a t) c", c=P)).then_inc(params_in, 16)
            eng.dma_start(rows[R_AN:R_END, :], attn_norm_w).then_inc(params_in, 16)
            eng.dma_start(lam_in[:, :, :], attn_lambda).then_inc(params_in, 16)
            eng.dma_start(dt_bias[:, :], ssm_dt_bias.rearrange("a h -> h a")).then_inc(params_in, 16)
            eng.dma_start(a_bc[:, :], ssm_a_log[0, :].partition_broadcast(P)).then_inc(params_in, 16)
            eng.dma_start(d_bc[:, :], ssm_d[0, :].partition_broadcast(P)).then_inc(params_in, 16)
            eng.dma_start(wd_raw, w_in_t[:, :, C_DT:C_DT + SH]).then_inc(wd_in, 16)
            for r in range(2, CH):
                load_x(r)
            eng.wait_ge(acum_row, 1)
            eng.dma_start(acum_dram, dt_row[:, :]).then_inc(acum_st, 16)
            eng.wait_ge(acum_st, 16)
            with eng.Fori(0, HEADS) as i:
                for step, a in STEPS:
                    if step == "load":
                        at, by = TILES[a]
                        eng.wait_ge(w_lo_ok, i * NT + a + 1)
                        eng.dma_start(w_raw[:, a % 2, :, :], w_in_t[:, :, bass.ds(i * by + at, P)]).then_inc(w_in_ok[a % 2], 16)
                    elif step == "store_attn":
                        eng.wait_ge(attn_ok, i * QB + QB + 1)
                        eng.dma_start(y_dram[bass.ds(i * P, P), :], gate[:, META:L]).then_inc(attn_st, 16)
                    elif step == "conv":
                        eng.wait_ge(convg_ok, i + 1)
                        eng.dma_start(y_dram[bass.ds(i * P + HEADS * P, P), :], conv_y[:, :]).then_inc(convg_st, 16)
                    elif step == "decay":
                        eng.wait_ge(seg_ok, i * QB + max(a - 2, 0) + 1)
                        eng.dma_start(acum_b[:, a % 2, :, :],
                                      acum_dram[bass.ds(i * R, R), a * P:(a + 1) * P].partition_broadcast(P)).then_inc(acum_in[a % 2], 16)
                    elif step == "store_ssm":
                        eng.wait_ge(ys_ok, i * QB + QB + 1)
                        for t in range(2):
                            eng.dma_start(y_dram[bass.ds(i * GW + (2 * HEADS + t) * P, P), :], ys[:, t, :]).then_inc(ssm_st, 16)
            eng.wait_ge(attn_st, 16 * HEADS + 16)
            eng.wait_ge(convg_st, 16 * HEADS + 16)
            eng.wait_ge(ssm_st, 32 * HEADS + 16)
            eng.wait_ge(scan_done, HEADS * CH + 1)
            eng.dma_start(h_res, x_rows.rearrange("(t p) d -> p t d", p=P)).then_inc(x_res, 16)
            eng.dma_start(w_fin, final_norm_w.partition_broadcast(P)).then_inc(x_res, 16)

            def load_k(half, j, first):
                for b in range(2):
                    n = half * KO + 2 * j + b
                    if not first:
                        eng.wait_ge(y_lo_ok, n - 1 + 1)
                        eng.wait_ge(wo_lo_ok, n - 1 + 1)
                    eng.dma_start(y_raw[:, b, :], y_dram[bass.ds((2 * j + b) * P, P), :]).then_inc(yw_in[b], 16)
                    eng.dma_start(wo_raw[:, b, :], w_out_rows[bass.ds((2 * j + b) * P, P), bass.ds(half * HALF, HALF)]).then_inc(yw_in[b], 16)

            load_k(0, 0, True)
            with eng.Fori(1, KO // 2) as j:
                load_k(0, j, False)
            with eng.Fori(0, KO // 2) as j:
                load_k(1, j, False)
            for t in range(QB):
                eng.wait_ge(f_ok, t + 1)
                eng.dma_start(out_rows[t * P:(t + 1) * P, :], h_res[:, t, :]).then_inc(out_st, 16)
            eng.wait_ge(out_st, 16 * QB)

        @block.gpsimd
        def _(eng):
            own = pool_own
            own(eng, eng.memset(ident[:, :], 0.0))
            own(eng, eng.memset(mask_b[:, :], 0.0))
            own(eng, eng.memset(tri[:, :], 1.0))
            own(eng, eng.memset(valid[:, :], 1.0))
            eng.affine_select(out=ident[:, :], in_=ident[:, :], compare_op=ALU.not_equal, fill=1.0, base=0,
                              pattern=[[-1, P]], channel_multiplier=1).then_inc(consts, 1)
            eng.affine_select(out=mask_b[:, :], in_=mask_b[:, :], compare_op=ALU.is_ge, fill=MASK, base=0,
                              pattern=[[-1, P]], channel_multiplier=1).then_inc(consts, 1)
            if True:
                eng.affine_select(out=tri[:, :], in_=tri[:, :], compare_op=ALU.is_ge, fill=0.0, base=0,
                                  pattern=[[1, P]], channel_multiplier=-1).then_inc(consts, 1)
            eng.affine_select(out=valid[:, :], in_=valid[:, :], compare_op=ALU.is_ge, fill=0.0, base=META - 1,
                              pattern=[[0, 1]], channel_multiplier=-1).then_inc(consts, 1)
            eng.memset(ones[:, :], 1.0).then_inc(consts, 1)
            eng.memset(m_half[:, :], -0.5).then_inc(consts, 1)
            eng.memset(u_hi[:, :, L:LP].bitcast(F32), 0.0).then_inc(consts, 1)
            eng.memset(u_lo[:, :, L:LP].bitcast(F32), 0.0).then_inc(consts, 1)
            eng.wait_ge(consts, 8)

            def power(n, to, of, rows_=P):
                return eng.tensor_tensor(to[0:rows_, n:n + 1], of[0:rows_, n:n + 1], m_half[0:rows_, :], ALU.pow)

            def x_power(r):
                eng.wait_ge(x_ms, r + 1)
                power(r % 2, rs, ms, META if r == 0 else P).then_inc(x_rs, 1)

            x_power(0)
            for r in range(CH):
                if r + 1 < CH:
                    x_power(r + 1)
                a, b = token_cols(r)
                src = (k_t, v_t)[r % 2][:, 0:KD * (b - a)].rearrange("p (k n) -> p k n", k=KD)
                eng.wait_ge(u_hi_ok, r + 1)
                eng.tensor_tensor(u_lo[:, :, a:b], src, u_hi[:, :, a:b].bitcast(F32), ALU.subtract).then_inc(u_lo_ok, 1)
            eng.wait_ge(w_hi_ok, 1)
            eng.tensor_tensor(wd_lo, wd_raw, wd_hi.bitcast(F32), ALU.subtract).then_inc(w_lo_ok, 1)
            with eng.Fori(0, HEADS) as i:
                for step, a in STEPS:
                    if step == "split":
                        eng.wait_ge(w_hi_ok, i * NT + a + 2)
                        eng.tensor_tensor(w_lo[:, a % 2, :, :], w_raw[:, a % 2, :, :],
                                          w_hi[:, a % 2, :, :].bitcast(F32), ALU.subtract).then_inc(w_lo_ok, 1)
                    elif step == "attn_out":
                        eng.wait_ge(o_ms_ok, i * QB + a + 2)
                        power(0, o_rs, o_ms).then_inc(o_rs_ok, 1)
                    elif step == "chunk" and a < CH - 1:
                        n = META if a == 0 else P
                        eng.wait_ge(xdt_ok, i * CH + a + 1)
                        eng.wait_ge(scan_done, i * CH + max(a - 1, 0) + 1)
                        eng.tensor_tensor(xdd[0:n, a % 2, :].rearrange("p (r d) -> p r d", r=R),
                                          xdt[0:n, a % 2, :].rearrange("p (r d) -> p r d", r=R),
                                          sg[0:n, 2, a, :].unsqueeze(2).to_broadcast([n, R, HD]), ALU.mult).then_inc(xdd_ok, 1)
                    elif step == "z" and a < CH - 1:
                        eng.wait_ge(state_ok, i * (CH - 1) + a + 1)
                        eng.tensor_tensor(state_d[:, :].rearrange("p (r d) -> p r d", r=R),
                                          state[:, :].rearrange("p (r d) -> p r d", r=R),
                                          sg[:, 4, a, :].unsqueeze(2).to_broadcast([P, R, HD]), ALU.mult).then_inc(sd_ok, 1)
                    elif step == "ssm_out":
                        eng.wait_ge(z_ms_ok, i * QB + a + 1)
                        power(a % 2, z_rs, z_ms).then_inc(z_rs_ok, 1)

            def low_w(n, b):
                eng.wait_ge(yw_hi, n + 1)
                eng.tensor_tensor(wo_lo[:, b, :], wo_raw[:, b, :], wo_hi[:, b, :].bitcast(F32), ALU.subtract).then_inc(wo_lo_ok, 1)

            with eng.Fori(0, KO) as j:
                for b in range(2):
                    low_w(2 * j + b, b)
            for t in range(QB):
                eng.wait_ge(f_ms_ok, t + 1)
                power(t, f_rs, f_ms).then_inc(f_rs_ok, 1)

        @block.scalar
        def _(eng):
            def x_square(r):
                n = META if r == 0 else P
                eng.wait_ge(x_in[r % 2], 16 * (r // 2 + 1))
                eng.wait_ge(x_ms, max(r - 1, 0))
                eng.wait_ge(x_sq, r)
                eng.activation(th_tile[0:n, 0:D], prob[r % 2][0:n, 0:D], ACT.Square,
                               accum_out=ss[0:n, r % 2:r % 2 + 1]).then_inc(x_sq, 1)

            x_square(0)
            for r in range(CH):
                if r + 1 < CH:
                    x_square(r + 1)
                a, b = token_cols(r)
                src = (k_t, v_t)[r % 2][:, 0:KD * (b - a)].rearrange("p (k n) -> p k n", k=KD)
                eng.wait_ge(u_prod, r + 1)
                eng.copy(u_hi[:, :, a:b], src).then_inc(u_hi_ok, 1)
            eng.wait_ge(lam_sum, 1)
            eng.activation(lam_s[:, 2:4], lam_s[:, 0:2], ACT.Exp).then_inc(lam_exp, 1)
            eng.wait_ge(wd_in, 16)
            eng.copy(wd_hi, wd_raw).then_inc(w_hi_ok, 1)
            eng.activation(a_bc[:, :], a_bc[:, :], ACT.Exp).then_inc(lam_exp, 1)
            eng.wait_ge(dt_x, 1)
            eng.activation(sp[:, 1, :], sp[:, 0, :], ACT.Abs).then_inc(dt_e, 1)
            eng.wait_ge(dt_e, 1)
            eng.activation(sp[:, 2, :], sp[:, 1, :], ACT.Exp, scale=-1.0).then_inc(dt_e, 1)
            eng.wait_ge(stat_x, 1)
            for n in (2, 3, 4):
                ins = eng.activation(stat[:, n, :, :], stat[:, n, :, :], ACT.Exp)
            ins.then_inc(stat_e, 1)

            with eng.Fori(0, HEADS) as i:
                for step, a in STEPS:
                    if step == "split":
                        b = a % 2
                        last = {0: 0, 1: 0}.get(a, PIECES * (a - 1))
                        eng.wait_ge(w_in_ok[b], i * (16 * NT // 2) + 16 * (a // 2 + 1))
                        eng.wait_ge(piece_done, i * PPI + last + 1)
                        if a == 0:
                            eng.wait_ge(dt_pe, PIECES)
                        eng.copy(w_hi[:, b, :, :], w_raw[:, b, :, :]).then_inc(w_hi_ok, 1)
                    elif step == "piece":
                        t, tc = divmod(a, PIECES)
                        cols = slice(tc * PW, (tc + 1) * PW)
                        src = pb[a % 2][:, 0:PW]
                        if t in (TQ, TV, TG, TXS0, TXS1, TB, TC, TGC):
                            eng.wait_ge(piece_done, i * PPI + a + 2)
                        if t == TQ:
                            eng.wait_ge(s_done, i * 2 * QB + 1)
                            eng.mul(q_map[0][0:QK, cols], src[0:QK, :], QK ** -0.5)
                            eng.mul(q_map[1][QK:P, cols], src[QK:P, :], QK ** -0.5).then_inc(bank_free[a % 2], 1)
                        elif t == TV:
                            eng.wait_ge(v_tr, i + 1)
                            eng.copy(v_t[:, cols], src).then_inc(bank_free[a % 2], 1)
                        elif t in (TG, TGC):
                            eng.activation(th_piece[:, a % 2, :], src, ACT.Tanh, scale=0.5).then_inc(th_ok, 1)
                        elif TXS0 <= t <= TC:
                            eng.wait_ge(raw_free, i * 4 + t - TXS0 + 1)
                            eng.copy(raw[:, 3 + tc * PW:3 + (tc + 1) * PW], src).then_inc(bank_free[a % 2], 1)
                    elif step == "gate_taps":
                        n = a - TXS0
                        eng.wait_ge(raw_free, i * 4 + n + 2)
                        dst = (xs[:, 0, :], xs[:, 1, :], b_t, c_t)[n]
                        eng.wait_ge(conv_ok, i * 4 + n + 1)
                        eng.activation(th_tile[:, :], dst, ACT.Tanh, scale=0.5).then_inc(thc_ok, 1)
                    elif step == "turn_v":
                        eng.wait_ge(v_blk_ok, i + 1)
                        eng.copy(v_blk[:, 4:8, :], t_ps[1][:, :])
                        eng.copy(v_meta, o_ps[0:META, 0:P]).then_inc(v_meta_ok, 1)
                    elif step == "scores":
                        s, m = a
                        nk = P * (s + 1) + META
                        eng.wait_ge(max_ok, i * 2 * QB + 2 * s + m + 1)
                        if m == 0:
                            eng.wait_ge(a_tr, i * QB + s + 1)
                        else:
                            eng.wait_ge(mix_ok, i * QB + s + 1)
                        eng.activation(prob[m][:, 0:nk], s_ps[:, 0:nk], ACT.Exp, bias=mx[:, m:m + 1],
                                       accum_out=psum_e[:, s % 2, m:m + 1]).then_inc(exp_ok, 1)
                    elif step == "turn":
                        eng.wait_ge(a_tr, i * QB + a + 2)
                        if a >= 4:
                            eng.copy(a_t[:, 4:a + 1, :], t_ps[1][:, 0:P * (a - 3)])
                        eng.copy(a_meta, o_ps[0:META, 0:P]).then_inc(a_m_ok, 1)
                    elif step == "values":
                        eng.wait_ge(o_c_ok, i * QB + a + 1)
                        eng.wait_ge(o_ms_ok, i * QB + a + 1)
                        eng.wait_ge(o_sq, i * QB + a + 1)
                        eng.activation(th_tile[:, 0:P], o_n, ACT.Square, accum_out=o_ss[:, :]).then_inc(o_sq, 1)
                    elif step == "decay":
                        eng.wait_ge(seg_ok, i * QB + a + 1)
                        eng.activation(lmat[:, a % 2, :, :], lmat[:, a % 2, :, :], ACT.Exp).then_inc(l_ok, 1)
                    elif step == "z":
                        p = NP + a - 1
                        eng.wait_ge(piece_done, i * PPI + p + 2)
                        eng.activation(th_piece[:, p % 2, 0:GW], pb[p % 2][:, 0:GW], ACT.Tanh, scale=0.5).then_inc(zth_ok, 1)
                    elif step == "ssm_out":
                        n = i * QB + a
                        eng.wait_ge(y_gated, n + 1)
                        eng.wait_ge(z_ms_ok, n - 1 + 1)
                        eng.activation(th_tile[:, 0:GW], y_n[:, a % 2, :], ACT.Square, accum_out=z_ss[:, a % 2:a % 2 + 1]).then_inc(z_sq, 1)
                        eng.wait_ge(z_rs_ok, n)
                        eng.activation(y_n[:, a % 2, :], y_n[:, a % 2, :], ACT.Copy, scale=z_rs[:, a % 2:a % 2 + 1]).then_inc(y_n_ok, 1)
                        eng.wait_ge(y_tr, n + 1)
                        if a == 1:
                            eng.wait_ge(ssm_st, i * 32 + 16)
                        for t in range(2):
                            ins = eng.activation(ys[:, t, (a - 1) * P:a * P], yt_ps[:, t * P:(t + 1) * P], ACT.Copy, scale=par_sn[:, t:t + 1])
                        ins.then_inc(ys_ok, 1)

            def high(n, b):
                eng.wait_ge(out_k, n - 1 + 1)
                eng.copy(y_hi[:, b, :], y_raw[:, b, :])
                eng.copy(wo_hi[:, b, :], wo_raw[:, b, :]).then_inc(yw_hi, 1)

            eng.wait_ge(piece_done, HEADS * PPI + 1)
            for b in range(2):
                eng.wait_ge(yw_in[b], 32)
                eng.copy(y_hi[:, b, :], y_raw[:, b, :])
                eng.copy(wo_hi[:, b, :], wo_raw[:, b, :]).then_inc(yw_hi, 1)
            with eng.Fori(1, KO) as j:
                for b in range(2):
                    eng.wait_ge(yw_in[b], j * 32 + 32)
                    high(2 * j + b, b)
            for t in range(QB):
                eng.wait_ge(h_ok, QB + t + 1)
                eng.wait_ge(f_sq, t)
                eng.activation(th_tile[:, 0:D], h_res[:, t, :], ACT.Square, accum_out=f_ss[:, t:t + 1]).then_inc(f_sq, 1)

        @block.vector
        def _(eng):
            own = dve_own
            own(eng, eng.memset(raw[:, 0:3], 0.0))
            own(eng, eng.memset(conv_u[:, 0:2], 0.0))
            eng.memset(q_map[0][QK:P, :], 0.0)
            own(eng, eng.memset(q_map[1][0:QK, :], 0.0))
            eng.memset(dt_row[:, META:P], 0.0)
            eng.wait_ge(consts, 8)
            own(eng, eng.tensor_copy(ident_b[:, :], ident[:, :]))
            eng.wait_ge(par_tr, 1)
            own(eng, eng.tensor_copy(par[:, :], o_ps[:, 0:R_END]))
            own(eng, eng.tensor_scalar(a_norm[:, :], par[:, R_AN:R_END], 0.5 * (1.0 - LAM_INIT), None, ALU.mult))
            eng.wait_ge(params_in, 160)
            own(eng, eng.tensor_scalar(d_bc[:, :], d_bc[:, :], 0.5, None, ALU.mult))
            own(eng, eng.tensor_tensor(lam_p[:, :, :], lam_in[:, 0:4:2, :], lam_in[:, 1:4:2, :], ALU.mult))
            eng.tensor_reduce(lam_s[:, 0:2], lam_p[:, :, :], AX.X, ALU.add).then_inc(lam_sum, 1)

            def x_mean(r):
                n = META if r == 0 else P
                eng.wait_ge(x_sq, r + 1)
                eng.tensor_scalar(ms[0:n, r % 2:r % 2 + 1], ss[0:n, r % 2:r % 2 + 1], 1.0 / D, EPS, ALU.mult, ALU.add).then_inc(x_ms, 1)

            def x_scale(r):
                n = META if r == 0 else P
                eng.wait_ge(x_rs, r + 1)
                eng.tensor_scalar(prob[r % 2][0:n, 0:D], prob[r % 2][0:n, 0:D], rs[0:n, r % 2:r % 2 + 1], None, ALU.mult).then_inc(x_n, 1)

            x_mean(0)
            x_scale(0)
            for r in range(CH):
                if r + 1 < CH:
                    x_mean(r + 1)
                    x_scale(r + 1)
                a, b = token_cols(r)
                dst = (k_t, v_t)[r % 2][:, 0:KD * (b - a)].rearrange("p (k n) -> p k n", k=KD)
                eng.wait_ge(x_tr, r + 1)
                eng.wait_ge(u_lo_ok, max(r - 1, 0))
                eng.tensor_tensor(dst, u_ps[r % 2].rearrange("p (k n) -> p k n", k=KD)[:, :, 0:b - a],
                                  par[:, R_NW:R_AN].unsqueeze(2).to_broadcast([P, KD, b - a]), ALU.mult).then_inc(u_prod, 1)
            eng.wait_ge(lam_exp, 1)
            own(eng, eng.tensor_tensor(lam_s[:, 4:5], lam_s[:, 2:3], lam_s[:, 3:4], ALU.subtract))
            eng.tensor_scalar(lam_s[:, 5:6], lam_s[:, 4:5], LAM_INIT, -1.0, ALU.add, ALU.mult).then_inc(lam_row, 1)
            eng.wait_ge(lam_pe, 1)
            eng.tensor_copy(n_lam[:, :], o_ps[:, 0:1]).then_inc(lam_ok, 1)
            eng.wait_ge(lam_ok, 1)

            eng.wait_ge(dt_pe, PIECES)
            for tc in range(PIECES):
                src = ps[0:SH, 5 + tc, :]
                lo = META if tc == 0 else 0
                hi = L - (PIECES - 1) * PW if tc == PIECES - 1 else PW
                if tc == 0:
                    eng.tensor_scalar(dt_row[:, 0:META], src[:, 0:META], dt_bias[:, :], None, ALU.add)
                at = tc * PW + P - META
                ins = eng.tensor_scalar(dt_row[:, at + lo:at + hi], src[:, lo:hi], dt_bias[:, :], None, ALU.add)
            ins.then_inc(dt_row_ok, 1)
            eng.wait_ge(dt_tr, 1)
            eng.tensor_copy(sp[:, 0, :], ps[:, 5, 0:CH * SH]).then_inc(dt_x, 1)
            eng.wait_ge(dt_e, 2)
            own(eng, eng.tensor_scalar(sp[:, 3, :], sp[:, 2, :], 2.0, None, ALU.add))
            own(eng, eng.reciprocal(sp[:, 4, :], sp[:, 3, :]))
            own(eng, eng.tensor_tensor(sp[:, 1, :], sp[:, 2, :], sp[:, 4, :], ALU.mult))
            own(eng, eng.tensor_tensor(sp[:, 3, :], sp[:, 1, :], sp[:, 1, :], ALU.mult))
            own(eng, eng.tensor_scalar(sp[:, 4, :], sp[:, 3, :], 1.0 / 17, None, ALU.mult))
            for n in range(15, 1, -2):
                own(eng, eng.scalar_tensor_tensor(sp[:, 4, :], sp[:, 4, :], 1.0 / n, sp[:, 3, :], ALU.add, ALU.mult))
            own(eng, eng.scalar_tensor_tensor(sp[:, 4, :], sp[:, 4, :], 1.0, sp[:, 1, :], ALU.add, ALU.mult))
            own(eng, eng.tensor_scalar(sp[:, 5, :], sp[:, 0, :], 0.0, None, ALU.max))
            own(eng, eng.scalar_tensor_tensor(sp[:, 5, :], sp[:, 4, :], 2.0, sp[:, 5, :], ALU.mult, ALU.add))
            own(eng, eng.tensor_scalar(sp[:, 5, 0:SH], sp[:, 5, 0:SH], valid[:, :], None, ALU.mult))
            own(eng, eng.tensor_scalar(stat[:, 0, :, :], sp[:, 5, :], 0.5, None, ALU.mult))
            eng.wait_ge(lam_exp, 2)
            eng.scalar_tensor_tensor(sp[:, 4, :].rearrange("p (c h) -> p c h", c=CH), sp[:, 5, :].rearrange("p (c h) -> p c h", c=CH), -1.0,
                                     a_bc[:, :].unsqueeze(1).to_broadcast([P, CH, SH]), ALU.mult, ALU.mult).then_inc(adt_ok, 1)
            eng.wait_ge(cum_pe, 1)
            eng.tensor_copy(stat[:, 1, :, :], o_ps[:, 0:CH * SH]).then_inc(acum_ok, 1)
            eng.wait_ge(acum_ok, 1)
            own(eng, eng.tensor_copy(stat[:, 4, :, :], o_ps[:, CH * SH:2 * CH * SH]))
            own(eng, eng.tensor_copy(stat[:, 3, :, :], stat[:, 1, :, :]))
            eng.tensor_tensor(stat[:, 2, :, :], stat[:, 4, :, :], stat[:, 1, :, :], ALU.subtract).then_inc(stat_x, 1)
            eng.wait_ge(acum_tr, 1)
            eng.tensor_copy(dt_row[:, 0:4 * P], ps[0:SH, 5, :])
            eng.tensor_copy(dt_row[:, 4 * P:8 * P], ps[0:SH, 6, :])
            eng.tensor_copy(dt_row[:, 8 * P:9 * P], ps[0:SH, 7, 0:P]).then_inc(acum_row, 1)
            eng.wait_ge(stat_e, 1)
            own(eng, eng.tensor_scalar(stat[:, 2:4, :, :], stat[:, 2:4, :, :], 0.5, None, ALU.mult))

            eng.wait_ge(acum_st, 16)
            prologue = own.n
            with eng.Fori(0, HEADS) as i:
                own.enter(i)
                for step, a in STEPS:
                    if step == "params":
                        eng.wait_ge(scan_done, i * CH + 1)
                        eng.wait_ge(g_ok, i * QB + 1)
                        eng.wait_ge(ys_ok, i * QB + 1)
                        taps = par[:, R_CW:R_CB].rearrange("p (j t) -> p j t", j=4)
                        eng.tensor_copy(par_cw[:, :, 0:2], taps[:, :, bass.ds(2 * i, 2)])
                        eng.tensor_copy(par_cw[:, :, 2:3], taps[:, :, bass.ds(i + XT, 1)])
                        eng.tensor_copy(par_cw[:, :, 3:4], taps[:, :, bass.ds(i + XT + HEADS, 1)])
                        eng.tensor_copy(par_cb[:, 0:2], par[:, bass.ds(2 * i + R_CB, 2)])
                        eng.tensor_copy(par_cb[:, 2:3], par[:, bass.ds(i + R_CB + XT, 1)])
                        eng.tensor_copy(par_cb[:, 3:4], par[:, bass.ds(i + R_CB + XT + HEADS, 1)])
                        eng.tensor_copy(par_sw[:, :], par[:, R_SW:R_SN].rearrange("p (j t) -> p j t", j=3)[:, :, bass.ds(i, 1)])
                        eng.tensor_scalar(par_sn[:, :], par[:, bass.ds(2 * i + R_SN, 2)], 0.5, None, ALU.mult)
                        eng.tensor_copy(dg[:, :], d_bc[:, bass.ds(R * i, R)])
                        own(eng, eng.tensor_copy(sg[:, :, :, :].rearrange("p s c r -> p (s c) r"),
                                                 stat[:, :, :, :].rearrange("p s c h -> p (s c) h")[:, :, bass.ds(R * i, R)]))
                        eng.tensor_copy(ms[:, 0:1], m_half[:, :]).then_inc(sg_ok, 1)
                    elif step == "piece":
                        t, tc = divmod(a, PIECES)
                        cols = slice(tc * PW, (tc + 1) * PW)
                        src = pb[a % 2][:, 0:PW]
                        done = bank_free[a % 2]
                        if t == TK:
                            eng.wait_ge(piece_done, i * PPI + a + 2)
                            eng.wait_ge(s_done, i * 2 * QB + 1)
                            eng.tensor_copy(k_t[:, cols], src).then_inc(done, 1)
                        elif t == TG:
                            eng.wait_ge(attn_st, i * 16 + 16)
                            eng.wait_ge(th_ok, i * 6 + tc + 1)
                            eng.scalar_tensor_tensor(gate[:, cols], th_piece[:, a % 2, :], 1.0, src, ALU.add, ALU.mult).then_inc(done, 1)
                        elif t == TCB:
                            eng.wait_ge(piece_done, i * PPI + a + 2)
                            eng.tensor_copy(conv_b_s[:, cols], src).then_inc(done, 1)
                        elif t == TCC:
                            eng.wait_ge(piece_done, i * PPI + a + 2)
                            eng.tensor_copy(conv_u[:, 2 + tc * PW:2 + (tc + 1) * PW], src).then_inc(done, 1)
                        elif t == TCH:
                            eng.wait_ge(piece_done, i * PPI + a + 2)
                            eng.wait_ge(bank_free[(a - PIECES) % 2], i * (PPI // 2) + (a - PIECES) // 2 + 2)
                            c2 = slice(2 + tc * PW, 2 + (tc + 1) * PW)
                            eng.tensor_tensor(conv_u[:, c2], src, conv_u[:, c2], ALU.mult).then_inc(done, 1)
                        elif t == TGC:
                            eng.wait_ge(th_ok, i * 6 + 3 + tc + 1)
                            eng.scalar_tensor_tensor(conv_g[:, cols], th_piece[:, a % 2, :], 1.0, src, ALU.add, ALU.mult).then_inc(done, 1)
                    elif step == "taps":
                        n = a - TXS0
                        dst = (xs[:, 0, :], xs[:, 1, :], b_t, c_t)[n]
                        for b in range(2):
                            eng.wait_ge(bank_free[b], i * (PPI // 2) + (PIECES * (a + 1) + 1 - b) // 2 + 1)
                        own(eng, eng.tensor_scalar(dst, raw[:, 0:LP], par_cw[:, 0, n:n + 1], par_cb[:, n:n + 1], ALU.mult, ALU.add))
                        for j in range(1, 4):
                            ins = eng.scalar_tensor_tensor(dst, raw[:, j:j + LP], par_cw[:, j, n:n + 1], dst, ALU.mult, ALU.add)
                            if j < 3:
                                own(eng, ins)
                        ins.then_inc(raw_free, 1)
                    elif step == "gate_taps":
                        n = a - TXS0
                        dst = (xs[:, 0, :], xs[:, 1, :], b_t, c_t)[n]
                        eng.wait_ge(thc_ok, i * 4 + n + 1)
                        eng.scalar_tensor_tensor(dst, th_tile[:, :], 1.0, dst, ALU.add, ALU.mult).then_inc(conv_ok, 1)
                    elif step == "turn_v":
                        eng.wait_ge(v_tr, i + 2)
                        eng.tensor_copy(v_blk[:, 0:4, :], t_ps[0][:, :]).then_inc(v_blk_ok, 1)
                    elif step == "scores":
                        s, m = a
                        nk = P * (s + 1) + META
                        n = i * 2 * QB + 2 * s + m
                        eng.wait_ge(s_done, n + 2)
                        if s > 0:
                            eng.wait_ge(exp_ok, n - 1 + 1)
                        eng.tensor_reduce(mx[:, m:m + 1], s_ps[:, 0:nk], AX.X, ALU.max, negate=True).then_inc(max_ok, 1)
                    elif step == "mix":
                        nk = P * (a + 1) + META
                        b = a % 2
                        eng.wait_ge(exp_ok, i * 2 * QB + 2 * a + 2 + 1)
                        own(eng, eng.reciprocal(rinv[:, b, :], psum_e[:, b, :]))
                        own(eng, eng.scalar_tensor_tensor(cmix[:, :], rinv[:, b, 1:2], psum_e[:, b, 0:1], n_lam[:, :], ALU.mult, ALU.mult))
                        eng.scalar_tensor_tensor(prob[0][:, 0:nk], prob[1][:, 0:nk], cmix[:, 0:1], prob[0][:, 0:nk],
                                                 ALU.mult, ALU.add).then_inc(mix_ok, 1)
                    elif step == "turn":
                        nb = min(a + 1, 4)
                        eng.wait_ge(a_tr, i * QB + a + 2)
                        eng.tensor_copy(a_t[:, 0:nb, :], t_ps[0][:, 0:nb * P]).then_inc(a_t_ok, 1)
                    elif step == "values":
                        b = a % 2
                        eng.wait_ge(o_done, i * QB + a + 1)
                        own(eng, eng.tensor_scalar(o_n, o_ps[:, P:2 * P], rinv[:, b, 0:1], O_TOP, ALU.mult, ALU.min))
                        eng.tensor_scalar(o_n, o_n, -O_TOP, O_TOP ** -0.5, ALU.max, ALU.mult).then_inc(o_c_ok, 1)
                    elif step == "attn_out":
                        n = i * QB + a
                        b = a % 2
                        eng.wait_ge(o_sq, n + 2)
                        own(eng, eng.tensor_scalar(o_fit[:, :], o_ss[:, :], O_TOP, None, ALU.is_lt))
                        eng.tensor_scalar(o_ms[:, :], o_ss[:, :], 1.0 / P, EPS / O_TOP, ALU.mult, ALU.add).then_inc(o_ms_ok, 1)
                        eng.wait_ge(o_rs_ok, n + 1)
                        eng.tensor_scalar(o_n, o_n, o_rs[:, 0:1], o_fit[:, 0:1], ALU.mult, ALU.mult).then_inc(o_n_ok, 1)
                        eng.wait_ge(o_tr, n + 1)
                        ca, cb = token_cols(a + 1)
                        eng.scalar_tensor_tensor(gate[:, ca:cb], o_ps[:, 2 * P:3 * P], a_norm[:, 0:1], gate[:, ca:cb],
                                                 ALU.mult, ALU.mult).then_inc(attn_ok, 1)
                    elif step == "conv":
                        eng.wait_ge(convg_st, i * 16 + 16)
                        own(eng, eng.tensor_scalar(conv_y[:, :], conv_u[:, META:META + T], par_sw[:, 0:1], None, ALU.mult))
                        for j in range(1, 3):
                            own(eng, eng.scalar_tensor_tensor(conv_y[:, :], conv_u[:, META + j:META + j + T], par_sw[:, j:j + 1],
                                                              conv_y[:, :], ALU.mult, ALU.add))
                        own(eng, eng.tensor_tensor(conv_y[:, :], conv_y[:, :], conv_b_s[:, META:L], ALU.mult))
                        eng.scalar_tensor_tensor(conv_y[:, :], conv_y[:, :], 0.5, conv_g[:, META:L], ALU.mult, ALU.mult).then_inc(convg_ok, 1)
                    elif step == "decay":
                        eng.wait_ge(acum_in[a % 2], i * 64 + 16 * ((a + 1) // 2))
                        eng.wait_ge(scan_done, i * CH + max(a - 1, 0) + 1)
                        for r in range(R):
                            ins = eng.tensor_scalar(lmat[:, a % 2, r, :], acum_b[:, a % 2, r, :], sg[:, 1, a, r:r + 1], 0.0,
                                                    ALU.subtract, ALU.min)
                        ins.then_inc(seg_ok, 1)
                    elif step == "chunk":
                        n = META if a == 0 else P
                        b = a % 2
                        eng.wait_ge(x_done, i * CH + a + 1)
                        eng.wait_ge(scan_done, i * CH + max(a - 1, 0) + 1)
                        eng.wait_ge(xdd_ok, i * (CH - 1) + max(a - 1, 0) + 1)
                        x3 = x_ps[b][0:n, 0:GW].rearrange("p (r d) -> p r d", r=R)
                        eng.tensor_tensor(xdt[0:n, b, :].rearrange("p (r d) -> p r d", r=R), x3,
                                          sg[0:n, 0, a, :].unsqueeze(2).to_broadcast([n, R, HD]), ALU.mult).then_inc(xdt_ok, 1)
                        if a > 0:
                            eng.tensor_tensor(xd[:, b, :].rearrange("p (r d) -> p r d", r=R), x3,
                                              dg[:, :].unsqueeze(2).to_broadcast([P, R, HD]), ALU.mult)
                            own(eng, eng.scalar_tensor_tensor(cbm[:, b, :], x_ps[b][:, 3 * P:4 * P], 0.25, tri[:, :], ALU.mult, ALU.mult))
                        eng.tensor_copy(b_n[0:n, b, :], x_ps[b][0:n, 2 * P:3 * P]).then_inc(x_free, 1)
                        if a > 0:
                            eng.wait_ge(l_ok, i * QB + a)
                            eng.wait_ge(scan_done, i * CH + a + 1)
                            eng.tensor_tensor(lmat[:, b, :, :], lmat[:, b, :, :],
                                              cbm[:, b, :].unsqueeze(1).to_broadcast([P, R, P]), ALU.mult).then_inc(g_ok, 1)
                    elif step == "z":
                        p = NP + a - 1
                        eng.wait_ge(zth_ok, i * QB + a)
                        own(eng, eng.scalar_tensor_tensor(z_n[:, a % 2, :], th_piece[:, p % 2, 0:GW], 1.0, pb[p % 2][:, 0:GW],
                                                          ALU.add, ALU.mult))
                        eng.tensor_copy(ms[:, 0:1], m_half[:, :]).then_inc(bank_free[p % 2], 1)
                    elif step == "scan":
                        b = a % 2
                        eng.wait_ge(scan_done, i * CH + a + 2)
                        if a == 0:
                            eng.tensor_copy(state[:, :], st_ps[:, 0:GW]).then_inc(state_ok, 1)
                        elif a < CH - 1:
                            eng.wait_ge(sd_ok, i * (CH - 2) + a)
                            eng.tensor_tensor(state[:, :], state_d[:, :], st_ps[:, 0:GW], ALU.add).then_inc(state_ok, 1)
                        if a > 0:
                            own(eng, eng.tensor_tensor(y_a[:, :].rearrange("p (r d) -> p r d", r=R),
                                                       y_ps[b][:, GW:2 * GW].rearrange("p (r d) -> p r d", r=R),
                                                       sg[:, 3, a, :].unsqueeze(2).to_broadcast([P, R, HD]), ALU.mult))
                            own(eng, eng.tensor_tensor(y_a[:, :], y_ps[b][:, 0:GW], y_a[:, :], ALU.add))
                            own(eng, eng.tensor_tensor(y_a[:, :], y_a[:, :], xd[:, b, :], ALU.add))
                            eng.wait_ge(y_tr, i * QB + max(a - 2, 0) + 1)
                            eng.tensor_tensor(y_n[:, b, :], y_a[:, :], z_n[:, b, :], ALU.mult).then_inc(y_gated, 1)
                    elif step == "ssm_out":
                        eng.wait_ge(z_sq, i * QB + a)
                        eng.tensor_scalar(z_ms[:, a % 2:a % 2 + 1], z_ss[:, a % 2:a % 2 + 1], 0.25 / GW, EPS, ALU.mult, ALU.add).then_inc(z_ms_ok, 1)
            own.leave(prologue, HEADS)

            def low_y(n, b):
                eng.wait_ge(yw_hi, n + 1)
                eng.tensor_tensor(y_lo[:, b, :], y_raw[:, b, :], y_hi[:, b, :].bitcast(F32), ALU.subtract).then_inc(y_lo_ok, 1)

            eng.wait_ge(x_res, 32)
            for half in range(2):
                with eng.Fori(0, KO // 2) as j:
                    for b in range(2):
                        low_y(half * KO + 2 * j + b, b)
                for t in range(QB):
                    eng.wait_ge(out_bank, half * QB + t + 1)
                    h = h_res[:, t, half * HALF:(half + 1) * HALF]
                    eng.tensor_tensor(h, ps[:, t, :], h, ALU.add).then_inc(h_ok, 1)
            for t in range(QB):
                eng.wait_ge(f_sq, t + 1)
                eng.tensor_scalar(f_ms[:, t:t + 1], f_ss[:, t:t + 1], 1.0 / D, EPS, ALU.mult, ALU.add).then_inc(f_ms_ok, 1)
                eng.wait_ge(f_rs_ok, t + 1)
                eng.scalar_tensor_tensor(h_res[:, t, :], h_res[:, t, :], f_rs[:, t:t + 1], w_fin, ALU.mult, ALU.mult).then_inc(f_ok, 1)

        @block.tensor
        def _(eng):
            def turn(dst, src, n=P):
                return eng.transpose(dst, src, ident[0:n, 0:n])

            eng.wait_ge(consts, 8)
            eng.wait_ge(params_in, 160)
            turn(o_ps[:, 0:R_END], rows[0:R_END, :], R_END).then_inc(par_tr, 1)
            for r in range(CH):
                n = META if r == 0 else P
                eng.wait_ge(x_n, r + 1)
                eng.wait_ge(u_prod, max(r - 1, 0))
                for k in range(KD):
                    ins = turn(u_ps[r % 2][:, k * P:k * P + n], prob[r % 2][0:n, k * P:(k + 1) * P], n)
                ins.then_inc(x_tr, 1)
            eng.wait_ge(par_tr, 1)
            eng.wait_ge(lam_row, 1)
            eng.matmul(o_ps[:, 0:1], ones[0:1, :], lam_s[0:1, 5:6], start=True, stop=True).then_inc(lam_pe, 1)

            def project(dst, m, cols, wh, wl):
                terms = [(wh, u_hi), (wh, u_lo), (wl, u_hi)]
                for k in range(KD):
                    for n, (w, u) in enumerate(terms):
                        ins = eng.matmul(dst, w[:, k, 0:m], u[:, k, cols], start=(k == 0 and n == 0), stop=(k == KD - 1 and n == 2))
                return ins

            eng.wait_ge(u_lo_ok, CH)
            eng.wait_ge(w_lo_ok, 1 + 1)
            for tc in range(PIECES):
                if tc == 2:
                    eng.wait_ge(lam_ok, 1)
                project(ps[0:SH, 5 + tc, 0:PW], SH, slice(tc * PW, (tc + 1) * PW), wd_hi, wd_lo).then_inc(dt_pe, 1)
            eng.wait_ge(dt_row_ok, 1)
            for c in range(CH):
                ins = turn(ps[:, 5, c * SH:(c + 1) * SH], dt_row[:, c * P:(c + 1) * P], SH)
            ins.then_inc(dt_tr, 1)
            eng.wait_ge(adt_ok, 1)
            eng.matmul(o_ps[:, 0:CH * SH], tri[:, :], sp[:, 4, :], start=True, stop=True)
            eng.matmul(o_ps[:, CH * SH:2 * CH * SH], ones[:, :], sp[:, 4, :], start=True, stop=True).then_inc(cum_pe, 1)
            eng.wait_ge(acum_ok, 1)
            eng.wait_ge(stat_x, 1)
            for c in range(CH):
                ins = turn(ps[0:SH, 5 + c // 4, (c % 4) * P:(c % 4 + 1) * P], stat[:, 1, c, :])
            ins.then_inc(acum_tr, 1)
            eng.wait_ge(acum_row, 1)

            with eng.Fori(0, HEADS) as i:
                for step, a in STEPS:
                    if step == "piece":
                        t, tc = divmod(a, PIECES)
                        if tc == 0:
                            eng.wait_ge(w_lo_ok, i * NT + t + 2 + 1)
                        eng.wait_ge(bank_free[a % 2], i * (PPI // 2) + a // 2 + 1)
                        project(pb[a % 2][:, 0:PW], P, slice(tc * PW, (tc + 1) * PW), w_hi[:, t % 2], w_lo[:, t % 2]).then_inc(piece_done, 1)
                    elif step == "turn_v":
                        for b in range(2):
                            eng.wait_ge(bank_free[b], i * (PPI // 2) + (PIECES * (TV + 1) + 1 - b) // 2 + 1)
                        eng.wait_ge(ys_ok, i * QB + 1)
                        eng.wait_ge(state_ok, i * (CH - 1) + 1)
                        eng.wait_ge(y_gated, i * QB + 1)
                        for n in range(QB):
                            turn(t_ps[n // 4][:, (n % 4) * P:(n % 4 + 1) * P], v_t[:, META + n * P:META + (n + 1) * P])
                        turn(o_ps[0:META, 0:P], v_t[:, 0:META]).then_inc(v_tr, 1)
                    elif step == "scores":
                        s, m = a
                        n = i * 2 * QB + 2 * s + m
                        if (s, m) == (0, 0):
                            for b in range(2):
                                eng.wait_ge(bank_free[b], i * (PPI // 2) + PIECES * (TK + 1) // 2 + 1)
                            eng.wait_ge(x_free, i * CH + 1)
                            eng.wait_ge(y_gated, i * QB + 1)
                        eng.wait_ge(exp_ok, n + 1)
                        qa, qb = token_cols(s + 1)
                        q = q_map[m][:, qa:qb]
                        for at in range(0, (s + 1) * P, 512):
                            w = min(512, (s + 1) * P - at)
                            last = at + w == (s + 1) * P
                            eng.matmul(s_ps[:, at:at + w], q, k_t[:, META + at:META + at + w], start=True, stop=not last)
                            if last:
                                eng.matmul(s_ps[:, s * P:(s + 1) * P], ident_b[:, :], mask_b[:, :], start=False, stop=True)
                        eng.matmul(s_ps[:, (s + 1) * P:(s + 1) * P + META], q, k_t[:, 0:META], start=True, stop=True).then_inc(s_done, 1)
                    elif step == "turn":
                        eng.wait_ge(mix_ok, i * QB + a + 2)
                        if a == 0:
                            eng.wait_ge(v_meta_ok, i + 1)
                            eng.wait_ge(v_blk_ok, i + 1)
                        eng.wait_ge(a_t_ok, i * QB + a + 1)
                        eng.wait_ge(a_m_ok, i * QB + a + 1)
                        eng.wait_ge(attn_ok, i * QB + a + 1)
                        for n in range(a + 1):
                            turn(t_ps[n // 4][:, (n % 4) * P:(n % 4 + 1) * P], prob[0][:, n * P:(n + 1) * P])
                        turn(o_ps[0:META, 0:P], prob[0][:, (a + 1) * P:(a + 1) * P + META]).then_inc(a_tr, 1)
                    elif step == "values":
                        eng.wait_ge(a_t_ok, i * QB + a + 2)
                        eng.wait_ge(a_m_ok, i * QB + a + 2)
                        for n in range(a + 1):
                            eng.matmul(o_ps[:, P:2 * P], a_t[:, n, :], v_blk[:, n, :], start=(n == 0), stop=False)
                        eng.matmul(o_ps[:, P:2 * P], a_meta, v_meta, start=False, stop=True).then_inc(o_done, 1)
                    elif step == "attn_out":
                        eng.wait_ge(o_n_ok, i * QB + a + 1)
                        turn(o_ps[:, 2 * P:3 * P], o_n).then_inc(o_tr, 1)
                    elif step == "chunk":
                        n = META if a == 0 else P
                        ca, cb = token_cols(a)
                        b = a % 2
                        if a == 0:
                            eng.wait_ge(conv_ok, i * 4 + 4 + 1)
                            eng.wait_ge(exp_ok, i * 2 * QB + 2 * QB + 1)
                            eng.wait_ge(attn_ok, i * QB + QB + 1)
                        if a >= 2:
                            eng.wait_ge(x_free, i * CH + a - 1 + 1)
                        for t in range(2):
                            turn(x_ps[b][0:n, t * P:(t + 1) * P], xs[:, t, ca:cb])
                        ins = turn(x_ps[b][0:n, 2 * P:3 * P], b_t[:, ca:cb])
                        if a > 0:
                            ins = eng.matmul(x_ps[b][:, 3 * P:4 * P], b_t[:, ca:cb], c_t[:, ca:cb], start=True, stop=True)
                        ins.then_inc(x_done, 1)
                    elif step == "z":
                        p = NP + a - 1
                        ca, cb = token_cols(a)
                        if a == 1:
                            eng.wait_ge(w_lo_ok, i * NT + TZ1 + 2 + 1)
                        eng.wait_ge(bank_free[p % 2], i * (PPI // 2) + p // 2 + 1)
                        terms = [(u_hi, w_hi), (u_hi, w_lo), (u_lo, w_hi)]
                        for k in range(KD):
                            for n, (u, w) in enumerate(terms):
                                ins = eng.matmul(pb[p % 2][:, 0:GW], u[:, k, ca:cb], w[:, :, k, :], start=(k == 0 and n == 0), stop=(k == KD - 1 and n == 2))
                        ins.then_inc(piece_done, 1)
                    elif step == "scan":
                        n = META if a == 0 else P
                        ca, cb = token_cols(a)
                        b = a % 2
                        if a > 0:
                            eng.wait_ge(y_gated, i * QB + max(a - 2, 0) + 1)
                            eng.wait_ge(g_ok, i * QB + a + 1)
                            for r in range(R):
                                eng.matmul(y_ps[b][:, r * HD:(r + 1) * HD], lmat[:, b, r, :], xdt[:, b, r * HD:(r + 1) * HD], start=True, stop=True)
                            eng.wait_ge(state_ok, i * (CH - 1) + a + 1)
                            ins = eng.matmul(y_ps[b][:, GW:2 * GW], c_t[:, ca:cb], state[:, :], start=True, stop=True)
                        if a < CH - 1:
                            eng.wait_ge(xdd_ok, i * (CH - 1) + a + 2)
                            eng.wait_ge(x_free, i * CH + a + 2)
                            ins = eng.matmul(st_ps[:, 0:GW], b_n[0:n, b, :], xdd[0:n, b, :], start=True, stop=True)
                        ins.then_inc(scan_done, 1)
                    elif step == "ssm_out":
                        eng.wait_ge(y_n_ok, i * QB + a)
                        eng.wait_ge(ys_ok, i * QB + a - 1 + 1)
                        turn(yt_ps[:, 0:P], y_n[:, a % 2, 0:P])
                        turn(yt_ps[:, P:2 * P], y_n[:, a % 2, P:2 * P]).then_inc(y_tr, 1)

            def out_pair(half, j, first, last):
                for b in range(2):
                    n = half * KO + 2 * j + b
                    eng.wait_ge(y_lo_ok, n + 2)
                    eng.wait_ge(wo_lo_ok, n + 2)
                    for t in range(QB):
                        if first and b == 0 and half == 1:
                            eng.wait_ge(h_ok, t + 1)
                        terms = [(y_hi, wo_hi), (y_hi, wo_lo), (y_lo, wo_hi)]
                        for m, (y, w) in enumerate(terms):
                            ins = eng.matmul(ps[:, t, :], y[:, b, t * P:(t + 1) * P], w[:, b, :],
                                             start=(first and b == 0 and m == 0), stop=(last and b == 1 and m == 2), skip_group_check=True)
                        if last and b == 1:
                            ins.then_inc(out_bank, 1)
                    if not (last and b == 1):
                        ins.then_inc(out_k, 1)
                    else:
                        eng.matmul

            for b in range(2):
                eng.wait_ge(bank_free[b], HEADS * PPI // 2 + 1)
            eng.wait_ge(y_gated, HEADS * QB + 1)
            eng.wait_ge(ys_ok, HEADS * QB + 1)
            for half in range(2):
                out_pair(half, 0, True, False)
                with eng.Fori(1, KO // 2 - 1) as j:
                    out_pair(half, j, False, False)
                out_pair(half, KO // 2 - 1, False, True)


_INS = ["x", "meta_tokens", "norm_w", "w_in", "w_out", "attn_lambda", "attn_norm_w", "sconv_w", "ssm_conv_w",
        "ssm_conv_b", "ssm_a_log", "ssm_dt_bias", "ssm_d", "ssm_norm_w", "final_norm_w"]


def kernel(**inputs):
    import concourse.bacc as bacc
    from concourse.bass_utils import run_bass_kernel_spmd

    nc = bacc.Bacc("TRN2", target_bir_lowering=False, num_devices=1)
    arrays, args = {}, []
    for name in _INS:
        a = np.ascontiguousarray(inputs[name])
        arrays[f"in_{name}"] = a
        args.append(nc.dram_tensor(f"in_{name}", a.shape, mybir.dt.from_np(a.dtype), kind="ExternalInput").ap())
    args.append(nc.dram_tensor("out_0", (1, T, D), F32, kind="ExternalOutput").ap())
    args.append(nc.dram_tensor("y_scratch", (2 * D, T), F32, kind="Internal").ap())
    args.append(nc.dram_tensor("acum_scratch", (SH, CH * P), F32, kind="Internal").ap())
    build(nc, *args)
    r = run_bass_kernel_spmd(nc, [arrays], core_ids=[0])
    return r.results[0]["out_0"]
```

```python
import math
from contextlib import ExitStack

import numpy as np

import concourse.bass as bass
from concourse import mybir

F32 = mybir.dt.float32
F32R = mybir.dt.float32r
BF16 = mybir.dt.bfloat16
ALU = mybir.AluOpType
ACT = mybir.ActivationFunctionType
AX = mybir.AxisListType

P = 128
D = 1024
T = 1024
META = 16
L = META + T
PIECES = 3
PW = 348
LP = PIECES * PW
KD = D // P
N_IN = 7184
HEADS = 4
QK = 64
QB = T // P
CH = QB + 1
SH = 16
R = SH // HEADS
HD = 64
GW = R * HD
OB = 4
XT = D // P
KO = 2 * D // P
HALF = D // 2
EPS = 1e-5
LAM_INIT = 0.8 - 0.6 * math.exp(-0.3 * 0)
MASK = -1e30
O_TOP = 2.0 ** 64

C_Q, C_K, C_V, C_G, C_CB, C_CC, C_CH, C_GC = (512 * n for n in range(8))
C_Z, C_XS, C_B, C_C, C_DT = 4096, 5120, 6144, 6656, 7168

TILES = [(C_Q, P), (C_K, P), (C_V, P), (C_G, P), (C_XS, GW), (C_XS + P, GW), (C_B, P), (C_C, P),
         (C_Z, GW), (C_Z + P, GW), (C_CB, P), (C_CC, P), (C_CH, P), (C_GC, P)]
NT = len(TILES)
(TQ, TK, TV, TG, TXS0, TXS1, TB, TC, TZ0, TZ1, TCB, TCC, TCH, TGC) = range(NT)
PZ = TZ0 * PIECES
PPI = (NT - 2) * PIECES + QB


def first_piece(t):
    return t * PIECES if t <= TZ0 else PZ + QB + (t - TCB) * PIECES


def tile_of(p):
    return divmod(p, PIECES) if p < PZ else (TCB + (p - PZ - QB) // PIECES, (p - PZ - QB) % PIECES)


R_CW, R_CB, R_SW, R_SN, R_NW, R_AN, R_END = 0, 64, 80, 92, 100, 108, 109


def schedule(last):
    out = []

    def add(name, arg=0, d=0):
        if not (last and d):
            out.append((name, arg, d))

    def ahead(name, t, d):
        add(name, t % NT, d + t // NT)

    def half_pieces(tiles, d):
        units = [[] for _ in range(len(tiles) * PIECES * 2)]
        tail = [[] for _ in range(6)]
        places = units + tail
        n = 0
        for t in tiles:
            units[n] += [("load", t + 2, d), ("split", t + 1, d)]
            if t == TXS0:
                units[n].append(("params", 0, d))
            for tc in range(PIECES):
                p = first_piece(t) + tc
                units[n].append(("project", (p, 0), d))
                units[n + 1] += [("project", (p, 1), d), ("piece", p, d)]
                n += 2
            if TXS0 <= t <= TC:
                for tap in range(4):
                    places[n - 1 + tap].append(("taps", (t, tap), d))
                places[n + 3].append(("gate_taps", t, d))
            if t == TGC:
                for part in range(5):
                    places[n - 1 + part].append(("conv", part, d))
        return units, tail

    def filler(units, slots):
        state = [0, 0.0]

        def fill(weight=1.0):
            state[1] += weight
            while state[0] < len(units) and state[0] < len(units) * state[1] / slots - 1e-9:
                emit(units[state[0]])
                state[0] += 1
        return fill

    def emit(unit):
        for name, arg, d in unit:
            if name in ("load", "split"):
                ahead(name, arg, d)
            else:
                add(name, arg, d)

    units, tail = half_pieces([TG, TXS0, TXS1, TB, TC], 0)
    units[-1] += [("split", TZ1, 0), ("load", TCB, 0), ("load", TCC, 0)]
    fill = filler(units, sum(ATT_FILL))
    for s in range(QB + 1):
        f = ATT_FILL[s] / 3
        if s < QB:
            add("scores", (s, 0))
        if s == 0:
            add("turn_v")
        if s >= 2:
            add("attn_out", s - 2)
        fill(f)
        if s >= 1:
            add("turn", s - 1)
        if s < QB:
            add("exp", (s, 0))
        if s == QB:
            emit(tail[0])
            emit(tail[1])
            add("z", 1)
        fill(f)
        if s < QB:
            add("scores", (s, 1))
            add("exp", (s, 1))
        if s >= 1:
            add("values", s - 1)
        if s < QB:
            add("mix", s)
        if s >= 1:
            add("o_norm", s - 1)
        fill(f)
    add("z", 2)
    emit(tail[2])
    emit(tail[3])
    add("z", 3)
    add("chunk", 0)
    add("attn_out", QB - 1)
    add("store_attn")
    add("decay", 1)
    units = [[("z", a, 0)] for a in range(4, QB + 1)]
    units[-1].append(("split", TCB, 0))
    conv, tail = half_pieces([TCB, TCC, TCH, TGC], 0)
    if last:
        for n in range(len(conv)):
            if ("split", TGC, 0) in conv[n]:
                conv[n].append(("out_load", 0, 0))
        units += conv
    else:
        more = half_pieces([TQ, TK, TV], 1)[0]
        for n, unit in enumerate(tail):
            more[n] += unit
        tail = []
        units += conv + more
    slots = LAST_FILL if last else SCAN_FILL
    fill = filler(units, sum(slots))
    for c in range(1, CH + 3):
        f = slots[c - 1] / 3
        if c < CH:
            add("chunk", c)
        if 1 <= c - 2 < CH:
            add("norm", c - 2)
        fill(f)
        if c - 1 < CH:
            add("scan", c - 1)
            if 0 < c < CH - 1:
                add("carry", c)
        if c + 1 < CH:
            add("decay", c + 1)
        fill(f)
        if 1 <= c - 2 < CH:
            add("ssm_out", c - 2)
        fill(f)
        if c == CH and last:
            for unit in tail:
                emit(unit)
            add("out_split", 0)
            add("out_split", 1)
            add("out_begin")
    add("store_ssm")
    if last:
        add("out_split", 2)
        add("out_split", 3)
    return out


ATT_FILL = (2, 2, 2, 2, 2, 2, 2, 2, 0)
SCAN_FILL = (1,) * 10 + (0,)
LAST_FILL = (1,) * 9 + (0, 0)
BODY = schedule(False)
LAST = schedule(True)
AHEAD = [("load", 0, 1), ("load", 1, 1), ("split", 0, 1)] + [s for s in BODY if s[2] == 1 and s[:2] not in (("load", 0), ("load", 1), ("split", 0))]
DVE_OWN = 82


class Chain:

    def __init__(self, sem, per):
        self.sem, self.per, self.base, self.n, self.before = sem, per, 0, 0, None

    def begin(self, i):
        if self.before is None:
            self.before = self.n
        self.base, self.n = self.before + i * self.per, 0

    def end(self):
        assert self.n == self.per, self.n

    def __call__(self, eng, ins):
        self.n += 1
        ins.then_inc(self.sem, 1)
        eng.wait_ge(self.sem, self.base + self.n)


def token_cols(c):
    return (0, META) if c == 0 else (META + P * (c - 1), META + P * c)


def build(nc, x, meta_tokens, norm_w, w_in, w_out, attn_lambda, attn_norm_w, sconv_w, ssm_conv_w,
          ssm_conv_b, ssm_a_log, ssm_dt_bias, ssm_d, ssm_norm_w, final_norm_w, out, y_dram, acum_dram):
    x_rows = x.rearrange("b t d -> (b t) d")
    out_rows = out.rearrange("b t d -> (b t) d")
    w_in_t = w_in.rearrange("a (k p) n -> p (a k) n", p=P)
    w_out_rows = w_out.rearrange("a k n -> (a k) n")

    with ExitStack() as ctx:
        def sb(name, shape, dt=F32):
            return ctx.enter_context(nc.sbuf_tensor(name, shape, dt))

        def sem(name):
            return ctx.enter_context(nc.semaphore(name))

        u_hi = sb("u_hi", [P, KD, LP], F32R)
        u_lo = sb("u_lo", [P, KD, LP], F32R)
        w_raw = sb("w_raw", [P, 2, KD, P])
        w_hi = sb("w_hi", [P, 2, KD, P], F32R)
        w_lo = sb("w_lo", [P, 2, KD, P], F32R)
        wd_raw, wd_hi, wd_lo = (w[:, 1, :, 0:SH] for w in (w_raw, w_hi, w_lo))

        work = sb("work", [P, 12528])
        taken = [0]

        def part(n):
            taken[0] += n
            return work[:, taken[0] - n:taken[0]]

        q_map = [part(LP), part(LP)]
        k_t = part(LP)
        v_t = part(LP)
        gate = part(LP)
        prob_flat = part(2 * L)
        prob = [prob_flat[:, 0:L], prob_flat[:, L:2 * L]]
        z_n = prob_flat[:, 0:QB * GW].rearrange("p (c n) -> p c n", c=QB)
        xs_flat = part(2 * LP)
        xs = xs_flat.rearrange("p (t n) -> p t n", t=2)
        dt_row = xs_flat[0:SH, 0:CH * P]
        b_t = part(LP)
        c_t = part(LP)
        raw = part(3 + LP)
        y_raw = work[:, 0:OB * T].rearrange("p (b n) -> p b n", b=OB)
        h_res = work[:, OB * T:OB * T + QB * D].rearrange("p (t d) -> p t d", t=QB)
        assert OB * T <= 4 * LP and OB * T + QB * D <= taken[0] <= 12528
        y_hi = u_hi[:, :, :].rearrange("p k n -> p (k n)")[:, 0:OB * T].rearrange("p (b n) -> p b n", b=OB)
        y_lo = u_lo[:, :, :].rearrange("p k n -> p (k n)")[:, 0:OB * T].rearrange("p (b n) -> p b n", b=OB)
        wo_raw = w_raw[:, :, :, :].rearrange("p b k n -> p (b k n)").rearrange("p (b n) -> p b n", b=OB)
        wo_hi = w_hi[:, :, :, :].rearrange("p b k n -> p (b k n)").rearrange("p (b n) -> p b n", b=OB)
        wo_lo = w_lo[:, :, :, :].rearrange("p b k n -> p (b k n)").rearrange("p (b n) -> p b n", b=OB)

        th_tile = sb("th_tile", [P, LP])
        th_piece = sb("th_piece", [P, 2, PW])
        v_blk = sb("v_blk", [P, QB, P])
        a_t = sb("a_t", [P, QB, P])
        conv_b_s = sb("conv_b_s", [P, LP])
        conv_u = sb("conv_u", [P, 2 + LP])
        conv_g = sb("conv_g", [P, LP])
        conv_y = sb("conv_y", [P, T])
        w_fin = conv_y[:, :]
        acum_b = sb("acum_b", [P, 2, R, P])
        lm_buf = sb("lm_buf", [P, 3 + LP])
        lmat = lm_buf[:, 0:2 * R * P].rearrange("p (b r n) -> p b r n", b=2, r=R)
        raws = [raw, lm_buf[:, :]]
        xdt = sb("xdt", [P, 2, GW])
        xdd = sb("xdd", [P, 2, GW])
        xd = sb("xd", [P, 2, GW])
        b_n = sb("b_n", [P, 2, P])
        cbm = sb("cbm", [P, 2, P])
        state = sb("state", [P, GW])
        state_d = sb("state_d", [P, GW])
        y_a = sb("y_a", [P, GW])
        v_meta = y_a[0:META, 0:P]
        o_n = y_a[:, P:2 * P]
        y_n = sb("y_n", [P, 2, GW])
        a_meta = sb("a_meta", [META, P])
        o_squares = sb("o_squares", [P, P])
        ys = sb("ys", [P, 2, T])

        ident = sb("ident", [P, P])
        ident_b = sb("ident_b", [P, P], BF16)
        mask_b = sb("mask_b", [P, P], BF16)
        tri = sb("tri", [P, P])
        ones = sb("ones", [P, P])
        valid = sb("valid", [P, 1])
        m_half = sb("m_half", [P, 1])
        rows = conv_g[:, 0:P]
        par = sb("par", [P, R_END])
        par_cw = sb("par_cw", [P, 4, 4])
        par_cb = sb("par_cb", [P, 4])
        par_cbh = sb("par_cbh", [P, 4])
        par_sw = sb("par_sw", [P, 3])
        par_sn = sb("par_sn", [P, 2])
        a_norm = sb("a_norm", [P, 1])
        lam_in = conv_b_s[0:1, 0:4 * QK].rearrange("p (r d) -> p r d", r=4)
        lam_p = conv_b_s[0:1, 4 * QK:6 * QK].rearrange("p (r d) -> p r d", r=2)
        lam_s = sb("lam_s", [1, 8])
        n_lam = sb("n_lam", [P, 1])
        dt_bias = sb("dt_bias", [SH, 1])
        a_bc = sb("a_bc", [P, SH])
        d_bc = sb("d_bc", [P, SH])
        sp = conv_y[:, 0:6 * CH * SH].rearrange("p (s n) -> p s n", s=6)
        stat = sb("stat", [P, 5, CH, SH])
        sg = sb("sg", [P, 5, CH, R])
        small = sb("small", [P, 96])
        used = [0]

        def few(n):
            used[0] += n
            return small[:, used[0] - n:used[0]]

        dg = few(R)
        ss = few(2)
        ms = few(2)
        rs = few(2)
        mx = few(2)
        psum_e = few(4).rearrange("p (b m) -> p b m", b=2)
        rinv = few(4).rearrange("p (b m) -> p b m", b=2)
        cmix = few(1)
        o_ss = few(1)
        o_ms = few(1)
        o_fit = few(1)
        o_rs = few(1)
        z_ss = few(2)
        z_ms = few(2)
        z_rs = few(2)
        f_ss = few(2 * QB)
        f_m0 = few(QB)
        f_ms = few(QB)
        f_rs = few(QB)

        ps = ctx.enter_context(nc.psum_tensor("ps", [P, 8, 512], F32))
        pb = [ps[:, 0, :], ps[:, 1, :]]
        s_ps = ps[:, 2:5, :].rearrange("p b n -> p (b n)")
        t_ps = [ps[:, 5, :], ps[:, 6, :]]
        o_ps = ps[:, 7, :]
        x_ps = [ps[:, 2, :], ps[:, 3, :]]
        y_ps = [ps[:, 4, :], ps[:, 5, :]]
        st_ps = ps[:, 6, :]
        yt_ps = ps[:, 7, :]
        u_ps = [ps[:, 2:4, :].rearrange("p b n -> p (b n)"), ps[:, 5:7, :].rearrange("p b n -> p (b n)")]

        params_in = sem("params_in")
        x_in = [sem("x_in0"), sem("x_in1")]
        consts = sem("consts")
        x_sq = sem("x_sq")
        x_ms = sem("x_ms")
        x_rs = sem("x_rs")
        x_n = sem("x_n")
        x_tr = sem("x_tr")
        u_prod = sem("u_prod")
        u_hi_ok = sem("u_hi_ok")
        u_lo_ok = sem("u_lo_ok")
        par_tr = sem("par_tr")
        par_ok = sem("par_ok")
        lam_sum = sem("lam_sum")
        lam_exp = sem("lam_exp")
        lam_row = sem("lam_row")
        lam_pe = sem("lam_pe")
        lam_ok = sem("lam_ok")
        wd_in = sem("wd_in")
        dt_pe = sem("dt_pe")
        dt_row_ok = sem("dt_row_ok")
        dt_tr = sem("dt_tr")
        dt_x = sem("dt_x")
        dt_e = sem("dt_e")
        adt_ok = sem("adt_ok")
        cum_pe = sem("cum_pe")
        acum_ok = sem("acum_ok")
        acum_tr = sem("acum_tr")
        acum_row = sem("acum_row")
        acum_st = sem("acum_st")
        stat_x = sem("stat_x")
        stat_e = sem("stat_e")
        stat_ok = sem("stat_ok")
        w_in_ok = [sem("w_in_ok0"), sem("w_in_ok1")]
        w_hi_ok = sem("w_hi_ok")
        w_lo_ok = sem("w_lo_ok")
        piece_done = sem("piece_done")
        bank_free = [sem("bank_free0"), sem("bank_free1")]
        q_ok = sem("q_ok")
        k_ok = sem("k_ok")
        v_ok = sem("v_ok")
        th_ok = sem("th_ok")
        gate_ok = sem("gate_ok")
        raw_ok = sem("raw_ok")
        raw_free = sem("raw_free")
        thc_ok = sem("thc_ok")
        conv_ok = sem("conv_ok")
        v_tr = sem("v_tr")
        v_blk_ok = sem("v_blk_ok")
        v_meta_ok = sem("v_meta_ok")
        s_done = sem("s_done")
        max_ok = sem("max_ok")
        exp_ok = sem("exp_ok")
        mix_ok = sem("mix_ok")
        a_tr = sem("a_tr")
        a_t_ok = sem("a_t_ok")
        a_m_ok = sem("a_m_ok")
        o_done = sem("o_done")
        o_sq = sem("o_sq")
        o_c_ok = sem("o_c_ok")
        o_ms_ok = sem("o_ms_ok")
        o_rs_ok = sem("o_rs_ok")
        o_n_ok = sem("o_n_ok")
        o_tr = sem("o_tr")
        attn_ok = sem("attn_ok")
        attn_st = sem("attn_st")
        convg_ok = sem("convg_ok")
        convg_st = sem("convg_st")
        acum_in = [sem("acum_in0"), sem("acum_in1")]
        seg_ok = sem("seg_ok")
        l_ok = sem("l_ok")
        x_done = sem("x_done")
        xdt_ok = sem("xdt_ok")
        x_free = sem("x_free")
        xdd_ok = sem("xdd_ok")
        g_ok = sem("g_ok")
        scan_done = sem("scan_done")
        sd_ok = sem("sd_ok")
        state_ok = sem("state_ok")
        zth_ok = sem("zth_ok")
        y_gated = sem("y_gated")
        z_sq = sem("z_sq")
        z_ms_ok = sem("z_ms_ok")
        z_rs_ok = sem("z_rs_ok")
        y_n_ok = sem("y_n_ok")
        y_tr = sem("y_tr")
        ys_ok = sem("ys_ok")
        ssm_st = sem("ssm_st")
        yw_in = [sem(f"yw_in{b}") for b in range(OB)]
        yw_hi = sem("yw_hi")
        y_lo_ok = sem("y_lo_ok")
        wo_lo_ok = sem("wo_lo_ok")
        out_k = sem("out_k")
        x_res = sem("x_res")
        out_bank = sem("out_bank")
        h_ok = sem("h_ok")
        f0_ok = sem("f0_ok")
        f_m0_ok = sem("f_m0_ok")
        hw_ok = sem("hw_ok")
        f_sq = sem("f_sq")
        f_ms_ok = sem("f_ms_ok")
        f_rs_ok = sem("f_rs_ok")
        f_ok = sem("f_ok")
        out_st = sem("out_st")
        dve_own = Chain(sem("dve_own"), DVE_OWN)
        act_own = Chain(sem("act_own"), 0)
        pool_own = Chain(sem("pool_own"), 0)


        primed = [a_m_ok, convg_ok, a_t_ok, a_tr, attn_ok, conv_ok, exp_ok, g_ok, mix_ok, o_ms_ok, o_sq, out_k, piece_done, raw_free, s_done, scan_done, seg_ok, state_ok, v_tr, w_lo_ok, wo_lo_ok, x_free, xdd_ok, y_gated, y_lo_ok, y_tr, ys_ok, z_ms_ok, *bank_free]
        primed_dma = [attn_st, convg_st, ssm_st]

        block = ctx.enter_context(nc.Block())

        @block.sync
        def _(eng):
            def load_x(r):
                if r >= 2:
                    eng.wait_ge(x_tr, r - 1)
                if r == 0:
                    eng.dma_start(prob[0][0:META, 0:D], meta_tokens).then_inc(x_in[0], 16)
                else:
                    eng.dma_start(prob[r % 2][:, 0:D], x_rows[(r - 1) * P:r * P, :]).then_inc(x_in[r % 2], 16)

            for guard in primed:
                eng.sem_inc(guard, 1)
            eng.sem_inc(raw_free, 1)
            for guard in primed_dma:
                eng.sem_inc(guard, 16)
            load_x(0)
            load_x(1)
            eng.dma_start(rows[R_CW:R_CB, :], ssm_conv_w.rearrange("a j (t c) -> (a j t) c", c=P)).then_inc(params_in, 16)
            eng.dma_start(rows[R_CB:R_SW, :], ssm_conv_b.rearrange("a (t c) -> (a t) c", c=P)).then_inc(params_in, 16)
            eng.dma_start(rows[R_SW:R_SN, :], sconv_w.rearrange("a j (t c) -> (a j t) c", c=P)).then_inc(params_in, 16)
            eng.dma_start(rows[R_SN:R_NW, :], ssm_norm_w.rearrange("a (t c) -> (a t) c", c=P)).then_inc(params_in, 16)
            eng.dma_start(rows[R_NW:R_AN, :], norm_w.rearrange("a (t c) -> (a t) c", c=P)).then_inc(params_in, 16)
            eng.dma_start(rows[R_AN:R_END, :], attn_norm_w).then_inc(params_in, 16)
            eng.dma_start(lam_in[:, :, :], attn_lambda).then_inc(params_in, 16)
            eng.dma_start(dt_bias[:, :], ssm_dt_bias.rearrange("a h -> h a")).then_inc(params_in, 16)
            eng.dma_start(a_bc[:, :], ssm_a_log[0, :].partition_broadcast(P)).then_inc(params_in, 16)
            eng.dma_start(d_bc[:, :], ssm_d[0, :].partition_broadcast(P)).then_inc(params_in, 16)
            eng.dma_start(wd_raw, w_in_t[:, :, C_DT:C_DT + SH]).then_inc(wd_in, 16)
            for r in range(2, CH):
                load_x(r)
            eng.wait_ge(acum_row, 1)
            eng.dma_start(acum_dram, dt_row[:, :]).then_inc(acum_st, 16)
            eng.wait_ge(acum_st, 16)
            x_tiles = x_rows.rearrange("(t p) d -> p t d", p=P)

            def load_out(half, k, b):
                eng.dma_start(y_raw[:, b, :], y_dram[bass.ds(k * P, P), :]).then_inc(yw_in[b], 16)
                eng.dma_start(wo_raw[:, b, :], w_out_rows[bass.ds(k * P, P), half * HALF:(half + 1) * HALF]).then_inc(yw_in[b], 16)

            def iteration(i, steps):
                for step, a, d in steps:
                    it = i + d
                    if step == "load":
                        at, by = TILES[a]
                        eng.wait_ge(w_lo_ok, it * NT + a + 1)
                        eng.dma_start(w_raw[:, a % 2, :, :], w_in_t[:, :, bass.ds(it * by + at, P)]).then_inc(w_in_ok[a % 2], 16)
                    elif step == "store_attn":
                        eng.wait_ge(attn_ok, it * QB + QB + 1)
                        eng.dma_start(y_dram[bass.ds(it * P, P), :], gate[:, META:L]).then_inc(attn_st, 16)
                    elif step == "conv" and a == 4:
                        eng.wait_ge(convg_ok, it + 2)
                        eng.dma_start(y_dram[bass.ds(it * P + HEADS * P, P), :], conv_y[:, :]).then_inc(convg_st, 16)
                    elif step == "decay":
                        eng.wait_ge(seg_ok, it * QB + max(a - 2, 0) + 1)
                        eng.dma_start(acum_b[:, a % 2, :, :],
                                      acum_dram[bass.ds(it * R, R), a * P:(a + 1) * P].partition_broadcast(P)).then_inc(acum_in[a % 2], 16)
                    elif step == "store_ssm":
                        eng.wait_ge(ys_ok, it * QB + QB + 1)
                        for t in range(2):
                            eng.dma_start(y_dram[bass.ds(it * GW + (2 * HEADS + t) * P, P), :], ys[:, t, :]).then_inc(ssm_st, 16)
                    elif step == "out_load":
                        eng.wait_ge(attn_st, 16 * HEADS + 16)
                        eng.wait_ge(s_done, HEADS * 2 * QB + 1)
                        eng.wait_ge(v_tr, HEADS + 1)
                        eng.wait_ge(w_lo_ok, HEADS * NT + 2)
                        for b in range(OB):
                            load_out(0, b, b)

            iteration(-1, AHEAD)
            with eng.Fori(0, HEADS - 1) as i:
                iteration(i, BODY)
            iteration(HEADS - 1, LAST)

            def load_group(half, g):
                for b in range(OB):
                    n = half * KO + OB * g + b
                    eng.wait_ge(y_lo_ok, n - OB + 2)
                    eng.wait_ge(wo_lo_ok, n - OB + 2)
                    load_out(half, OB * g + b, b)

            eng.wait_ge(convg_st, 16 * HEADS + 16)
            eng.wait_ge(ssm_st, 32 * HEADS + 16)
            eng.wait_ge(scan_done, HEADS * CH + 1)
            eng.wait_ge(g_ok, HEADS * QB + 1)
            eng.dma_start(w_fin, final_norm_w.partition_broadcast(P)).then_inc(x_res, 16)
            with eng.Fori(1, KO // OB) as g:
                load_group(0, g)
                eng.dma_start(h_res[:, bass.ds(2 * g - 2, 2), :], x_tiles[:, bass.ds(2 * g - 2, 2), :]).then_inc(x_res, 16)
            eng.dma_start(h_res[:, QB - 2:QB, :], x_tiles[:, QB - 2:QB, :]).then_inc(x_res, 16)
            with eng.Fori(0, KO // OB) as g:
                load_group(1, g)
            for t in range(QB):
                eng.wait_ge(f_ok, t + 1)
                eng.wait_ge(f0_ok, t + 1)
                eng.dma_start(out_rows[t * P:(t + 1) * P, :], h_res[:, t, :]).then_inc(out_st, 16)
            eng.wait_ge(out_st, 16 * QB)

        @block.gpsimd
        def _(eng):
            own = pool_own
            own(eng, eng.memset(ident[:, :], 0.0))
            own(eng, eng.memset(mask_b[:, :], 0.0))
            own(eng, eng.memset(tri[:, :], 1.0))
            own(eng, eng.memset(valid[:, :], 1.0))
            eng.affine_select(out=ident[:, :], in_=ident[:, :], compare_op=ALU.not_equal, fill=1.0, base=0,
                              pattern=[[-1, P]], channel_multiplier=1).then_inc(consts, 1)
            eng.affine_select(out=mask_b[:, :], in_=mask_b[:, :], compare_op=ALU.is_ge, fill=MASK, base=0,
                              pattern=[[-1, P]], channel_multiplier=1).then_inc(consts, 1)
            eng.affine_select(out=tri[:, :], in_=tri[:, :], compare_op=ALU.is_ge, fill=0.0, base=0,
                              pattern=[[1, P]], channel_multiplier=-1).then_inc(consts, 1)
            eng.affine_select(out=valid[:, :], in_=valid[:, :], compare_op=ALU.is_ge, fill=0.0, base=META - 1,
                              pattern=[[0, 1]], channel_multiplier=-1).then_inc(consts, 1)
            eng.memset(ones[:, :], 1.0).then_inc(consts, 1)
            eng.memset(m_half[:, :], -0.5).then_inc(consts, 1)
            eng.memset(u_hi[:, :, L:LP].bitcast(F32), 0.0).then_inc(consts, 1)
            eng.memset(u_lo[:, :, L:LP].bitcast(F32), 0.0).then_inc(consts, 1)
            eng.wait_ge(consts, 8)

            def power(n, to, of, rows_=P):
                return eng.tensor_tensor(to[0:rows_, n:n + 1], of[0:rows_, n:n + 1], m_half[0:rows_, :], ALU.pow)

            def x_power(r):
                eng.wait_ge(x_ms, r + 1)
                power(r % 2, rs, ms, META if r == 0 else P).then_inc(x_rs, 1)

            x_power(0)
            for r in range(CH):
                if r + 1 < CH:
                    x_power(r + 1)
                a, b = token_cols(r)
                src = (k_t, v_t)[r % 2][:, 0:KD * (b - a)].rearrange("p (k n) -> p k n", k=KD)
                eng.wait_ge(u_hi_ok, r + 1)
                eng.tensor_tensor(u_lo[:, :, a:b], src, u_hi[:, :, a:b].bitcast(F32), ALU.subtract).then_inc(u_lo_ok, 1)
            eng.wait_ge(w_hi_ok, 1)
            eng.tensor_tensor(wd_lo, wd_raw, wd_hi.bitcast(F32), ALU.subtract).then_inc(w_lo_ok, 1)
            def low_w(n, b):
                eng.wait_ge(yw_hi, n + 1)
                eng.tensor_tensor(wo_lo[:, b, :], wo_raw[:, b, :], wo_hi[:, b, :].bitcast(F32), ALU.subtract).then_inc(wo_lo_ok, 1)

            def iteration(i, steps):
                for step, a, d in steps:
                    it = i + d
                    if step == "split":
                        eng.wait_ge(w_hi_ok, it * NT + a + 2)
                        eng.tensor_tensor(w_lo[:, a % 2, :, :], w_raw[:, a % 2, :, :],
                                          w_hi[:, a % 2, :, :].bitcast(F32), ALU.subtract).then_inc(w_lo_ok, 1)
                    elif step == "o_norm":
                        eng.wait_ge(o_ms_ok, it * QB + a + 2)
                        power(0, o_rs, o_ms).then_inc(o_rs_ok, 1)
                    elif step == "chunk" and a < CH - 1:
                        n = META if a == 0 else P
                        eng.wait_ge(xdt_ok, it * CH + a + 1)
                        eng.wait_ge(scan_done, it * CH + max(a - 1, 0) + 1)
                        eng.tensor_tensor(xdd[0:n, a % 2, :].rearrange("p (r d) -> p r d", r=R),
                                          xdt[0:n, a % 2, :].rearrange("p (r d) -> p r d", r=R),
                                          sg[0:n, 2, a, :].unsqueeze(2).to_broadcast([n, R, HD]), ALU.mult).then_inc(xdd_ok, 1)
                    elif step == "carry":
                        eng.wait_ge(state_ok, it * (CH - 1) + a + 1)
                        eng.tensor_tensor(state_d[:, :].rearrange("p (r d) -> p r d", r=R),
                                          state[:, :].rearrange("p (r d) -> p r d", r=R),
                                          sg[:, 4, a, :].unsqueeze(2).to_broadcast([P, R, HD]), ALU.mult).then_inc(sd_ok, 1)
                    elif step == "norm":
                        eng.wait_ge(z_ms_ok, it * QB + a + 1)
                        power(a % 2, z_rs, z_ms).then_inc(z_rs_ok, 1)
                    elif step == "out_split":
                        low_w(a, a)

            iteration(-1, AHEAD)
            with eng.Fori(0, HEADS - 1) as i:
                iteration(i, BODY)
            iteration(HEADS - 1, LAST)

            with eng.Fori(1, 2 * KO // OB) as g:
                for b in range(OB):
                    low_w(OB * g + b, b)
            for t in range(QB):
                eng.wait_ge(f_ms_ok, t + 1)
                power(t, f_rs, f_ms).then_inc(f_rs_ok, 1)

        @block.scalar
        def _(eng):
            def x_square(r):
                n = META if r == 0 else P
                eng.wait_ge(x_in[r % 2], 16 * (r // 2 + 1))
                eng.wait_ge(x_ms, max(r - 1, 0))
                eng.wait_ge(x_sq, r)
                eng.activation(th_tile[0:n, 0:D], prob[r % 2][0:n, 0:D], ACT.Square,
                               accum_out=ss[0:n, r % 2:r % 2 + 1]).then_inc(x_sq, 1)

            x_square(0)
            for r in range(CH):
                if r + 1 < CH:
                    x_square(r + 1)
                a, b = token_cols(r)
                src = (k_t, v_t)[r % 2][:, 0:KD * (b - a)].rearrange("p (k n) -> p k n", k=KD)
                eng.wait_ge(u_prod, r + 1)
                eng.copy(u_hi[:, :, a:b], src).then_inc(u_hi_ok, 1)
            eng.wait_ge(lam_sum, 1)
            eng.activation(lam_s[:, 2:4], lam_s[:, 0:2], ACT.Exp).then_inc(lam_exp, 1)
            eng.wait_ge(wd_in, 16)
            eng.copy(wd_hi, wd_raw).then_inc(w_hi_ok, 1)
            eng.activation(a_bc[:, :], a_bc[:, :], ACT.Exp).then_inc(lam_exp, 1)
            eng.wait_ge(dt_x, 1)
            eng.activation(sp[:, 1, :], sp[:, 0, :], ACT.Abs).then_inc(dt_e, 1)
            eng.wait_ge(dt_e, 1)
            eng.activation(sp[:, 2, :], sp[:, 1, :], ACT.Exp, scale=-1.0).then_inc(dt_e, 1)
            eng.wait_ge(stat_x, 1)
            for n in (2, 3, 4):
                ins = eng.activation(stat[:, n, :, :], stat[:, n, :, :], ACT.Exp)
            ins.then_inc(stat_e, 1)

            def high(n, b):
                eng.wait_ge(yw_in[b], (n - b) * (32 // OB) + 32)
                eng.copy(y_hi[:, b, :], y_raw[:, b, :])
                eng.copy(wo_hi[:, b, :], wo_raw[:, b, :]).then_inc(yw_hi, 1)

            def iteration(i, steps):
                for step, a, d in steps:
                    it = i + d
                    if step == "split":
                        b = a % 2
                        free = it * PPI + {0: -PIECES, 1: 0, TCB: PZ + QB, TCC: PZ + QB}.get(a, first_piece(max(a - 1, 0)))
                        eng.wait_ge(w_in_ok[b], it * (16 * NT // 2) + 16 * (a // 2 + 1))
                        if a >= 2 or steps is not AHEAD:
                            eng.wait_ge(piece_done, free + 1)
                        if a == 1:
                            eng.wait_ge(dt_pe, PIECES)
                        eng.copy(w_hi[:, b, :, :], w_raw[:, b, :, :]).then_inc(w_hi_ok, 1)
                    elif step == "piece":
                        t, tc = tile_of(a)
                        cols = slice(tc * PW, (tc + 1) * PW)
                        src = pb[a % 2][:, 0:PW]
                        if t not in (TK, TCH):
                            eng.wait_ge(piece_done, it * PPI + a + 2)
                        if t == TQ:
                            eng.wait_ge(s_done, it * 2 * QB + 1)
                            eng.mul(q_map[0][0:QK, cols], src[0:QK, :], QK ** -0.5)
                            eng.mul(q_map[1][QK:P, cols], src[QK:P, :], QK ** -0.5).then_inc(bank_free[a % 2], 1)
                        elif t == TV:
                            eng.wait_ge(v_tr, it + 1)
                            eng.copy(v_t[:, cols], src).then_inc(bank_free[a % 2], 1)
                        elif t == TCB:
                            eng.wait_ge(convg_ok, it + 1)
                            eng.copy(conv_b_s[:, cols], src).then_inc(bank_free[a % 2], 1)
                        elif t == TCC:
                            eng.wait_ge(convg_ok, it + 1)
                            eng.copy(conv_u[:, 2 + tc * PW:2 + (tc + 1) * PW], src).then_inc(bank_free[a % 2], 1)
                        elif t in (TG, TGC):
                            eng.activation(th_piece[:, a % 2, :], src, ACT.Tanh, scale=0.5).then_inc(th_ok, 1)
                        elif TXS0 <= t <= TC:
                            eng.wait_ge(raw_free, it * 4 + t - TXS0 + 1)
                            if t == TXS1:
                                eng.wait_ge(scan_done, it * CH + 1)
                            eng.copy(raws[(t - TXS0) % 2][:, 3 + tc * PW:3 + (tc + 1) * PW], src).then_inc(bank_free[a % 2], 1)
                    elif step == "gate_taps":
                        n = a - TXS0
                        eng.wait_ge(raw_free, it * 4 + n + 3)
                        dst = (xs[:, 0, :], xs[:, 1, :], b_t, c_t)[n]
                        eng.wait_ge(conv_ok, it * 4 + n + 1)
                        eng.activation(th_tile[:, :], dst, ACT.Tanh, scale=0.5).then_inc(thc_ok, 1)
                    elif step == "turn_v":
                        eng.wait_ge(v_blk_ok, it + 1)
                        eng.copy(v_blk[:, 4:8, :], t_ps[1][:, :])
                        eng.copy(v_meta, o_ps[0:META, 0:P]).then_inc(v_meta_ok, 1)
                    elif step == "exp":
                        s, m = a
                        nk = P * (s + 1) + META
                        eng.wait_ge(max_ok, it * 2 * QB + 2 * s + m + 1)
                        if m == 0:
                            eng.wait_ge(a_tr, it * QB + s + 1)
                        else:
                            eng.wait_ge(mix_ok, it * QB + s + 1)
                        eng.activation(prob[m][:, 0:nk], s_ps[:, 0:nk], ACT.Exp, bias=mx[:, m:m + 1],
                                       accum_out=psum_e[:, s % 2, m:m + 1]).then_inc(exp_ok, 1)
                    elif step == "turn":
                        eng.wait_ge(a_tr, it * QB + a + 2)
                        if a >= 4:
                            eng.copy(a_t[:, 4:a + 1, :], t_ps[1][:, 0:P * (a - 3)])
                        eng.copy(a_meta[:, :], o_ps[0:META, 0:P]).then_inc(a_m_ok, 1)
                    elif step == "values":
                        eng.wait_ge(o_c_ok, it * QB + a + 1)
                        eng.wait_ge(o_ms_ok, it * QB + a + 1)
                        eng.wait_ge(o_sq, it * QB + a + 1)
                        eng.activation(o_squares[:, :], o_n, ACT.Square, accum_out=o_ss[:, :]).then_inc(o_sq, 1)
                    elif step == "decay":
                        eng.wait_ge(seg_ok, it * QB + a + 1)
                        eng.activation(lmat[:, a % 2, :, :], lmat[:, a % 2, :, :], ACT.Exp).then_inc(l_ok, 1)
                    elif step == "z":
                        p = PZ + a - 1
                        eng.wait_ge(piece_done, it * PPI + p + 2)
                        eng.activation(th_piece[:, p % 2, 0:GW], pb[p % 2][:, 0:GW], ACT.Tanh, scale=0.5).then_inc(zth_ok, 1)
                    elif step == "norm":
                        n = it * QB + a
                        eng.wait_ge(y_gated, n + 1)
                        eng.wait_ge(z_ms_ok, n - 1 + 1)
                        eng.activation(th_tile[:, 0:GW], y_n[:, a % 2, :], ACT.Square, accum_out=z_ss[:, a % 2:a % 2 + 1]).then_inc(z_sq, 1)
                        eng.wait_ge(z_rs_ok, n)
                        eng.activation(y_n[:, a % 2, :], y_n[:, a % 2, :], ACT.Copy, scale=z_rs[:, a % 2:a % 2 + 1]).then_inc(y_n_ok, 1)
                    elif step == "ssm_out":
                        n = it * QB + a
                        eng.wait_ge(y_tr, n + 1)
                        if a == 1:
                            eng.wait_ge(ssm_st, it * 32 + 16)
                        for t in range(2):
                            ins = eng.activation(ys[:, t, (a - 1) * P:a * P], yt_ps[:, t * P:(t + 1) * P], ACT.Copy, scale=par_sn[:, t:t + 1])
                        ins.then_inc(ys_ok, 1)
                    elif step == "out_split":
                        eng.wait_ge(piece_done, HEADS * PPI + 1)
                        high(a, a)

            iteration(-1, AHEAD)
            with eng.Fori(0, HEADS - 1) as i:
                iteration(i, BODY)
            iteration(HEADS - 1, LAST)

            with eng.Fori(1, KO // OB) as g:
                for b in range(OB):
                    eng.wait_ge(out_k, OB * g + b - OB + 2)
                    high(OB * g + b, b)
            for b in range(OB):
                if b < OB - 2:
                    eng.wait_ge(out_k, KO + b - OB + 2)
                else:
                    eng.wait_ge(out_bank, QB)
                high(KO + b, b)
            for t in range(QB):
                eng.wait_ge(h_ok, t + 1)
                if t > 0:
                    eng.wait_ge(f_sq, t)
                eng.activation(th_tile[:, 0:HALF], h_res[:, t, 0:HALF], ACT.Square, accum_out=f_ss[:, t:t + 1]).then_inc(f_sq, 1)
            with eng.Fori(KO // OB + 1, 2 * KO // OB) as g:
                for b in range(OB):
                    eng.wait_ge(out_k, OB * g + b - OB)
                    high(OB * g + b, b)
            for t in range(QB):
                n = QB + t
                eng.wait_ge(h_ok, n + 1)
                eng.wait_ge(f_sq, n)
                eng.activation(th_tile[:, 0:HALF], h_res[:, t, HALF:D], ACT.Square, accum_out=f_ss[:, n:n + 1]).then_inc(f_sq, 1)
                eng.wait_ge(f_rs_ok, t + 1)
                eng.wait_ge(hw_ok, t + 1)
                eng.activation(h_res[:, t, 0:HALF], h_res[:, t, 0:HALF], ACT.Copy, scale=f_rs[:, t:t + 1]).then_inc(f0_ok, 1)

        @block.vector
        def _(eng):
            own = dve_own
            own(eng, eng.memset(raw[:, 0:3], 0.0))
            own(eng, eng.memset(conv_u[:, 0:2], 0.0))
            eng.memset(q_map[0][QK:P, :], 0.0)
            own(eng, eng.memset(q_map[1][0:QK, :], 0.0))
            eng.memset(dt_row[:, META:P], 0.0)
            eng.wait_ge(consts, 8)
            own(eng, eng.tensor_copy(ident_b[:, :], ident[:, :]))
            eng.wait_ge(par_tr, 1)
            own(eng, eng.tensor_copy(par[:, :], o_ps[:, 0:R_END]))
            own(eng, eng.tensor_scalar(a_norm[:, :], par[:, R_AN:R_END], 0.5 * (1.0 - LAM_INIT), None, ALU.mult))
            eng.wait_ge(params_in, 160)
            own(eng, eng.tensor_scalar(d_bc[:, :], d_bc[:, :], 0.5, None, ALU.mult))
            own(eng, eng.tensor_tensor(lam_p[:, :, :], lam_in[:, 0:4:2, :], lam_in[:, 1:4:2, :], ALU.mult))
            eng.tensor_reduce(lam_s[:, 0:2], lam_p[:, :, :], AX.X, ALU.add).then_inc(lam_sum, 1)

            def x_mean(r):
                n = META if r == 0 else P
                eng.wait_ge(x_sq, r + 1)
                eng.tensor_scalar(ms[0:n, r % 2:r % 2 + 1], ss[0:n, r % 2:r % 2 + 1], 1.0 / D, EPS, ALU.mult, ALU.add).then_inc(x_ms, 1)

            def x_scale(r):
                n = META if r == 0 else P
                eng.wait_ge(x_rs, r + 1)
                eng.tensor_scalar(prob[r % 2][0:n, 0:D], prob[r % 2][0:n, 0:D], rs[0:n, r % 2:r % 2 + 1], None, ALU.mult).then_inc(x_n, 1)

            x_mean(0)
            x_scale(0)
            for r in range(CH):
                if r + 1 < CH:
                    x_mean(r + 1)
                    x_scale(r + 1)
                a, b = token_cols(r)
                dst = (k_t, v_t)[r % 2][:, 0:KD * (b - a)].rearrange("p (k n) -> p k n", k=KD)
                eng.wait_ge(x_tr, r + 1)
                eng.wait_ge(u_lo_ok, max(r - 1, 0))
                eng.tensor_tensor(dst, u_ps[r % 2].rearrange("p (k n) -> p k n", k=KD)[:, :, 0:b - a],
                                  par[:, R_NW:R_AN].unsqueeze(2).to_broadcast([P, KD, b - a]), ALU.mult).then_inc(u_prod, 1)
            eng.wait_ge(lam_exp, 1)
            own(eng, eng.tensor_tensor(lam_s[:, 4:5], lam_s[:, 2:3], lam_s[:, 3:4], ALU.subtract))
            eng.tensor_scalar(lam_s[:, 5:6], lam_s[:, 4:5], LAM_INIT, -1.0, ALU.add, ALU.mult).then_inc(lam_row, 1)
            eng.wait_ge(lam_pe, 1)
            eng.tensor_copy(n_lam[:, :], o_ps[:, 0:1]).then_inc(lam_ok, 1)
            eng.wait_ge(lam_ok, 1)

            eng.wait_ge(dt_pe, PIECES)
            for tc in range(PIECES):
                src = ps[0:SH, 5 + tc, :]
                lo = META if tc == 0 else 0
                hi = L - (PIECES - 1) * PW if tc == PIECES - 1 else PW
                if tc == 0:
                    eng.tensor_scalar(dt_row[:, 0:META], src[:, 0:META], dt_bias[:, :], None, ALU.add)
                at = tc * PW + P - META
                ins = eng.tensor_scalar(dt_row[:, at + lo:at + hi], src[:, lo:hi], dt_bias[:, :], None, ALU.add)
            ins.then_inc(dt_row_ok, 1)
            eng.wait_ge(dt_tr, 1)
            eng.tensor_copy(sp[:, 0, :], ps[:, 5, 0:CH * SH]).then_inc(dt_x, 1)
            eng.wait_ge(dt_e, 2)
            own(eng, eng.tensor_scalar(sp[:, 3, :], sp[:, 2, :], 2.0, None, ALU.add))
            own(eng, eng.reciprocal(sp[:, 4, :], sp[:, 3, :]))
            own(eng, eng.tensor_tensor(sp[:, 1, :], sp[:, 2, :], sp[:, 4, :], ALU.mult))
            own(eng, eng.tensor_tensor(sp[:, 3, :], sp[:, 1, :], sp[:, 1, :], ALU.mult))
            own(eng, eng.tensor_scalar(sp[:, 4, :], sp[:, 3, :], 1.0 / 17, None, ALU.mult))
            for n in range(15, 1, -2):
                own(eng, eng.scalar_tensor_tensor(sp[:, 4, :], sp[:, 4, :], 1.0 / n, sp[:, 3, :], ALU.add, ALU.mult))
            own(eng, eng.scalar_tensor_tensor(sp[:, 4, :], sp[:, 4, :], 1.0, sp[:, 1, :], ALU.add, ALU.mult))
            own(eng, eng.tensor_scalar(sp[:, 5, :], sp[:, 0, :], 0.0, None, ALU.max))
            own(eng, eng.scalar_tensor_tensor(sp[:, 5, :], sp[:, 4, :], 2.0, sp[:, 5, :], ALU.mult, ALU.add))
            own(eng, eng.tensor_scalar(sp[:, 5, 0:SH], sp[:, 5, 0:SH], valid[:, :], None, ALU.mult))
            own(eng, eng.tensor_scalar(stat[:, 0, :, :], sp[:, 5, :], 0.5, None, ALU.mult))
            eng.wait_ge(lam_exp, 2)
            eng.scalar_tensor_tensor(sp[:, 4, :].rearrange("p (c h) -> p c h", c=CH), sp[:, 5, :].rearrange("p (c h) -> p c h", c=CH), -1.0,
                                     a_bc[:, :].unsqueeze(1).to_broadcast([P, CH, SH]), ALU.mult, ALU.mult).then_inc(adt_ok, 1)
            eng.wait_ge(cum_pe, 1)
            eng.tensor_copy(stat[:, 1, :, :], o_ps[:, 0:CH * SH]).then_inc(acum_ok, 1)
            eng.wait_ge(acum_ok, 1)
            own(eng, eng.tensor_copy(stat[:, 4, :, :], o_ps[:, CH * SH:2 * CH * SH]))
            own(eng, eng.tensor_copy(stat[:, 3, :, :], stat[:, 1, :, :]))
            eng.tensor_tensor(stat[:, 2, :, :], stat[:, 4, :, :], stat[:, 1, :, :], ALU.subtract).then_inc(stat_x, 1)
            eng.wait_ge(acum_tr, 1)
            eng.tensor_copy(dt_row[:, 0:4 * P], ps[0:SH, 5, :])
            eng.tensor_copy(dt_row[:, 4 * P:8 * P], ps[0:SH, 6, :])
            eng.tensor_copy(dt_row[:, 8 * P:9 * P], ps[0:SH, 7, 0:P]).then_inc(acum_row, 1)
            eng.wait_ge(stat_e, 1)
            own(eng, eng.tensor_scalar(stat[:, 2:4, :, :], stat[:, 2:4, :, :], 0.5, None, ALU.mult))

            eng.wait_ge(acum_st, 16)

            def low_y(n, b):
                eng.wait_ge(yw_hi, n + 1)
                eng.tensor_tensor(y_lo[:, b, :], y_raw[:, b, :], y_hi[:, b, :].bitcast(F32), ALU.subtract).then_inc(y_lo_ok, 1)

            def iteration(i, steps):
                for step, a, d in steps:
                    it = i + d
                    if step == "params":
                        eng.wait_ge(scan_done, it * CH + 1)
                        eng.wait_ge(g_ok, it * QB + 1)
                        eng.wait_ge(ys_ok, it * QB + 1)
                        taps = par[:, R_CW:R_CB].rearrange("p (j t) -> p j t", j=4)
                        eng.tensor_copy(par_cw[:, :, 0:2], taps[:, :, bass.ds(2 * it, 2)])
                        eng.tensor_copy(par_cw[:, :, 2:3], taps[:, :, bass.ds(it + XT, 1)])
                        eng.tensor_copy(par_cw[:, :, 3:4], taps[:, :, bass.ds(it + XT + HEADS, 1)])
                        eng.tensor_copy(par_cb[:, 0:2], par[:, bass.ds(2 * it + R_CB, 2)])
                        eng.tensor_copy(par_cb[:, 2:3], par[:, bass.ds(it + R_CB + XT, 1)])
                        eng.tensor_copy(par_cb[:, 3:4], par[:, bass.ds(it + R_CB + XT + HEADS, 1)])
                        eng.tensor_copy(par_sw[:, :], par[:, R_SW:R_SN].rearrange("p (j t) -> p j t", j=3)[:, :, bass.ds(i, 1)])
                        eng.tensor_scalar(par_sn[:, :], par[:, bass.ds(2 * it + R_SN, 2)], 0.5, None, ALU.mult)
                        eng.tensor_copy(dg[:, :], d_bc[:, bass.ds(R * it, R)])
                        own(eng, eng.tensor_copy(sg[:, :, :, :].rearrange("p s c r -> p (s c) r"),
                                                 stat[:, :, :, :].rearrange("p s c h -> p (s c) h")[:, :, bass.ds(R * it, R)]))
                        own(eng, eng.memset(raws[1][:, 0:3], 0.0))
                    elif step == "piece":
                        t, tc = tile_of(a)
                        cols = slice(tc * PW, (tc + 1) * PW)
                        src = pb[a % 2][:, 0:PW]
                        done = bank_free[a % 2]
                        if t == TK:
                            eng.wait_ge(piece_done, it * PPI + a + 2)
                            eng.wait_ge(s_done, it * 2 * QB + 1)
                            eng.tensor_copy(k_t[:, cols], src).then_inc(done, 1)
                        elif t == TG:
                            eng.wait_ge(attn_st, it * 16 + 16)
                            eng.wait_ge(th_ok, it * 6 + tc + 1)
                            eng.scalar_tensor_tensor(gate[:, cols], th_piece[:, a % 2, :], 1.0, src, ALU.add, ALU.mult).then_inc(done, 1)
                        elif t == TCH:
                            eng.wait_ge(piece_done, it * PPI + a + 2)
                            eng.wait_ge(bank_free[(a - PIECES) % 2], it * (PPI // 2) + (a - PIECES) // 2 + 2)
                            c2 = slice(2 + tc * PW, 2 + (tc + 1) * PW)
                            eng.tensor_tensor(conv_u[:, c2], src, conv_u[:, c2], ALU.mult).then_inc(done, 1)
                        elif t == TGC:
                            eng.wait_ge(th_ok, it * 6 + 3 + tc + 1)
                            eng.scalar_tensor_tensor(conv_g[:, cols], th_piece[:, a % 2, :], 1.0, src, ALU.add, ALU.mult).then_inc(done, 1)
                    elif step == "taps":
                        t, j = a
                        n = t - TXS0
                        dst = (xs[:, 0, :], xs[:, 1, :], b_t, c_t)[n]
                        src = raws[n % 2]
                        if j == 0:
                            for b in range(2):
                                eng.wait_ge(bank_free[b], it * (PPI // 2) + (PIECES * (t + 1) + 1 - b) // 2 + 1)
                            own(eng, eng.tensor_scalar(dst, src[:, 0:LP], par_cw[:, 0, n:n + 1], par_cb[:, n:n + 1], ALU.mult, ALU.add))
                        else:
                            ins = eng.scalar_tensor_tensor(dst, src[:, j:j + LP], par_cw[:, j, n:n + 1], dst, ALU.mult, ALU.add)
                            if j < 3:
                                own(eng, ins)
                            else:
                                ins.then_inc(raw_free, 1)
                    elif step == "gate_taps":
                        n = a - TXS0
                        dst = (xs[:, 0, :], xs[:, 1, :], b_t, c_t)[n]
                        eng.wait_ge(thc_ok, it * 4 + n + 1)
                        eng.scalar_tensor_tensor(dst, th_tile[:, :], 1.0, dst, ALU.add, ALU.mult).then_inc(conv_ok, 1)
                    elif step == "turn_v":
                        eng.wait_ge(v_tr, it + 2)
                        eng.tensor_copy(v_blk[:, 0:4, :], t_ps[0][:, :]).then_inc(v_blk_ok, 1)
                    elif step == "scores":
                        s, m = a
                        nk = P * (s + 1) + META
                        n = it * 2 * QB + 2 * s + m
                        eng.wait_ge(s_done, n + 2)
                        if s > 0:
                            eng.wait_ge(exp_ok, n - 1 + 1)
                        eng.tensor_reduce(mx[:, m:m + 1], s_ps[:, 0:nk], AX.X, ALU.max, negate=True).then_inc(max_ok, 1)
                    elif step == "mix":
                        nk = P * (a + 1) + META
                        b = a % 2
                        eng.wait_ge(exp_ok, it * 2 * QB + 2 * a + 2 + 1)
                        own(eng, eng.reciprocal(rinv[:, b, :], psum_e[:, b, :]))
                        own(eng, eng.scalar_tensor_tensor(cmix[:, :], rinv[:, b, 1:2], psum_e[:, b, 0:1], n_lam[:, :], ALU.mult, ALU.mult))
                        eng.scalar_tensor_tensor(prob[0][:, 0:nk], prob[1][:, 0:nk], cmix[:, 0:1], prob[0][:, 0:nk],
                                                 ALU.mult, ALU.add).then_inc(mix_ok, 1)
                    elif step == "turn":
                        nb = min(a + 1, 4)
                        eng.wait_ge(a_tr, it * QB + a + 2)
                        eng.tensor_copy(a_t[:, 0:nb, :], t_ps[0][:, 0:nb * P]).then_inc(a_t_ok, 1)
                    elif step == "values":
                        b = a % 2
                        eng.wait_ge(o_done, it * QB + a + 1)
                        own(eng, eng.tensor_scalar(o_n, o_ps[:, P:2 * P], rinv[:, b, 0:1], O_TOP, ALU.mult, ALU.min))
                        eng.tensor_scalar(o_n, o_n, -O_TOP, O_TOP ** -0.5, ALU.max, ALU.mult).then_inc(o_c_ok, 1)
                    elif step == "o_norm":
                        n = it * QB + a
                        eng.wait_ge(o_sq, n + 2)
                        own(eng, eng.tensor_scalar(o_fit[:, :], o_ss[:, :], O_TOP, None, ALU.is_lt))
                        eng.tensor_scalar(o_ms[:, :], o_ss[:, :], 1.0 / P, EPS / O_TOP, ALU.mult, ALU.add).then_inc(o_ms_ok, 1)
                        eng.wait_ge(o_rs_ok, n + 1)
                        eng.tensor_scalar(o_n, o_n, o_rs[:, 0:1], o_fit[:, 0:1], ALU.mult, ALU.mult).then_inc(o_n_ok, 1)
                    elif step == "attn_out":
                        eng.wait_ge(o_tr, it * QB + a + 1)
                        ca, cb = token_cols(a + 1)
                        eng.scalar_tensor_tensor(gate[:, ca:cb], o_ps[:, 2 * P:3 * P], a_norm[:, 0:1], gate[:, ca:cb],
                                                 ALU.mult, ALU.mult).then_inc(attn_ok, 1)
                    elif step == "conv":
                        if a == 0:
                            eng.wait_ge(convg_st, it * 16 + 16)
                            own(eng, eng.tensor_scalar(conv_y[:, :], conv_u[:, META:META + T], par_sw[:, 0:1], None, ALU.mult))
                        elif a < 3:
                            own(eng, eng.scalar_tensor_tensor(conv_y[:, :], conv_u[:, META + a:META + a + T], par_sw[:, a:a + 1],
                                                              conv_y[:, :], ALU.mult, ALU.add))
                        elif a == 3:
                            own(eng, eng.tensor_tensor(conv_y[:, :], conv_y[:, :], conv_b_s[:, META:L], ALU.mult))
                        else:
                            eng.scalar_tensor_tensor(conv_y[:, :], conv_y[:, :], 0.5, conv_g[:, META:L], ALU.mult, ALU.mult).then_inc(convg_ok, 1)
                    elif step == "decay":
                        eng.wait_ge(acum_in[a % 2], it * 64 + 16 * ((a + 1) // 2))
                        eng.wait_ge(scan_done, it * CH + max(a - 1, 0) + 1)
                        for r in range(R):
                            ins = eng.tensor_scalar(lmat[:, a % 2, r, :], acum_b[:, a % 2, r, :], sg[:, 1, a, r:r + 1], 0.0,
                                                    ALU.subtract, ALU.min)
                        ins.then_inc(seg_ok, 1)
                    elif step == "chunk":
                        n = META if a == 0 else P
                        b = a % 2
                        eng.wait_ge(x_done, it * CH + a + 1)
                        eng.wait_ge(scan_done, it * CH + max(a - 1, 0) + 1)
                        eng.wait_ge(xdd_ok, it * (CH - 1) + max(a - 1, 0) + 1)
                        x3 = x_ps[b][0:n, 0:GW].rearrange("p (r d) -> p r d", r=R)
                        eng.tensor_tensor(xdt[0:n, b, :].rearrange("p (r d) -> p r d", r=R), x3,
                                          sg[0:n, 0, a, :].unsqueeze(2).to_broadcast([n, R, HD]), ALU.mult).then_inc(xdt_ok, 1)
                        if a > 0:
                            eng.tensor_tensor(xd[:, b, :].rearrange("p (r d) -> p r d", r=R), x3,
                                              dg[:, :].unsqueeze(2).to_broadcast([P, R, HD]), ALU.mult)
                            own(eng, eng.scalar_tensor_tensor(cbm[:, b, :], x_ps[b][:, 3 * P:4 * P], 0.25, tri[:, :], ALU.mult, ALU.mult))
                        eng.tensor_copy(b_n[0:n, b, :], x_ps[b][0:n, 2 * P:3 * P]).then_inc(x_free, 1)
                        if a > 0:
                            eng.wait_ge(l_ok, it * QB + a)
                            eng.wait_ge(scan_done, it * CH + a + 1)
                            eng.tensor_tensor(lmat[:, b, :, :], lmat[:, b, :, :],
                                              cbm[:, b, :].unsqueeze(1).to_broadcast([P, R, P]), ALU.mult).then_inc(g_ok, 1)
                    elif step == "z":
                        p = PZ + a - 1
                        eng.wait_ge(zth_ok, it * QB + a)
                        eng.wait_ge(a_tr, it * QB + QB + 1)
                        eng.wait_ge(mix_ok, it * QB + QB + 1)
                        eng.scalar_tensor_tensor(z_n[:, a - 1, :], th_piece[:, p % 2, 0:GW], 1.0, pb[p % 2][:, 0:GW],
                                                 ALU.add, ALU.mult).then_inc(bank_free[p % 2], 1)
                    elif step == "scan":
                        b = a % 2
                        eng.wait_ge(scan_done, it * CH + a + 2)
                        if a == 0:
                            eng.tensor_copy(state[:, :], st_ps[:, 0:GW]).then_inc(state_ok, 1)
                        elif a < CH - 1:
                            eng.wait_ge(sd_ok, it * (CH - 2) + a)
                            eng.tensor_tensor(state[:, :], state_d[:, :], st_ps[:, 0:GW], ALU.add).then_inc(state_ok, 1)
                        if a > 0:
                            own(eng, eng.tensor_tensor(y_a[:, :].rearrange("p (r d) -> p r d", r=R),
                                                       y_ps[b][:, GW:2 * GW].rearrange("p (r d) -> p r d", r=R),
                                                       sg[:, 3, a, :].unsqueeze(2).to_broadcast([P, R, HD]), ALU.mult))
                            own(eng, eng.tensor_tensor(y_a[:, :], y_ps[b][:, 0:GW], y_a[:, :], ALU.add))
                            own(eng, eng.tensor_tensor(y_a[:, :], y_a[:, :], xd[:, b, :], ALU.add))
                            eng.wait_ge(y_tr, it * QB + max(a - 2, 0) + 1)
                            p = PZ + a - 1
                            eng.wait_ge(bank_free[p % 2], it * (PPI // 2) + p // 2 + 2)
                            eng.tensor_tensor(y_n[:, b, :], y_a[:, :], z_n[:, a - 1, :], ALU.mult).then_inc(y_gated, 1)
                    elif step == "out_split":
                        low_y(a, a)
                    elif step == "norm":
                        eng.wait_ge(z_sq, it * QB + a)
                        eng.tensor_scalar(z_ms[:, a % 2:a % 2 + 1], z_ss[:, a % 2:a % 2 + 1], 0.25 / GW, EPS, ALU.mult, ALU.add).then_inc(z_ms_ok, 1)

            iteration(-1, AHEAD)
            with eng.Fori(0, HEADS - 1) as i:
                own.begin(i)
                iteration(i, BODY)
                own.end()
            own.begin(HEADS - 1)
            iteration(HEADS - 1, LAST)
            own.end()

            def add_bank(half, t):
                eng.wait_ge(out_bank, half * QB + t + 1)
                h = h_res[:, t, half * HALF:(half + 1) * HALF]
                eng.tensor_tensor(h, ps[:, t, :], h, ALU.add).then_inc(h_ok, 1)

            with eng.Fori(1, KO // OB) as g:
                for b in range(OB):
                    low_y(OB * g + b, b)
            eng.wait_ge(x_res, 16 * (QB // 2 + 1))
            for t in range(QB):
                if t >= QB - 2:
                    low_y(KO + t - (QB - 2), t - (QB - 2))
                add_bank(0, t)
            for b in range(2, OB):
                low_y(KO + b, b)
            for t in range(QB):
                eng.wait_ge(f_sq, t + 1)
                eng.tensor_scalar(f_m0[:, t:t + 1], f_ss[:, t:t + 1], 1.0 / D, EPS, ALU.mult, ALU.add).then_inc(f_m0_ok, 1)
                eng.tensor_tensor(h_res[:, t, 0:HALF], h_res[:, t, 0:HALF], w_fin[:, 0:HALF], ALU.mult).then_inc(hw_ok, 1)
            with eng.Fori(KO // OB + 1, 2 * KO // OB) as g:
                for b in range(OB):
                    low_y(OB * g + b, b)

            def finish(t):
                eng.wait_ge(f_rs_ok, t + 1)
                eng.scalar_tensor_tensor(h_res[:, t, HALF:D], h_res[:, t, HALF:D], f_rs[:, t:t + 1], w_fin[:, HALF:D], ALU.mult, ALU.mult).then_inc(f_ok, 1)

            for t in range(QB):
                add_bank(1, t)
                eng.wait_ge(f_sq, QB + t + 1)
                eng.wait_ge(f_m0_ok, t + 1)
                eng.scalar_tensor_tensor(f_ms[:, t:t + 1], f_ss[:, QB + t:QB + t + 1], 1.0 / D, f_m0[:, t:t + 1], ALU.mult, ALU.add).then_inc(f_ms_ok, 1)
                finish(t)

        @block.tensor
        def _(eng):
            def turn(dst, src, n=P):
                return eng.transpose(dst, src, ident[0:n, 0:n])

            eng.wait_ge(consts, 8)
            eng.wait_ge(params_in, 160)
            turn(o_ps[:, 0:R_END], rows[0:R_END, :], R_END).then_inc(par_tr, 1)
            for r in range(CH):
                n = META if r == 0 else P
                eng.wait_ge(x_n, r + 1)
                eng.wait_ge(u_prod, max(r - 1, 0))
                for k in range(KD):
                    ins = turn(u_ps[r % 2][:, k * P:k * P + n], prob[r % 2][0:n, k * P:(k + 1) * P], n)
                ins.then_inc(x_tr, 1)
            eng.wait_ge(par_tr, 1)
            eng.wait_ge(lam_row, 1)
            eng.matmul(o_ps[:, 0:1], ones[0:1, :], lam_s[0:1, 5:6], start=True, stop=True).then_inc(lam_pe, 1)

            def project(dst, m, cols, wh, wl, ks=range(KD)):
                terms = [(wh, u_hi), (wh, u_lo), (wl, u_hi)]
                for k in ks:
                    for n, (w, u) in enumerate(terms):
                        ins = eng.matmul(dst, w[:, k, 0:m], u[:, k, cols], start=(k == 0 and n == 0), stop=(k == KD - 1 and n == 2))
                return ins

            eng.wait_ge(u_lo_ok, CH)
            eng.wait_ge(w_lo_ok, 1 + 1)
            for tc in range(PIECES):
                if tc == 2:
                    eng.wait_ge(lam_ok, 1)
                project(ps[0:SH, 5 + tc, 0:PW], SH, slice(tc * PW, (tc + 1) * PW), wd_hi, wd_lo).then_inc(dt_pe, 1)
            eng.wait_ge(dt_row_ok, 1)
            for c in range(CH):
                ins = turn(ps[:, 5, c * SH:(c + 1) * SH], dt_row[:, c * P:(c + 1) * P], SH)
            ins.then_inc(dt_tr, 1)
            eng.wait_ge(adt_ok, 1)
            eng.matmul(o_ps[:, 0:CH * SH], tri[:, :], sp[:, 4, :], start=True, stop=True)
            eng.matmul(o_ps[:, CH * SH:2 * CH * SH], ones[:, :], sp[:, 4, :], start=True, stop=True).then_inc(cum_pe, 1)
            eng.wait_ge(acum_ok, 1)
            eng.wait_ge(stat_x, 1)
            for c in range(CH):
                ins = turn(ps[0:SH, 5 + c // 4, (c % 4) * P:(c % 4 + 1) * P], stat[:, 1, c, :])
            ins.then_inc(acum_tr, 1)
            eng.wait_ge(acum_row, 1)

            def multiply(n, b, t, first, last):
                terms = [(y_hi, wo_hi), (y_hi, wo_lo), (y_lo, wo_hi)]
                for m, (y, w) in enumerate(terms):
                    ins = eng.matmul(ps[:, t, :], y[:, b, t * P:(t + 1) * P], w[:, b, :], start=(first and m == 0),
                                     stop=(last and m == 2), skip_group_check=True)
                return ins

            def out_tile(n, b, half, first, banks=range(QB)):
                eng.wait_ge(y_lo_ok, n + 2)
                eng.wait_ge(wo_lo_ok, n + 2)
                for t in banks:
                    if first and half == 1:
                        eng.wait_ge(h_ok, t + 1)
                    ins = multiply(n, b, t, first, False)
                if banks[-1] == QB - 1:
                    ins.then_inc(out_k, 1)

            def iteration(i, steps):
                for step, a, d in steps:
                    it = i + d
                    if step == "project":
                        p, h = a
                        t, tc = tile_of(p)
                        if (tc, h) == (0, 0):
                            eng.wait_ge(w_lo_ok, it * NT + t + 3)
                        if h == 0:
                            eng.wait_ge(bank_free[p % 2], it * (PPI // 2) + p // 2 + 1)
                        ins = project(pb[p % 2][:, 0:PW], P, slice(tc * PW, (tc + 1) * PW), w_hi[:, t % 2], w_lo[:, t % 2],
                                      range(h * KD // 2, (h + 1) * KD // 2))
                        if h == 1:
                            ins.then_inc(piece_done, 1)
                    elif step == "turn_v":
                        for b in range(2):
                            eng.wait_ge(bank_free[b], it * (PPI // 2) + (PIECES * (TV + 1) + 1 - b) // 2 + 1)
                        eng.wait_ge(ys_ok, it * QB + 1)
                        eng.wait_ge(state_ok, it * (CH - 1) + 1)
                        eng.wait_ge(y_gated, it * QB + 1)
                        for n in range(QB):
                            turn(t_ps[n // 4][:, (n % 4) * P:(n % 4 + 1) * P], v_t[:, META + n * P:META + (n + 1) * P])
                        turn(o_ps[0:META, 0:P], v_t[:, 0:META]).then_inc(v_tr, 1)
                    elif step == "scores":
                        s, m = a
                        n = it * 2 * QB + 2 * s + m
                        if (s, m) == (0, 0):
                            for b in range(2):
                                eng.wait_ge(bank_free[b], it * (PPI // 2) + PIECES * (TK + 1) // 2 + 1)
                            eng.wait_ge(x_free, it * CH + 1)
                            eng.wait_ge(y_gated, it * QB + 1)
                        eng.wait_ge(exp_ok, n + 1)
                        qa, qb = token_cols(s + 1)
                        q = q_map[m][:, qa:qb]
                        for at in range(0, (s + 1) * P, 512):
                            w = min(512, (s + 1) * P - at)
                            last = at + w == (s + 1) * P
                            eng.matmul(s_ps[:, at:at + w], q, k_t[:, META + at:META + at + w], start=True, stop=not last)
                            if last:
                                eng.matmul(s_ps[:, s * P:(s + 1) * P], ident_b[:, :], mask_b[:, :], start=False, stop=True)
                        eng.matmul(s_ps[:, (s + 1) * P:(s + 1) * P + META], q, k_t[:, 0:META], start=True, stop=True).then_inc(s_done, 1)
                    elif step == "turn":
                        eng.wait_ge(mix_ok, it * QB + a + 2)
                        if a == 0:
                            eng.wait_ge(v_meta_ok, it + 1)
                            eng.wait_ge(v_blk_ok, it + 1)
                        eng.wait_ge(a_t_ok, it * QB + a + 1)
                        eng.wait_ge(a_m_ok, it * QB + a + 1)
                        eng.wait_ge(attn_ok, it * QB + a + 1)
                        for n in range(a + 1):
                            turn(t_ps[n // 4][:, (n % 4) * P:(n % 4 + 1) * P], prob[0][:, n * P:(n + 1) * P])
                        turn(o_ps[0:META, 0:P], prob[0][:, (a + 1) * P:(a + 1) * P + META]).then_inc(a_tr, 1)
                    elif step == "values":
                        eng.wait_ge(a_t_ok, it * QB + a + 2)
                        eng.wait_ge(a_m_ok, it * QB + a + 2)
                        for n in range(a + 1):
                            eng.matmul(o_ps[:, P:2 * P], a_t[:, n, :], v_blk[:, n, :], start=(n == 0), stop=False)
                        eng.matmul(o_ps[:, P:2 * P], a_meta[:, :], v_meta, start=False, stop=True).then_inc(o_done, 1)
                    elif step == "attn_out":
                        eng.wait_ge(o_n_ok, it * QB + a + 1)
                        turn(o_ps[:, 2 * P:3 * P], o_n).then_inc(o_tr, 1)
                    elif step == "chunk":
                        n = META if a == 0 else P
                        ca, cb = token_cols(a)
                        b = a % 2
                        if a == 0:
                            eng.wait_ge(conv_ok, it * 4 + 4 + 1)
                            eng.wait_ge(exp_ok, it * 2 * QB + 2 * QB + 1)
                        if a >= 2:
                            eng.wait_ge(x_free, it * CH + a - 1 + 1)
                        for t in range(2):
                            turn(x_ps[b][0:n, t * P:(t + 1) * P], xs[:, t, ca:cb])
                        ins = turn(x_ps[b][0:n, 2 * P:3 * P], b_t[:, ca:cb])
                        if a > 0:
                            ins = eng.matmul(x_ps[b][:, 3 * P:4 * P], b_t[:, ca:cb], c_t[:, ca:cb], start=True, stop=True)
                        ins.then_inc(x_done, 1)
                    elif step == "z":
                        p = PZ + a - 1
                        ca, cb = token_cols(a)
                        if a == 1:
                            eng.wait_ge(w_lo_ok, it * NT + TZ1 + 2 + 1)
                        eng.wait_ge(bank_free[p % 2], it * (PPI // 2) + p // 2 + 1)
                        terms = [(u_hi, w_hi), (u_hi, w_lo), (u_lo, w_hi)]
                        for k in range(KD):
                            for n, (u, w) in enumerate(terms):
                                ins = eng.matmul(pb[p % 2][:, 0:GW], u[:, k, ca:cb], w[:, :, k, :], start=(k == 0 and n == 0), stop=(k == KD - 1 and n == 2))
                        ins.then_inc(piece_done, 1)
                    elif step == "scan":
                        n = META if a == 0 else P
                        ca, cb = token_cols(a)
                        b = a % 2
                        if a == 0:
                            eng.wait_ge(attn_ok, it * QB + QB + 1)
                        if a > 0:
                            eng.wait_ge(y_gated, it * QB + max(a - 2, 0) + 1)
                            eng.wait_ge(g_ok, it * QB + a + 1)
                            for r in range(R):
                                eng.matmul(y_ps[b][:, r * HD:(r + 1) * HD], lmat[:, b, r, :], xdt[:, b, r * HD:(r + 1) * HD], start=True, stop=True)
                            eng.wait_ge(state_ok, it * (CH - 1) + a + 1)
                            ins = eng.matmul(y_ps[b][:, GW:2 * GW], c_t[:, ca:cb], state[:, :], start=True, stop=True)
                        if a < CH - 1:
                            eng.wait_ge(xdd_ok, it * (CH - 1) + a + 2)
                            eng.wait_ge(x_free, it * CH + a + 2)
                            ins = eng.matmul(st_ps[:, 0:GW], b_n[0:n, b, :], xdd[0:n, b, :], start=True, stop=True)
                        ins.then_inc(scan_done, 1)
                    elif step == "out_begin":
                        for b in range(2):
                            eng.wait_ge(bank_free[b], HEADS * PPI // 2 + 1)
                        eng.wait_ge(x_free, HEADS * CH + 1)
                        for b in range(2):
                            out_tile(b, b, 0, b == 0, range(QB // 2))
                    elif step == "ssm_out":
                        eng.wait_ge(y_n_ok, it * QB + a)
                        eng.wait_ge(ys_ok, it * QB + a - 1 + 1)
                        turn(yt_ps[:, 0:P], y_n[:, a % 2, 0:P])
                        turn(yt_ps[:, P:2 * P], y_n[:, a % 2, P:2 * P]).then_inc(y_tr, 1)

            iteration(-1, AHEAD)
            with eng.Fori(0, HEADS - 1) as i:
                iteration(i, BODY)
            iteration(HEADS - 1, LAST)

            eng.wait_ge(y_gated, HEADS * QB + 1)
            eng.wait_ge(ys_ok, HEADS * QB + 1)
            for half in range(2):
                for b in range(OB):
                    out_tile(half * KO + b, b, half, b == 0, range(QB // 2 if half == 0 and b < 2 else 0, QB))
                with eng.Fori(1, KO // OB - 1) as g:
                    for b in range(OB):
                        out_tile(half * KO + OB * g + b, b, half, False)
                at = (half + 1) * KO - OB
                for b in range(OB - 2):
                    out_tile(at + b, b, half, False)
                eng.wait_ge(y_lo_ok, at + OB + 1)
                eng.wait_ge(wo_lo_ok, at + OB + 1)
                for t in range(QB):
                    for b in range(OB - 2, OB):
                        ins = multiply(at + b, b, t, False, b == OB - 1)
                    ins.then_inc(out_bank, 1)


_INS = ["x", "meta_tokens", "norm_w", "w_in", "w_out", "attn_lambda", "attn_norm_w", "sconv_w", "ssm_conv_w",
        "ssm_conv_b", "ssm_a_log", "ssm_dt_bias", "ssm_d", "ssm_norm_w", "final_norm_w"]


def kernel(**inputs):
    import concourse.bacc as bacc
    from concourse.bass_utils import run_bass_kernel_spmd

    nc = bacc.Bacc("TRN2", target_bir_lowering=False, num_devices=1)
    arrays, args = {}, []
    for name in _INS:
        a = np.ascontiguousarray(inputs[name])
        arrays[f"in_{name}"] = a
        args.append(nc.dram_tensor(f"in_{name}", a.shape, mybir.dt.from_np(a.dtype), kind="ExternalInput").ap())
    args.append(nc.dram_tensor("out_0", (1, T, D), F32, kind="ExternalOutput").ap())
    args.append(nc.dram_tensor("y_scratch", (2 * D, T), F32, kind="Internal").ap())
    args.append(nc.dram_tensor("acum_scratch", (SH, CH * P), F32, kind="Internal").ap())
    build(nc, *args)
    r = run_bass_kernel_spmd(nc, [arrays], core_ids=[0])
    return r.results[0]["out_0"]
```

```python
import math
from contextlib import ExitStack

import numpy as np

import concourse.bass as bass
from concourse import mybir

F32 = mybir.dt.float32
F32R = mybir.dt.float32r
BF16 = mybir.dt.bfloat16
ALU = mybir.AluOpType
ACT = mybir.ActivationFunctionType
AX = mybir.AxisListType

P = 128
D = 1024
T = 1024
META = 16
L = META + T
PIECES = 3
PW = 348
LP = PIECES * PW
KD = D // P
HEADS = 4
QK = 64
QB = T // P
CH = QB + 1
SH = 16
R = SH // HEADS
HD = 64
GW = R * HD
XB = 4
OB = 4
XT = D // P
WORK = -(-(10 * LP + 2 * L + 3) // 16) * 16
KO = 2 * D // P
HALF = D // 2
EPS = 1e-5
LAM_INIT = 0.8 - 0.6 * math.exp(-0.3 * 0)
MASK = -1e30
O_TOP = 2.0 ** 64

C_Q, C_K, C_V, C_G, C_CB, C_CC, C_CH, C_GC = (512 * n for n in range(8))
C_Z, C_XS, C_B, C_C, C_DT = 4096, 5120, 6144, 6656, 7168

TILES = [(C_Q, P), (C_K, P), (C_V, P), (C_G, P), (C_XS, GW), (C_XS + P, GW), (C_B, P), (C_C, P),
         (C_Z, GW), (C_Z + P, GW), (C_CB, P), (C_CC, P), (C_CH, P), (C_GC, P)]
NT = len(TILES)
(TQ, TK, TV, TG, TXS0, TXS1, TB, TC, TZ0, TZ1, TCB, TCC, TCH, TGC) = range(NT)
SHARED = (TZ1, TCB)
PZ = TZ0 * PIECES
PPI = (NT - 2) * PIECES + QB


def first_piece(t):
    return min(t, TZ0) * PIECES if t <= TZ1 else PZ + QB + (t - TCB) * PIECES


def tile_of(p):
    return divmod(p, PIECES) if p < PZ else (TCB + (p - PZ - QB) // PIECES, (p - PZ - QB) % PIECES)


R_CW, R_CB, R_SW, R_SN, R_NW, R_AN, R_END = 0, 64, 80, 92, 100, 108, 109




def half_pieces(tiles, d):
    units = [[] for _ in range(len(tiles) * PIECES * 2)]
    tail = [[] for _ in range(6)]
    places = units + tail
    n = 0
    for t in tiles:
        units[n] += [("load", t + 2, d), ("split", t + 1, d)]
        if t == TXS0:
            units[n].append(("params", 0, d))
        for tc in range(PIECES):
            p = first_piece(t) + tc
            units[n].append(("project", (p, 0), d))
            units[n + 1] += [("project", (p, 1), d), ("piece", p, d)]
            n += 2
        if TXS0 <= t <= TC:
            for tap in range(4):
                places[n - 1 + tap].append(("taps", (t, tap), d))
            places[n + 3].append(("gate_taps", t, d))
        if t == TGC:
            for part in range(5):
                places[n - 1 + part].append(("conv", part, d))
    return units, tail


def ahead():
    out = [("load", 0, 1)]
    units = half_pieces([TQ, TK, TV], 1)[0]
    beside = {5: "dt", 9: "dt_cum", 11: "dt_stat", 13: "dt_row"}

    def pieces(n):
        for _ in range(n):
            at = len(done)
            if at in beside:
                out.append((beside[at], 0, 1))
            out.extend(units[at])
            done.append(at)

    done = []
    for r in range(-3, CH + 2):
        if r == 0:
            out.append(("parameters", 0, 1))
        for name, lead in (("x_square", 3), ("x_mean", 2), ("x_power", 2), ("x_scale", 1), ("x_turn", 1), ("x_load", 1 + XB),
                           ("x_low", -1), ("x_low2", -2), ("x_prod", 0), ("x_high", 0)):
            if 0 <= r + lead < CH and not (name == "x_load" and r + lead < XB):
                out.append((name, r + lead, 1))
        if r == -1:
            out.append(("w_dt", 0, 1))
        if r == 1:
            out.append(("load", 1, 1))
            out.append(("lambda", 0, 1))
        if r == 2:
            out.append(("lambda_out", 0, 1))
        if r == CH - 3:
            out.append(("split", 0, 1))
        if r == CH - 2:
            out.append(("dt_piece", 0, 1))
            pieces(2)
    out.append(("dt_piece", 1, 1))
    pieces(2)
    out.append(("dt_piece", 2, 1))
    pieces(len(units) - len(done))
    return out


def schedule(last):
    out = []

    def add(name, arg=0, d=0):
        if not (last and d):
            out.append((name, arg, d))

    def add_tile(name, t, d):
        add(name, t % NT, d + t // NT)

    def filler(units, slots):
        state = [0, 0.0]

        def fill(weight=1.0):
            state[1] += weight
            while state[0] < len(units) and state[0] < len(units) * state[1] / slots - 1e-9:
                emit(units[state[0]])
                state[0] += 1
        return fill

    def emit(unit):
        for name, arg, d in unit:
            if name in ("load", "split"):
                add_tile(name, arg, d)
            else:
                add(name, arg, d)

    units, tail = half_pieces([TG, TXS0, TXS1, TB, TC], 0)
    units[-1] += [("split", TZ1, 0), ("load", TCB, 0), ("load", TCC, 0)]
    fill = filler(units, sum(ATT_FILL))
    for s in range(QB + 1):
        f = [ATT_FILL[s] * w for w in ATT_SPLIT]
        if s < QB:
            add("scores", (s, 0))
        if s >= 2:
            add("attn_out", s - 2)
        fill(f[0])
        if s == 0:
            add("turn_v")
        if s >= 1:
            add("turn", s - 1)
        if s < QB:
            add("exp", (s, 0))
        fill(f[1])
        if s < QB:
            add("scores", (s, 1))
            add("exp", (s, 1))
        if s >= 1:
            add("values", s - 1)
        if s < QB:
            add("mix", s)
        if s >= 1:
            add("o_norm", s - 1)
        fill(f[2])
    emit(tail[0])
    add("z", 1)
    emit(tail[1])
    add("z", 2)
    emit(tail[2])
    emit(tail[3])
    add("z", 3)
    add("attn_out", QB - 1)
    add("store_attn")
    add("z", 4)
    add("chunk", 0)
    add("decay", 1)
    units = [[("z", a, 0)] for a in range(5, QB + 1)]
    units[-1].append(("split", TCB, 0))
    units += [[]] * PAUSE
    conv, tail = half_pieces([TCB, TCC, TCH, TGC], 0)
    if last:
        for n in range(len(conv)):
            if ("split", TGC, 0) in conv[n]:
                for b in range(OB):
                    conv[n + 2 * b].append(("out_load", b, 0))
                conv[-4].append(("out_w", 0, 0))
                conv[-2].append(("out_w", 1, 0))
                break
        units += conv
    else:
        more = half_pieces([TQ, TK, TV], 1)[0]
        for n, unit in enumerate(tail):
            more[n] += unit
        tail = []
        units += conv + more
    slots = LAST_FILL if last else SCAN_FILL
    fill = filler(units, sum(slots))
    for c in range(1, CH + 3):
        f = [slots[c - 1] * w for w in SCAN_SPLIT]
        if c < CH:
            add("chunk", c)
        if 1 <= c - 2 < CH:
            add("norm", c - 2)
        fill(f[0])
        if c - 1 < CH:
            add("scan", c - 1)
            if 0 < c < CH - 1:
                add("carry", c)
        if c + 1 < CH:
            add("decay", c + 1)
        fill(f[1])
        if 1 <= c - 2 < CH:
            add("ssm_out", c - 2)
        fill(f[2])
        if c == CH and last:
            add("out_y", 0)
            add("out_y", 1)
            add("out_begin")
    add("store_ssm")
    if last:
        for unit in tail:
            emit(unit)
        add("out_y", 2)
        add("out_w", 2)
        add("out_y", 3)
        add("out_w", 3)
    return out


PAUSE = 4
ATT_SPLIT = (.3, .3, .4)
SCAN_SPLIT = (.2, .6, .2)
ATT_FILL = (1.5, 1.5, 2, 2, 2, 2, 2.5, 2.5, 1)
SCAN_FILL = (1,) * 8 + (1.5, 1.5, 0)
LAST_FILL = (1,) * 9 + (0, 0)
BODY = schedule(False)
LAST = schedule(True)
AHEAD = ahead()
DVE_OWN = 82


class Chain:

    def __init__(self, sem, per):
        self.sem, self.per, self.base, self.n, self.before = sem, per, 0, 0, None

    def begin(self, i):
        if self.before is None:
            self.before = self.n
        self.base, self.n = self.before + i * self.per, 0

    def end(self):
        assert self.n == self.per, self.n

    def __call__(self, eng, ins):
        self.n += 1
        ins.then_inc(self.sem, 1)
        eng.wait_ge(self.sem, self.base + self.n)


def tiles_of(tc):
    return -(-(min((tc + 1) * PW, L) - META) // P) + 1


def token_cols(c):
    return (0, META) if c == 0 else (META + P * (c - 1), META + P * c)


def build(nc, x, meta_tokens, norm_w, w_in, w_out, attn_lambda, attn_norm_w, sconv_w, ssm_conv_w,
          ssm_conv_b, ssm_a_log, ssm_dt_bias, ssm_d, ssm_norm_w, final_norm_w, out, y_dram, acum_dram):
    x_rows = x.rearrange("b t d -> (b t) d")
    out_rows = out.rearrange("b t d -> (b t) d")
    w_in_t = w_in.rearrange("a (k p) n -> p (a k) n", p=P)
    w_out_rows = w_out.rearrange("a k n -> (a k) n")

    with ExitStack() as ctx:
        def sb(name, shape, dt=F32):
            return ctx.enter_context(nc.sbuf_tensor(name, shape, dt))

        def sem(name):
            return ctx.enter_context(nc.semaphore(name))

        u_hi = sb("u_hi", [P, KD, LP], F32R)
        u_lo = sb("u_lo", [P, KD, LP], F32R)
        w_raw = sb("w_raw", [P, 2, KD, P])
        w_hi = sb("w_hi", [P, 2, KD, P], F32R)
        w_lo = sb("w_lo", [P, 2, KD, P], F32R)

        work = sb("work", [P, WORK])
        taken = [0]

        def part(n):
            taken[0] += n
            return work[:, taken[0] - n:taken[0]]

        q_map = [part(LP), part(LP)]
        k_t = part(LP)
        v_t = part(LP)
        gate = part(LP)
        prob_flat = part(2 * L)
        prob = [prob_flat[:, 0:L], prob_flat[:, L:2 * L]]
        z_n = prob_flat[:, 0:QB * GW].rearrange("p (c n) -> p c n", c=QB)
        xs_flat = part(2 * LP)
        xs = xs_flat.rearrange("p (t n) -> p t n", t=2)
        x_buf = [prob[0], prob[1], xs_flat[:, 0:LP], xs_flat[:, LP:2 * LP]]
        bc_flat = part(2 * LP)
        b_t, c_t = bc_flat[:, 0:LP], bc_flat[:, LP:2 * LP]
        dt_rows = bc_flat[0:SH, 0:CH * P]
        raw = part(3 + LP)
        y_raw = work[:, 0:OB * T].rearrange("p (b n) -> p b n", b=OB)
        h_res = work[:, OB * T:OB * T + QB * D].rearrange("p (t d) -> p t d", t=QB)
        assert OB * T <= 4 * LP and OB * T + QB * D <= taken[0] <= WORK
        y_hi = u_hi[:, :, :].rearrange("p k n -> p (k n)")[:, 0:OB * T].rearrange("p (b n) -> p b n", b=OB)
        y_lo = u_lo[:, :, :].rearrange("p k n -> p (k n)")[:, 0:OB * T].rearrange("p (b n) -> p b n", b=OB)
        wo_raw = w_raw[:, :, :, :].rearrange("p b k n -> p (b k n)").rearrange("p (b n) -> p b n", b=OB)
        wo_hi = w_hi[:, :, :, :].rearrange("p b k n -> p (b k n)").rearrange("p (b n) -> p b n", b=OB)
        wo_lo = w_lo[:, :, :, :].rearrange("p b k n -> p (b k n)").rearrange("p (b n) -> p b n", b=OB)

        th_tile = sb("th_tile", [P, LP])
        th_piece = sb("th_piece", [P, 2, PW])
        v_blk = sb("v_blk", [P, QB, P])
        a_t = sb("a_t", [P, QB, P])
        conv_b_s = sb("conv_b_s", [P, LP])
        conv_u = sb("conv_u", [P, 2 + LP])
        conv_g = sb("conv_g", [P, LP])
        conv_y = sb("conv_y", [P, T])
        w_fin = conv_y[:, :]
        acum_b = sb("acum_b", [P, 2, R, P])
        lm_buf = sb("lm_buf", [P, 3 + LP])
        lmat = lm_buf[:, 0:2 * R * P].rearrange("p (b r n) -> p b r n", b=2, r=R)
        raws = [raw, lm_buf[:, :]]
        xdt = sb("xdt", [P, 2, GW])
        xdd = sb("xdd", [P, 2, GW])
        xd = sb("xd", [P, 2, GW])
        b_n = sb("b_n", [P, 2, P])
        cbm = sb("cbm", [P, 2, P])
        state = sb("state", [P, GW])
        state_d = sb("state_d", [P, GW])
        y_a = sb("y_a", [P, GW])
        v_meta = y_a[0:META, 0:P]
        o_n = y_a[:, P:2 * P]
        y_n = sb("y_n", [P, 2, GW])
        a_meta = sb("a_meta", [META, P])
        o_squares = sb("o_squares", [P, P])
        ys = sb("ys", [P, 2, T])

        ident = sb("ident", [P, P])
        ident_b = sb("ident_b", [P, P], BF16)
        mask_b = sb("mask_b", [P, P], BF16)
        tri = sb("tri", [P, P])
        ones = sb("ones", [P, P])
        valid = sb("valid", [P, 1])
        m_half = sb("m_half", [P, 1])
        rows = conv_g[:, 0:P]
        w_dt = conv_g[:, P:P + KD * SH].rearrange("p (k n) -> p k n", k=KD)
        par = sb("par", [P, R_END])
        par_cw = sb("par_cw", [P, 4, 4])
        par_cb = sb("par_cb", [P, 4])
        par_sw = sb("par_sw", [P, 3])
        par_sn = sb("par_sn", [P, 2])
        a_norm = sb("a_norm", [P, 1])
        lam_in = conv_b_s[0:1, 0:4 * QK].rearrange("p (r d) -> p r d", r=4)
        lam_p = conv_b_s[0:1, 4 * QK:6 * QK].rearrange("p (r d) -> p r d", r=2)
        lam_s = sb("lam_s", [1, 8])
        n_lam = sb("n_lam", [P, 1])
        wd_hi = sb("wd_hi", [P, KD, SH], F32R)
        wd_lo = sb("wd_lo", [P, KD, SH], F32R)
        dt_bias = conv_g[0:SH, 3 * P:3 * P + 1]
        a_bc = sb("a_bc", [P, SH])
        d_bc = sb("d_bc", [P, SH])
        sp = conv_y[:, 0:6 * CH * SH].rearrange("p (s n) -> p s n", s=6)
        stat = sb("stat", [P, 5, CH, SH])
        sg = sb("sg", [P, 5, CH, R])
        small = sb("small", [P, 128])
        used = [0]

        def few(n):
            used[0] += n
            assert used[0] <= 128
            return small[:, used[0] - n:used[0]]

        dg = few(R)
        ss = few(XB)
        ms = few(XB)
        rs = few(XB)
        mx = few(2)
        psum_e = few(4).rearrange("p (b m) -> p b m", b=2)
        rinv = few(4).rearrange("p (b m) -> p b m", b=2)
        cmix = few(1)
        o_ss = few(1)
        o_ms = few(1)
        o_fit = few(1)
        o_rs = few(1)
        z_ss = few(2)
        z_ms = few(2)
        z_rs = few(2)
        f_ss = few(2 * QB)
        f_m0 = few(QB)
        f_ms = few(QB)
        f_rs = few(QB)

        ps = ctx.enter_context(nc.psum_tensor("ps", [P, 8, 512], F32))
        pb = [ps[:, 0, :], ps[:, 1, :]]
        s_ps = ps[:, 2:5, :].rearrange("p b n -> p (b n)")
        t_ps = [ps[:, 5, :], ps[:, 6, :]]
        o_ps = ps[:, 7, :]
        x_ps = [ps[:, 2, :], ps[:, 3, :]]
        y_ps = [ps[:, 4, :], ps[:, 5, :]]
        st_ps = ps[:, 6, :]
        yt_ps = ps[:, 7, :]
        dt_ps = [ps[:, 4, :], ps[:, 7, :], ps[:, 4, :]]
        u_ps = [ps[:, 2:4, :].rearrange("p b n -> p (b n)"), ps[:, 5:7, :].rearrange("p b n -> p (b n)")]

        params_in = sem("params_in")
        x_in = [sem(f"x_in{b}") for b in range(XB)]
        consts = sem("consts")
        x_sq = sem("x_sq")
        x_ms = sem("x_ms")
        x_rs = sem("x_rs")
        x_n = sem("x_n")
        x_tr = sem("x_tr")
        u_prod = sem("u_prod")
        u_hi_ok = sem("u_hi_ok")
        u_lo_ok = sem("u_lo_ok")
        u_lo2_ok = sem("u_lo2_ok")
        par_tr = sem("par_tr")
        lam_sum = sem("lam_sum")
        lam_exp = sem("lam_exp")
        lam_row = sem("lam_row")
        lam_pe = sem("lam_pe")
        lam_ok = sem("lam_ok")
        dt_pe = sem("dt_pe")
        wd_hi_ok = sem("wd_hi_ok")
        wd_lo_ok = sem("wd_lo_ok")
        rows_in = sem("rows_in")
        dt_row_ok = sem("dt_row_ok")
        dt_tr = sem("dt_tr")
        dt_x = sem("dt_x")
        dt_e = sem("dt_e")
        adt_ok = sem("adt_ok")
        cum_pe = sem("cum_pe")
        acum_ok = sem("acum_ok")
        acum_tr = sem("acum_tr")
        acum_row = sem("acum_row")
        acum_st = sem("acum_st")
        stat_x = sem("stat_x")
        stat_e = sem("stat_e")
        w_in_ok = [sem("w_in_ok0"), sem("w_in_ok1")]
        w_hi_ok = sem("w_hi_ok")
        w_lo_ok = sem("w_lo_ok")
        w_lo2_ok = sem("w_lo2_ok")
        piece_done = sem("piece_done")
        bank_free = [sem("bank_free0"), sem("bank_free1")]
        th_ok = sem("th_ok")
        raw_free = sem("raw_free")
        thc_ok = sem("thc_ok")
        conv_ok = sem("conv_ok")
        v_tr = sem("v_tr")
        v_blk_ok = sem("v_blk_ok")
        v_meta_ok = sem("v_meta_ok")
        s_done = sem("s_done")
        max_ok = sem("max_ok")
        exp_ok = sem("exp_ok")
        mix_ok = sem("mix_ok")
        a_tr = sem("a_tr")
        a_t_ok = sem("a_t_ok")
        a_m_ok = sem("a_m_ok")
        o_done = sem("o_done")
        o_sq = sem("o_sq")
        o_c_ok = sem("o_c_ok")
        o_ms_ok = sem("o_ms_ok")
        o_rs_ok = sem("o_rs_ok")
        o_n_ok = sem("o_n_ok")
        o_tr = sem("o_tr")
        attn_ok = sem("attn_ok")
        attn_st = sem("attn_st")
        convg_ok = sem("convg_ok")
        convg_st = sem("convg_st")
        acum_in = [sem("acum_in0"), sem("acum_in1")]
        seg_ok = sem("seg_ok")
        l_ok = sem("l_ok")
        x_done = sem("x_done")
        xdt_ok = sem("xdt_ok")
        x_free = sem("x_free")
        xdd_ok = sem("xdd_ok")
        g_ok = sem("g_ok")
        scan_done = sem("scan_done")
        sd_ok = sem("sd_ok")
        state_ok = sem("state_ok")
        zth_ok = sem("zth_ok")
        y_gated = sem("y_gated")
        z_sq = sem("z_sq")
        z_ms_ok = sem("z_ms_ok")
        z_rs_ok = sem("z_rs_ok")
        y_n_ok = sem("y_n_ok")
        y_tr = sem("y_tr")
        ys_ok = sem("ys_ok")
        ssm_st = sem("ssm_st")
        yw_in = [sem(f"yw_in{b}") for b in range(OB)]
        y_hi_ok = sem("y_hi_ok")
        wo_hi_ok = sem("wo_hi_ok")
        y_lo_ok = sem("y_lo_ok")
        wo_lo_ok = sem("wo_lo_ok")
        out_k = sem("out_k")
        x_res = sem("x_res")
        out_bank = sem("out_bank")
        h_ok = sem("h_ok")
        f0_ok = sem("f0_ok")
        f_m0_ok = sem("f_m0_ok")
        hw_ok = sem("hw_ok")
        f_sq = sem("f_sq")
        f_ms_ok = sem("f_ms_ok")
        f_rs_ok = sem("f_rs_ok")
        f_ok = sem("f_ok")
        out_st = sem("out_st")
        dve_own = Chain(sem("dve_own"), DVE_OWN)
        pool_own = Chain(sem("pool_own"), 0)

        primed = [a_m_ok, convg_ok, a_t_ok, a_tr, attn_ok, conv_ok, exp_ok, g_ok, mix_ok, o_ms_ok,
                  o_sq, out_k, piece_done, raw_free, s_done, scan_done, seg_ok, state_ok, v_tr,
                  w_lo_ok, wo_lo_ok, x_free, xdd_ok, y_gated, y_lo_ok, y_tr, ys_ok, z_ms_ok,
                  *bank_free]
        primed_dma = [attn_st, convg_st, ssm_st]

        block = ctx.enter_context(nc.Block())

        @block.sync
        def _(eng):
            def load_x(r):
                if r >= XB:
                    eng.wait_ge(x_tr, r - XB + 1)
                n = META if r == 0 else P
                src = meta_tokens if r == 0 else x_rows[(r - 1) * P:r * P, :]
                eng.dma_start(x_buf[r % XB][0:n, 0:D], src).then_inc(x_in[r % XB], 16)

            for guard in primed:
                eng.sem_inc(guard, 1)
            eng.sem_inc(raw_free, 1)
            eng.sem_inc(w_lo_ok, 1)
            for guard in primed_dma:
                eng.sem_inc(guard, 16)
            load_x(0)
            load_x(1)
            load_x(2)
            eng.dma_start(rows[R_CW:R_CB, :], ssm_conv_w.rearrange("a j (t c) -> (a j t) c", c=P)).then_inc(rows_in, 16)
            eng.dma_start(rows[R_CB:R_SW, :], ssm_conv_b.rearrange("a (t c) -> (a t) c", c=P)).then_inc(rows_in, 16)
            eng.dma_start(rows[R_SW:R_SN, :], sconv_w.rearrange("a j (t c) -> (a j t) c", c=P)).then_inc(rows_in, 16)
            eng.dma_start(rows[R_SN:R_NW, :], ssm_norm_w.rearrange("a (t c) -> (a t) c", c=P)).then_inc(rows_in, 16)
            eng.dma_start(rows[R_NW:R_AN, :], norm_w.rearrange("a (t c) -> (a t) c", c=P)).then_inc(rows_in, 16)
            eng.dma_start(rows[R_AN:R_END, :], attn_norm_w).then_inc(rows_in, 16)
            eng.dma_start(lam_in[:, :, :], attn_lambda).then_inc(params_in, 16)
            eng.dma_start(dt_bias, ssm_dt_bias.rearrange("a h -> h a")).then_inc(params_in, 16)
            eng.dma_start(a_bc[:, :], ssm_a_log[0, :].partition_broadcast(P)).then_inc(params_in, 16)
            eng.dma_start(d_bc[:, :], ssm_d[0, :].partition_broadcast(P)).then_inc(params_in, 16)
            eng.dma_start(w_dt, w_in_t[:, :, C_DT:C_DT + SH]).then_inc(params_in, 16)
            load_x(3)
            x_tiles = x_rows.rearrange("(t p) d -> p t d", p=P)

            def load_out(half, k, b):
                eng.dma_start(y_raw[:, b, :], y_dram[bass.ds(k * P, P), :]).then_inc(yw_in[b], 16)
                eng.dma_start(wo_raw[:, b, :], w_out_rows[bass.ds(k * P, P), half * HALF:(half + 1) * HALF]).then_inc(yw_in[b], 16)

            def iteration(i, steps):
                for step, a, d in steps:
                    it = i + d
                    if step == "load":
                        at, by = TILES[a]
                        if a - 2 in SHARED:
                            eng.wait_ge(piece_done, it * PPI + first_piece(a - 2) + 2)
                        else:
                            eng.wait_ge(w_lo_ok, it * NT + a + 1)
                        eng.dma_start(w_raw[:, a % 2, :, :], w_in_t[:, :, bass.ds(it * by + at, P)]).then_inc(w_in_ok[a % 2], 16)
                    elif step == "x_load":
                        load_x(a)
                    elif step == "dt_row":
                        eng.wait_ge(acum_row, 1)
                        eng.dma_start(acum_dram, dt_rows).then_inc(acum_st, 16)
                    elif step == "store_attn":
                        eng.wait_ge(attn_ok, it * QB + QB + 1)
                        eng.dma_start(y_dram[bass.ds(it * P, P), :], gate[:, META:L]).then_inc(attn_st, 16)
                    elif step == "conv" and a == 4:
                        eng.wait_ge(convg_ok, it + 2)
                        eng.dma_start(y_dram[bass.ds(it * P + HEADS * P, P), :], conv_y[:, :]).then_inc(convg_st, 16)
                    elif step == "decay":
                        eng.wait_ge(seg_ok, it * QB + max(a - 2, 0) + 1)
                        eng.dma_start(acum_b[:, a % 2, :, :],
                                      acum_dram[bass.ds(it * R, R), a * P:(a + 1) * P].partition_broadcast(P)).then_inc(acum_in[a % 2], 16)
                    elif step == "store_ssm":
                        eng.wait_ge(ys_ok, it * QB + QB + 1)
                        for t in range(2):
                            eng.dma_start(y_dram[bass.ds(it * GW + (2 * HEADS + t) * P, P), :], ys[:, t, :]).then_inc(ssm_st, 16)
                    elif step == "out_load":
                        eng.wait_ge(attn_st, 16 * HEADS + 16)
                        eng.wait_ge(s_done, HEADS * 2 * QB + 1)
                        eng.wait_ge(v_tr, HEADS + 1)
                        eng.wait_ge(w_lo_ok, HEADS * NT + 2)
                        load_out(0, a, a)

            iteration(-1, AHEAD)
            eng.wait_ge(acum_st, 16)
            with eng.Fori(0, HEADS - 1) as i:
                iteration(i, BODY)
            iteration(HEADS - 1, LAST)

            def load_group(half, g):
                for b in range(OB):
                    n = half * KO + OB * g + b
                    eng.wait_ge(y_lo_ok, n - OB + 2)
                    eng.wait_ge(wo_lo_ok, n - OB + 2)
                    load_out(half, OB * g + b, b)

            eng.wait_ge(convg_st, 16 * HEADS + 16)
            eng.wait_ge(ssm_st, 32 * HEADS + 16)
            eng.wait_ge(scan_done, HEADS * CH + 1)
            eng.wait_ge(g_ok, HEADS * QB + 1)
            eng.dma_start(w_fin, final_norm_w.partition_broadcast(P)).then_inc(x_res, 16)
            with eng.Fori(1, KO // OB) as g:
                load_group(0, g)
                eng.dma_start(h_res[:, bass.ds(2 * g - 2, 2), :], x_tiles[:, bass.ds(2 * g - 2, 2), :]).then_inc(x_res, 16)
            eng.dma_start(h_res[:, QB - 2:QB, :], x_tiles[:, QB - 2:QB, :]).then_inc(x_res, 16)
            with eng.Fori(0, KO // OB) as g:
                load_group(1, g)
            for t in range(QB):
                eng.wait_ge(f_ok, t + 1)
                eng.wait_ge(f0_ok, t + 1)
                eng.dma_start(out_rows[t * P:(t + 1) * P, :], h_res[:, t, :]).then_inc(out_st, 16)
            eng.wait_ge(out_st, 16 * QB)

        @block.gpsimd
        def _(eng):
            own = pool_own
            own(eng, eng.memset(ident[:, :], 0.0))
            own(eng, eng.memset(mask_b[:, :], 0.0))
            own(eng, eng.memset(tri[:, :], 1.0))
            own(eng, eng.memset(valid[:, :], 1.0))
            eng.affine_select(out=ident[:, :], in_=ident[:, :], compare_op=ALU.not_equal, fill=1.0, base=0,
                              pattern=[[-1, P]], channel_multiplier=1).then_inc(consts, 1)
            eng.affine_select(out=mask_b[:, :], in_=mask_b[:, :], compare_op=ALU.is_ge, fill=MASK, base=0,
                              pattern=[[-1, P]], channel_multiplier=1).then_inc(consts, 1)
            eng.affine_select(out=tri[:, :], in_=tri[:, :], compare_op=ALU.is_ge, fill=0.0, base=0,
                              pattern=[[1, P]], channel_multiplier=-1).then_inc(consts, 1)
            eng.affine_select(out=valid[:, :], in_=valid[:, :], compare_op=ALU.is_ge, fill=0.0, base=META - 1,
                              pattern=[[0, 1]], channel_multiplier=-1).then_inc(consts, 1)
            eng.memset(ones[:, :], 1.0).then_inc(consts, 1)
            eng.memset(m_half[:, :], -0.5).then_inc(consts, 1)
            eng.memset(u_hi[:, :, L:LP].bitcast(F32), 0.0).then_inc(consts, 1)
            eng.memset(u_lo[:, :, L:LP].bitcast(F32), 0.0).then_inc(consts, 1)
            eng.wait_ge(consts, 8)

            def power(n, to, of, rows_=P):
                return eng.tensor_tensor(to[0:rows_, n:n + 1], of[0:rows_, n:n + 1], m_half[0:rows_, :], ALU.pow)

            def low_w(n, b):
                eng.wait_ge(wo_hi_ok, n + 1)
                eng.tensor_tensor(wo_lo[:, b, :], wo_raw[:, b, :], wo_hi[:, b, :].bitcast(F32), ALU.subtract).then_inc(wo_lo_ok, 1)

            def iteration(i, steps):
                for step, a, d in steps:
                    it = i + d
                    if step == "split":
                        eng.wait_ge(w_hi_ok, it * NT + a + 1)
                        ks = slice(0, KD // 2 if a in SHARED else KD)
                        eng.tensor_tensor(w_lo[:, a % 2, ks, :], w_raw[:, a % 2, ks, :],
                                          w_hi[:, a % 2, ks, :].bitcast(F32), ALU.subtract).then_inc(w_lo_ok, 1)
                    elif step == "x_power":
                        eng.wait_ge(x_ms, a + 1)
                        power(a % XB, rs, ms, META if a == 0 else P).then_inc(x_rs, 1)
                    elif step == "w_dt":
                        eng.wait_ge(wd_hi_ok, 1)
                        eng.tensor_tensor(wd_lo[:, :, :], w_dt, wd_hi[:, :, :].bitcast(F32), ALU.subtract).then_inc(wd_lo_ok, 1)
                    elif step == "x_low":
                        ca, cb = token_cols(a)
                        src = (k_t, v_t)[a % 2][:, 0:KD * (cb - ca)].rearrange("p (k n) -> p k n", k=KD)
                        eng.wait_ge(u_hi_ok, a + 1)
                        ks = slice(0, KD // 2)
                        eng.tensor_tensor(u_lo[:, ks, ca:cb], src[:, ks], u_hi[:, ks, ca:cb].bitcast(F32), ALU.subtract).then_inc(u_lo_ok, 1)
                    elif step == "o_norm":
                        eng.wait_ge(o_ms_ok, it * QB + a + 2)
                        power(0, o_rs, o_ms).then_inc(o_rs_ok, 1)
                    elif step == "chunk" and a < CH - 1:
                        n = META if a == 0 else P
                        eng.wait_ge(xdt_ok, it * CH + a + 1)
                        eng.wait_ge(scan_done, it * CH + max(a - 1, 0) + 1)
                        eng.tensor_tensor(xdd[0:n, a % 2, :].rearrange("p (r d) -> p r d", r=R),
                                          xdt[0:n, a % 2, :].rearrange("p (r d) -> p r d", r=R),
                                          sg[0:n, 2, a, :].unsqueeze(2).to_broadcast([n, R, HD]), ALU.mult).then_inc(xdd_ok, 1)
                    elif step == "carry":
                        eng.wait_ge(state_ok, it * (CH - 1) + a + 1)
                        eng.tensor_tensor(state_d[:, :].rearrange("p (r d) -> p r d", r=R),
                                          state[:, :].rearrange("p (r d) -> p r d", r=R),
                                          sg[:, 4, a, :].unsqueeze(2).to_broadcast([P, R, HD]), ALU.mult).then_inc(sd_ok, 1)
                    elif step == "norm":
                        eng.wait_ge(z_ms_ok, it * QB + a + 1)
                        power(a % 2, z_rs, z_ms).then_inc(z_rs_ok, 1)
                    elif step == "out_w":
                        low_w(a, a)

            iteration(-1, AHEAD)
            with eng.Fori(0, HEADS - 1) as i:
                iteration(i, BODY)
            iteration(HEADS - 1, LAST)

            with eng.Fori(1, 2 * KO // OB) as g:
                for b in range(OB):
                    low_w(OB * g + b, b)
            for t in range(QB):
                eng.wait_ge(f_ms_ok, t + 1)
                power(t, f_rs, f_ms).then_inc(f_rs_ok, 1)

        @block.scalar
        def _(eng):
            def high_y(n, b):
                eng.wait_ge(yw_in[b], (n - b) * (32 // OB) + 32)
                eng.copy(y_hi[:, b, :], y_raw[:, b, :]).then_inc(y_hi_ok, 1)

            def high_w(n, b):
                eng.wait_ge(yw_in[b], (n - b) * (32 // OB) + 32)
                eng.copy(wo_hi[:, b, :], wo_raw[:, b, :]).then_inc(wo_hi_ok, 1)

            def iteration(i, steps):
                for step, a, d in steps:
                    it = i + d
                    if step == "split":
                        b = a % 2
                        free = it * PPI + {0: -PIECES, 1: 0, TCB: PZ + QB, TCC: PZ + QB}.get(a, first_piece(max(a - 1, 0)))
                        eng.wait_ge(w_in_ok[b], it * (16 * NT // 2) + 16 * (a // 2 + 1))
                        if a >= 2 or steps is not AHEAD:
                            eng.wait_ge(piece_done, free + 1)
                        eng.copy(w_hi[:, b, :, :], w_raw[:, b, :, :]).then_inc(w_hi_ok, 1)
                    elif step == "x_square":
                        n = META if a == 0 else P
                        at = a % XB
                        eng.wait_ge(x_in[at], 16 * (a // XB + 1))
                        if a >= XB:
                            eng.wait_ge(x_ms, a - XB + 1)
                        if a > 0:
                            eng.wait_ge(x_sq, a)
                        eng.activation(th_tile[0:n, 0:D], x_buf[at][0:n, 0:D], ACT.Square, accum_out=ss[0:n, at:at + 1]).then_inc(x_sq, 1)
                    elif step == "w_dt":
                        eng.wait_ge(params_in, 80)
                        eng.copy(wd_hi[:, :, :], w_dt).then_inc(wd_hi_ok, 1)
                    elif step == "x_high":
                        ca, cb = token_cols(a)
                        src = (k_t, v_t)[a % 2][:, 0:KD * (cb - ca)].rearrange("p (k n) -> p k n", k=KD)
                        eng.wait_ge(u_prod, a + 1)
                        eng.copy(u_hi[:, :, ca:cb], src).then_inc(u_hi_ok, 1)
                    elif step == "lambda":
                        eng.wait_ge(lam_sum, 1)
                        eng.activation(lam_s[:, 2:4], lam_s[:, 0:2], ACT.Exp).then_inc(lam_exp, 1)
                        eng.wait_ge(params_in, 80)
                        eng.activation(a_bc[:, :], a_bc[:, :], ACT.Exp).then_inc(lam_exp, 1)
                    elif step == "dt":
                        eng.wait_ge(dt_x, 1)
                        eng.activation(sp[:, 1, :], sp[:, 0, :], ACT.Abs).then_inc(dt_e, 1)
                        eng.wait_ge(dt_e, 1)
                        eng.activation(sp[:, 2, :], sp[:, 1, :], ACT.Exp, scale=-1.0).then_inc(dt_e, 1)
                    elif step == "dt_stat":
                        eng.wait_ge(stat_x, 1)
                        for n in (2, 3, 4):
                            ins = eng.activation(stat[:, n, :, :], stat[:, n, :, :], ACT.Exp)
                        ins.then_inc(stat_e, 1)
                    elif step == "piece":
                        t, tc = tile_of(a)
                        cols = slice(tc * PW, (tc + 1) * PW)
                        src = pb[a % 2][:, 0:PW]
                        if t not in (TK, TCH):
                            eng.wait_ge(piece_done, it * PPI + a + 2)
                        if t == TQ:
                            eng.wait_ge(s_done, it * 2 * QB + 1)
                            eng.mul(q_map[0][0:QK, cols], src[0:QK, :], QK ** -0.5)
                            eng.mul(q_map[1][QK:P, cols], src[QK:P, :], QK ** -0.5).then_inc(bank_free[a % 2], 1)
                        elif t == TV:
                            eng.wait_ge(v_tr, it + 1)
                            eng.copy(v_t[:, cols], src).then_inc(bank_free[a % 2], 1)
                        elif t == TCB:
                            eng.wait_ge(convg_ok, it + 1)
                            eng.copy(conv_b_s[:, cols], src).then_inc(bank_free[a % 2], 1)
                        elif t == TCC:
                            eng.wait_ge(convg_ok, it + 1)
                            eng.copy(conv_u[:, 2 + tc * PW:2 + (tc + 1) * PW], src).then_inc(bank_free[a % 2], 1)
                        elif t in (TG, TGC):
                            eng.activation(th_piece[:, a % 2, :], src, ACT.Tanh, scale=0.5).then_inc(th_ok, 1)
                        elif TXS0 <= t <= TC:
                            eng.wait_ge(raw_free, it * 4 + t - TXS0 + 1)
                            if t == TXS1:
                                eng.wait_ge(scan_done, it * CH + 1)
                            eng.copy(raws[(t - TXS0) % 2][:, 3 + tc * PW:3 + (tc + 1) * PW], src).then_inc(bank_free[a % 2], 1)
                    elif step == "gate_taps":
                        n = a - TXS0
                        eng.wait_ge(raw_free, it * 4 + n + 3)
                        dst = (xs[:, 0, :], xs[:, 1, :], b_t, c_t)[n]
                        eng.wait_ge(conv_ok, it * 4 + n + 1)
                        eng.activation(th_tile[:, :], dst, ACT.Tanh, scale=0.5).then_inc(thc_ok, 1)
                    elif step == "turn_v":
                        eng.wait_ge(v_blk_ok, it + 1)
                        eng.copy(v_blk[:, 4:8, :], t_ps[1][:, :])
                        eng.copy(v_meta, o_ps[0:META, 0:P]).then_inc(v_meta_ok, 1)
                    elif step == "exp":
                        s, m = a
                        nk = P * (s + 1) + META
                        eng.wait_ge(max_ok, it * 2 * QB + 2 * s + m + 1)
                        if m == 0:
                            eng.wait_ge(a_tr, it * QB + s + 1)
                        else:
                            eng.wait_ge(mix_ok, it * QB + s + 1)
                        eng.activation(prob[m][:, 0:nk], s_ps[:, 0:nk], ACT.Exp, bias=mx[:, m:m + 1],
                                       accum_out=psum_e[:, s % 2, m:m + 1]).then_inc(exp_ok, 1)
                    elif step == "turn":
                        eng.wait_ge(a_tr, it * QB + a + 2)
                        if a >= 4:
                            eng.copy(a_t[:, 4:a + 1, :], t_ps[1][:, 0:P * (a - 3)])
                        eng.copy(a_meta[:, :], o_ps[0:META, 0:P]).then_inc(a_m_ok, 1)
                    elif step == "values":
                        eng.wait_ge(o_c_ok, it * QB + a + 1)
                        eng.wait_ge(o_ms_ok, it * QB + a + 1)
                        eng.wait_ge(o_sq, it * QB + a + 1)
                        eng.activation(o_squares[:, :], o_n, ACT.Square, accum_out=o_ss[:, :]).then_inc(o_sq, 1)
                    elif step == "decay":
                        eng.wait_ge(seg_ok, it * QB + a + 1)
                        eng.activation(lmat[:, a % 2, :, :], lmat[:, a % 2, :, :], ACT.Exp).then_inc(l_ok, 1)
                    elif step == "z":
                        p = PZ + a - 1
                        eng.wait_ge(piece_done, it * PPI + p + 2)
                        eng.activation(th_piece[:, p % 2, 0:GW], pb[p % 2][:, 0:GW], ACT.Tanh, scale=0.5).then_inc(zth_ok, 1)
                    elif step == "norm":
                        n = it * QB + a
                        eng.wait_ge(y_gated, n + 1)
                        eng.wait_ge(z_ms_ok, n)
                        eng.activation(th_tile[:, 0:GW], y_n[:, a % 2, :], ACT.Square, accum_out=z_ss[:, a % 2:a % 2 + 1]).then_inc(z_sq, 1)
                        eng.wait_ge(z_rs_ok, n)
                        eng.activation(y_n[:, a % 2, :], y_n[:, a % 2, :], ACT.Copy, scale=z_rs[:, a % 2:a % 2 + 1]).then_inc(y_n_ok, 1)
                    elif step == "ssm_out":
                        n = it * QB + a
                        eng.wait_ge(y_tr, n + 1)
                        if a == 1:
                            eng.wait_ge(ssm_st, it * 32 + 16)
                        for t in range(2):
                            ins = eng.activation(ys[:, t, (a - 1) * P:a * P], yt_ps[:, t * P:(t + 1) * P], ACT.Copy, scale=par_sn[:, t:t + 1])
                        ins.then_inc(ys_ok, 1)
                    elif step == "out_w":
                        eng.wait_ge(piece_done, HEADS * PPI + 1 - (PIECES if a < 2 else 0))
                        high_w(a, a)
                    elif step == "out_y":
                        eng.wait_ge(piece_done, HEADS * PPI + 1)
                        high_y(a, a)

            iteration(-1, AHEAD)
            with eng.Fori(0, HEADS - 1) as i:
                iteration(i, BODY)
            iteration(HEADS - 1, LAST)

            with eng.Fori(1, KO // OB) as g:
                for b in range(OB):
                    eng.wait_ge(out_k, OB * g + b - OB + 2)
                    high_y(OB * g + b, b)
                    high_w(OB * g + b, b)
            for b in range(OB):
                if b < OB - 2:
                    eng.wait_ge(out_k, KO + b - OB + 2)
                else:
                    eng.wait_ge(out_bank, QB)
                high_y(KO + b, b)
                high_w(KO + b, b)
            for t in range(QB):
                eng.wait_ge(h_ok, t + 1)
                if t > 0:
                    eng.wait_ge(f_sq, t)
                eng.activation(th_tile[:, 0:HALF], h_res[:, t, 0:HALF], ACT.Square, accum_out=f_ss[:, t:t + 1]).then_inc(f_sq, 1)
            with eng.Fori(KO // OB + 1, 2 * KO // OB) as g:
                for b in range(OB):
                    eng.wait_ge(out_k, OB * g + b - OB)
                    high_y(OB * g + b, b)
                    high_w(OB * g + b, b)

            def finish(t):
                eng.wait_ge(f_rs_ok, t + 1)
                eng.wait_ge(hw_ok, t + 1)
                eng.activation(h_res[:, t, 0:HALF], h_res[:, t, 0:HALF], ACT.Copy, scale=f_rs[:, t:t + 1]).then_inc(f0_ok, 1)

            for t in range(QB):
                n = QB + t
                eng.wait_ge(h_ok, n + 1)
                eng.wait_ge(f_sq, n)
                eng.activation(th_tile[:, 0:HALF], h_res[:, t, HALF:D], ACT.Square, accum_out=f_ss[:, n:n + 1]).then_inc(f_sq, 1)
                if t > 0:
                    finish(t - 1)
            finish(QB - 1)

        @block.vector
        def _(eng):
            own = dve_own
            own(eng, eng.memset(raw[:, 0:3], 0.0))
            own(eng, eng.memset(conv_u[:, 0:2], 0.0))
            eng.memset(q_map[0][QK:P, :], 0.0)
            own(eng, eng.memset(q_map[1][0:QK, :], 0.0))
            eng.memset(dt_rows[:, META:P], 0.0)
            eng.wait_ge(consts, 8)
            own(eng, eng.tensor_copy(ident_b[:, :], ident[:, :]))
            def low_y(n, b):
                eng.wait_ge(y_hi_ok, n + 1)
                eng.tensor_tensor(y_lo[:, b, :], y_raw[:, b, :], y_hi[:, b, :].bitcast(F32), ALU.subtract).then_inc(y_lo_ok, 1)

            def iteration(i, steps):
                for step, a, d in steps:
                    it = i + d
                    if step == "parameters":
                        eng.wait_ge(par_tr, 1)
                        own(eng, eng.tensor_copy(par[:, :], o_ps[:, 0:R_END]))
                    elif step == "x_mean":
                        n = META if a == 0 else P
                        at = a % XB
                        eng.wait_ge(x_sq, a + 1)
                        if a >= XB:
                            eng.wait_ge(x_rs, a - XB + 1)
                        eng.tensor_scalar(ms[0:n, at:at + 1], ss[0:n, at:at + 1], 1.0 / D, EPS, ALU.mult, ALU.add).then_inc(x_ms, 1)
                    elif step == "x_scale":
                        n = META if a == 0 else P
                        at = a % XB
                        eng.wait_ge(x_rs, a + 1)
                        eng.tensor_scalar(x_buf[at][0:n, 0:D], x_buf[at][0:n, 0:D], rs[0:n, at:at + 1], None, ALU.mult).then_inc(x_n, 1)
                    elif step == "x_prod":
                        ca, cb = token_cols(a)
                        n = cb - ca
                        dst = (k_t, v_t)[a % 2][:, 0:KD * n].rearrange("p (k n) -> p k n", k=KD)
                        eng.wait_ge(x_tr, a + 1)
                        if a >= 2:
                            eng.wait_ge(u_lo_ok, a - 1)
                            eng.wait_ge(u_lo2_ok, a - 1)
                        eng.tensor_tensor(dst, u_ps[a % 2].rearrange("p (k n) -> p k n", k=KD)[:, :, 0:n],
                                          par[:, R_NW:R_AN].unsqueeze(2).to_broadcast([P, KD, n]), ALU.mult).then_inc(u_prod, 1)
                    elif step == "x_low2":
                        ca, cb = token_cols(a)
                        src = (k_t, v_t)[a % 2][:, 0:KD * (cb - ca)].rearrange("p (k n) -> p k n", k=KD)
                        eng.wait_ge(u_hi_ok, a + 1)
                        ks = slice(KD // 2, KD)
                        eng.tensor_tensor(u_lo[:, ks, ca:cb], src[:, ks], u_hi[:, ks, ca:cb].bitcast(F32), ALU.subtract).then_inc(u_lo2_ok, 1)
                    elif step == "lambda":
                        own(eng, eng.tensor_scalar(a_norm[:, :], par[:, R_AN:R_END], 0.5 * (1.0 - LAM_INIT), None, ALU.mult))
                        eng.wait_ge(params_in, 80)
                        own(eng, eng.tensor_scalar(d_bc[:, :], d_bc[:, :], 0.5, None, ALU.mult))
                        own(eng, eng.tensor_tensor(lam_p[:, :, :], lam_in[:, 0:4:2, :], lam_in[:, 1:4:2, :], ALU.mult))
                        eng.tensor_reduce(lam_s[:, 0:2], lam_p[:, :, :], AX.X, ALU.add).then_inc(lam_sum, 1)
                    elif step == "lambda_out":
                        eng.wait_ge(lam_exp, 1)
                        own(eng, eng.tensor_tensor(lam_s[:, 4:5], lam_s[:, 2:3], lam_s[:, 3:4], ALU.subtract))
                        eng.tensor_scalar(lam_s[:, 5:6], lam_s[:, 4:5], LAM_INIT, -1.0, ALU.add, ALU.mult).then_inc(lam_row, 1)
                        eng.wait_ge(lam_pe, 1)
                        eng.tensor_copy(n_lam[:, :], o_ps[:, 0:1]).then_inc(lam_ok, 1)
                        eng.wait_ge(lam_ok, 1)
                    elif step == "dt_piece":
                        eng.wait_ge(dt_pe, a + 1)
                        eng.wait_ge(params_in, 80)
                        src = dt_ps[a]
                        lo = META if a == 0 else 0
                        hi = min(L - a * PW, PW)
                        at = a * PW + P - META
                        if a == 0:
                            eng.tensor_scalar(dt_rows[:, 0:META], src[0:SH, 0:META], dt_bias, None, ALU.add)
                        eng.tensor_scalar(dt_rows[:, at + lo:at + hi], src[0:SH, lo:hi], dt_bias, None, ALU.add).then_inc(dt_row_ok, 1)
                    elif step == "dt":
                        eng.wait_ge(dt_tr, 1)
                        eng.tensor_copy(sp[:, 0, :], dt_ps[0][:, 0:CH * SH]).then_inc(dt_x, 1)
                        eng.wait_ge(dt_e, 2)
                        own(eng, eng.tensor_scalar(sp[:, 3, :], sp[:, 2, :], 2.0, None, ALU.add))
                        own(eng, eng.reciprocal(sp[:, 4, :], sp[:, 3, :]))
                        own(eng, eng.tensor_tensor(sp[:, 1, :], sp[:, 2, :], sp[:, 4, :], ALU.mult))
                        own(eng, eng.tensor_tensor(sp[:, 3, :], sp[:, 1, :], sp[:, 1, :], ALU.mult))
                        own(eng, eng.tensor_scalar(sp[:, 4, :], sp[:, 3, :], 1.0 / 17, None, ALU.mult))
                        for n in range(15, 1, -2):
                            own(eng, eng.scalar_tensor_tensor(sp[:, 4, :], sp[:, 4, :], 1.0 / n, sp[:, 3, :], ALU.add, ALU.mult))
                        own(eng, eng.scalar_tensor_tensor(sp[:, 4, :], sp[:, 4, :], 1.0, sp[:, 1, :], ALU.add, ALU.mult))
                        own(eng, eng.tensor_scalar(sp[:, 5, :], sp[:, 0, :], 0.0, None, ALU.max))
                        own(eng, eng.scalar_tensor_tensor(sp[:, 5, :], sp[:, 4, :], 2.0, sp[:, 5, :], ALU.mult, ALU.add))
                        own(eng, eng.tensor_scalar(sp[:, 5, 0:SH], sp[:, 5, 0:SH], valid[:, :], None, ALU.mult))
                        own(eng, eng.tensor_scalar(stat[:, 0, :, :], sp[:, 5, :], 0.5, None, ALU.mult))
                        eng.wait_ge(lam_exp, 2)
                        eng.scalar_tensor_tensor(sp[:, 4, :].rearrange("p (c h) -> p c h", c=CH), sp[:, 5, :].rearrange("p (c h) -> p c h", c=CH), -1.0,
                                                 a_bc[:, :].unsqueeze(1).to_broadcast([P, CH, SH]), ALU.mult, ALU.mult).then_inc(adt_ok, 1)
                    elif step == "dt_stat":
                        eng.wait_ge(cum_pe, 1)
                        eng.tensor_copy(stat[:, 1, :, :], o_ps[:, 0:CH * SH]).then_inc(acum_ok, 1)
                        eng.wait_ge(acum_ok, 1)
                        own(eng, eng.tensor_copy(stat[:, 4, :, :], o_ps[:, CH * SH:2 * CH * SH]))
                        own(eng, eng.tensor_copy(stat[:, 3, :, :], stat[:, 1, :, :]))
                        eng.tensor_tensor(stat[:, 2, :, :], stat[:, 4, :, :], stat[:, 1, :, :], ALU.subtract).then_inc(stat_x, 1)
                    elif step == "dt_row":
                        eng.wait_ge(acum_tr, 1)
                        eng.tensor_copy(dt_rows[:, 0:4 * P], ps[0:SH, 5, :])
                        eng.tensor_copy(dt_rows[:, 4 * P:8 * P], ps[0:SH, 6, :])
                        eng.tensor_copy(dt_rows[:, 8 * P:9 * P], ps[0:SH, 7, 0:P]).then_inc(acum_row, 1)
                        eng.wait_ge(stat_e, 1)
                        own(eng, eng.tensor_scalar(stat[:, 2:4, :, :], stat[:, 2:4, :, :], 0.5, None, ALU.mult))
                    elif step == "split" and a in SHARED:
                        ks = slice(KD // 2, KD)
                        eng.wait_ge(w_hi_ok, it * NT + a + 1)
                        eng.tensor_tensor(w_lo[:, a % 2, ks, :], w_raw[:, a % 2, ks, :],
                                          w_hi[:, a % 2, ks, :].bitcast(F32), ALU.subtract).then_inc(w_lo2_ok, 1)
                    elif step == "params":
                        eng.wait_ge(scan_done, it * CH + 1)
                        eng.wait_ge(g_ok, it * QB + 1)
                        eng.wait_ge(ys_ok, it * QB + 1)
                        taps = par[:, R_CW:R_CB].rearrange("p (j t) -> p j t", j=4)
                        eng.tensor_copy(par_cw[:, :, 0:2], taps[:, :, bass.ds(2 * it, 2)])
                        eng.tensor_copy(par_cw[:, :, 2:3], taps[:, :, bass.ds(it + XT, 1)])
                        eng.tensor_copy(par_cw[:, :, 3:4], taps[:, :, bass.ds(it + XT + HEADS, 1)])
                        eng.tensor_copy(par_cb[:, 0:2], par[:, bass.ds(2 * it + R_CB, 2)])
                        eng.tensor_copy(par_cb[:, 2:3], par[:, bass.ds(it + R_CB + XT, 1)])
                        eng.tensor_copy(par_cb[:, 3:4], par[:, bass.ds(it + R_CB + XT + HEADS, 1)])
                        eng.tensor_copy(par_sw[:, :], par[:, R_SW:R_SN].rearrange("p (j t) -> p j t", j=3)[:, :, bass.ds(i, 1)])
                        eng.tensor_scalar(par_sn[:, :], par[:, bass.ds(2 * it + R_SN, 2)], 0.5, None, ALU.mult)
                        eng.tensor_copy(dg[:, :], d_bc[:, bass.ds(R * it, R)])
                        own(eng, eng.tensor_copy(sg[:, :, :, :].rearrange("p s c r -> p (s c) r"),
                                                 stat[:, :, :, :].rearrange("p s c h -> p (s c) h")[:, :, bass.ds(R * it, R)]))
                        own(eng, eng.memset(raws[1][:, 0:3], 0.0))
                    elif step == "piece":
                        t, tc = tile_of(a)
                        cols = slice(tc * PW, (tc + 1) * PW)
                        src = pb[a % 2][:, 0:PW]
                        done = bank_free[a % 2]
                        if t == TK:
                            eng.wait_ge(piece_done, it * PPI + a + 2)
                            eng.wait_ge(s_done, it * 2 * QB + 1)
                            eng.tensor_copy(k_t[:, cols], src).then_inc(done, 1)
                        elif t == TG:
                            eng.wait_ge(attn_st, it * 16 + 16)
                            eng.wait_ge(th_ok, it * 6 + tc + 1)
                            eng.scalar_tensor_tensor(gate[:, cols], th_piece[:, a % 2, :], 1.0, src, ALU.add, ALU.mult).then_inc(done, 1)
                        elif t == TCH:
                            eng.wait_ge(piece_done, it * PPI + a + 2)
                            eng.wait_ge(bank_free[(a - PIECES) % 2], it * (PPI // 2) + (a - PIECES) // 2 + 2)
                            c2 = slice(2 + tc * PW, 2 + (tc + 1) * PW)
                            eng.tensor_tensor(conv_u[:, c2], src, conv_u[:, c2], ALU.mult).then_inc(done, 1)
                        elif t == TGC:
                            eng.wait_ge(th_ok, it * 6 + 3 + tc + 1)
                            eng.scalar_tensor_tensor(conv_g[:, cols], th_piece[:, a % 2, :], 1.0, src, ALU.add, ALU.mult).then_inc(done, 1)
                    elif step == "taps":
                        t, j = a
                        n = t - TXS0
                        dst = (xs[:, 0, :], xs[:, 1, :], b_t, c_t)[n]
                        src = raws[n % 2]
                        if j == 0:
                            for b in range(2):
                                eng.wait_ge(bank_free[b], it * (PPI // 2) + (PIECES * (t + 1) + 1 - b) // 2 + 1)
                            own(eng, eng.tensor_scalar(dst, src[:, 0:LP], par_cw[:, 0, n:n + 1], par_cb[:, n:n + 1], ALU.mult, ALU.add))
                        else:
                            ins = eng.scalar_tensor_tensor(dst, src[:, j:j + LP], par_cw[:, j, n:n + 1], dst, ALU.mult, ALU.add)
                            if j < 3:
                                own(eng, ins)
                            else:
                                ins.then_inc(raw_free, 1)
                    elif step == "gate_taps":
                        n = a - TXS0
                        dst = (xs[:, 0, :], xs[:, 1, :], b_t, c_t)[n]
                        eng.wait_ge(thc_ok, it * 4 + n + 1)
                        eng.scalar_tensor_tensor(dst, th_tile[:, :], 1.0, dst, ALU.add, ALU.mult).then_inc(conv_ok, 1)
                    elif step == "turn_v":
                        eng.wait_ge(v_tr, it + 2)
                        eng.tensor_copy(v_blk[:, 0:4, :], t_ps[0][:, :]).then_inc(v_blk_ok, 1)
                    elif step == "scores":
                        s, m = a
                        nk = P * (s + 1) + META
                        n = it * 2 * QB + 2 * s + m
                        eng.wait_ge(s_done, n + 2)
                        if s > 0:
                            eng.wait_ge(exp_ok, n)
                        eng.tensor_reduce(mx[:, m:m + 1], s_ps[:, 0:nk], AX.X, ALU.max, negate=True).then_inc(max_ok, 1)
                    elif step == "mix":
                        nk = P * (a + 1) + META
                        b = a % 2
                        eng.wait_ge(exp_ok, it * 2 * QB + 2 * a + 2 + 1)
                        own(eng, eng.reciprocal(rinv[:, b, :], psum_e[:, b, :]))
                        own(eng, eng.scalar_tensor_tensor(cmix[:, :], rinv[:, b, 1:2], psum_e[:, b, 0:1], n_lam[:, :], ALU.mult, ALU.mult))
                        eng.scalar_tensor_tensor(prob[0][:, 0:nk], prob[1][:, 0:nk], cmix[:, 0:1], prob[0][:, 0:nk],
                                                 ALU.mult, ALU.add).then_inc(mix_ok, 1)
                    elif step == "turn":
                        nb = min(a + 1, 4)
                        eng.wait_ge(a_tr, it * QB + a + 2)
                        eng.tensor_copy(a_t[:, 0:nb, :], t_ps[0][:, 0:nb * P]).then_inc(a_t_ok, 1)
                    elif step == "values":
                        b = a % 2
                        eng.wait_ge(o_done, it * QB + a + 1)
                        own(eng, eng.tensor_scalar(o_n, o_ps[:, P:2 * P], rinv[:, b, 0:1], O_TOP, ALU.mult, ALU.min))
                        eng.tensor_scalar(o_n, o_n, -O_TOP, O_TOP ** -0.5, ALU.max, ALU.mult).then_inc(o_c_ok, 1)
                    elif step == "o_norm":
                        n = it * QB + a
                        eng.wait_ge(o_sq, n + 2)
                        own(eng, eng.tensor_scalar(o_fit[:, :], o_ss[:, :], O_TOP, None, ALU.is_lt))
                        eng.tensor_scalar(o_ms[:, :], o_ss[:, :], 1.0 / P, EPS / O_TOP, ALU.mult, ALU.add).then_inc(o_ms_ok, 1)
                        eng.wait_ge(o_rs_ok, n + 1)
                        eng.tensor_scalar(o_n, o_n, o_rs[:, 0:1], o_fit[:, 0:1], ALU.mult, ALU.mult).then_inc(o_n_ok, 1)
                    elif step == "attn_out":
                        eng.wait_ge(o_tr, it * QB + a + 1)
                        ca, cb = token_cols(a + 1)
                        eng.scalar_tensor_tensor(gate[:, ca:cb], o_ps[:, 2 * P:3 * P], a_norm[:, 0:1], gate[:, ca:cb],
                                                 ALU.mult, ALU.mult).then_inc(attn_ok, 1)
                    elif step == "conv":
                        if a == 0:
                            eng.wait_ge(convg_st, it * 16 + 16)
                            own(eng, eng.tensor_scalar(conv_y[:, :], conv_u[:, META:META + T], par_sw[:, 0:1], None, ALU.mult))
                        elif a < 3:
                            own(eng, eng.scalar_tensor_tensor(conv_y[:, :], conv_u[:, META + a:META + a + T], par_sw[:, a:a + 1],
                                                              conv_y[:, :], ALU.mult, ALU.add))
                        elif a == 3:
                            own(eng, eng.tensor_tensor(conv_y[:, :], conv_y[:, :], conv_b_s[:, META:L], ALU.mult))
                        else:
                            eng.scalar_tensor_tensor(conv_y[:, :], conv_y[:, :], 0.5, conv_g[:, META:L], ALU.mult, ALU.mult).then_inc(convg_ok, 1)
                    elif step == "decay":
                        eng.wait_ge(acum_in[a % 2], it * 64 + 16 * ((a + 1) // 2))
                        eng.wait_ge(scan_done, it * CH + max(a - 1, 0) + 1)
                        for r in range(R):
                            ins = eng.tensor_scalar(lmat[:, a % 2, r, :], acum_b[:, a % 2, r, :], sg[:, 1, a, r:r + 1], 0.0,
                                                    ALU.subtract, ALU.min)
                        ins.then_inc(seg_ok, 1)
                    elif step == "chunk":
                        n = META if a == 0 else P
                        b = a % 2
                        eng.wait_ge(x_done, it * CH + a + 1)
                        eng.wait_ge(scan_done, it * CH + max(a - 1, 0) + 1)
                        eng.wait_ge(xdd_ok, it * (CH - 1) + max(a - 1, 0) + 1)
                        x3 = x_ps[b][0:n, 0:GW].rearrange("p (r d) -> p r d", r=R)
                        eng.tensor_tensor(xdt[0:n, b, :].rearrange("p (r d) -> p r d", r=R), x3,
                                          sg[0:n, 0, a, :].unsqueeze(2).to_broadcast([n, R, HD]), ALU.mult).then_inc(xdt_ok, 1)
                        if a > 0:
                            eng.tensor_tensor(xd[:, b, :].rearrange("p (r d) -> p r d", r=R), x3,
                                              dg[:, :].unsqueeze(2).to_broadcast([P, R, HD]), ALU.mult)
                            own(eng, eng.scalar_tensor_tensor(cbm[:, b, :], x_ps[b][:, 3 * P:4 * P], 0.25, tri[:, :], ALU.mult, ALU.mult))
                        eng.tensor_copy(b_n[0:n, b, :], x_ps[b][0:n, 2 * P:3 * P]).then_inc(x_free, 1)
                        if a > 0:
                            eng.wait_ge(l_ok, it * QB + a)
                            eng.wait_ge(scan_done, it * CH + a + 1)
                            eng.tensor_tensor(lmat[:, b, :, :], lmat[:, b, :, :],
                                              cbm[:, b, :].unsqueeze(1).to_broadcast([P, R, P]), ALU.mult).then_inc(g_ok, 1)
                    elif step == "z":
                        p = PZ + a - 1
                        eng.wait_ge(zth_ok, it * QB + a)
                        eng.wait_ge(a_tr, it * QB + QB + 1)
                        eng.wait_ge(mix_ok, it * QB + QB + 1)
                        eng.scalar_tensor_tensor(z_n[:, a - 1, :], th_piece[:, p % 2, 0:GW], 1.0, pb[p % 2][:, 0:GW],
                                                 ALU.add, ALU.mult).then_inc(bank_free[p % 2], 1)
                    elif step == "scan":
                        b = a % 2
                        eng.wait_ge(scan_done, it * CH + a + 2)
                        if a == 0:
                            eng.tensor_copy(state[:, :], st_ps[:, 0:GW]).then_inc(state_ok, 1)
                        elif a < CH - 1:
                            eng.wait_ge(sd_ok, it * (CH - 2) + a)
                            eng.tensor_tensor(state[:, :], state_d[:, :], st_ps[:, 0:GW], ALU.add).then_inc(state_ok, 1)
                        if a > 0:
                            own(eng, eng.tensor_tensor(y_a[:, :].rearrange("p (r d) -> p r d", r=R),
                                                       y_ps[b][:, GW:2 * GW].rearrange("p (r d) -> p r d", r=R),
                                                       sg[:, 3, a, :].unsqueeze(2).to_broadcast([P, R, HD]), ALU.mult))
                            own(eng, eng.tensor_tensor(y_a[:, :], y_ps[b][:, 0:GW], y_a[:, :], ALU.add))
                            own(eng, eng.tensor_tensor(y_a[:, :], y_a[:, :], xd[:, b, :], ALU.add))
                            eng.wait_ge(y_tr, it * QB + max(a - 2, 0) + 1)
                            p = PZ + a - 1
                            eng.wait_ge(bank_free[p % 2], it * (PPI // 2) + p // 2 + 2)
                            eng.tensor_tensor(y_n[:, b, :], y_a[:, :], z_n[:, a - 1, :], ALU.mult).then_inc(y_gated, 1)
                    elif step == "out_y":
                        low_y(a, a)
                    elif step == "norm":
                        eng.wait_ge(z_sq, it * QB + a)
                        eng.tensor_scalar(z_ms[:, a % 2:a % 2 + 1], z_ss[:, a % 2:a % 2 + 1], 0.25 / GW, EPS, ALU.mult, ALU.add).then_inc(z_ms_ok, 1)

            iteration(-1, AHEAD)
            eng.wait_ge(acum_st, 16)
            with eng.Fori(0, HEADS - 1) as i:
                own.begin(i)
                iteration(i, BODY)
                own.end()
            own.begin(HEADS - 1)
            iteration(HEADS - 1, LAST)
            own.end()

            def add_bank(half, t):
                eng.wait_ge(out_bank, half * QB + t + 1)
                h = h_res[:, t, half * HALF:(half + 1) * HALF]
                eng.tensor_tensor(h, ps[:, t, :], h, ALU.add).then_inc(h_ok, 1)

            with eng.Fori(1, KO // OB) as g:
                for b in range(OB):
                    low_y(OB * g + b, b)
            eng.wait_ge(x_res, 16 * (QB // 2 + 1))
            for t in range(QB):
                if t >= QB - 2:
                    low_y(KO + t - (QB - 2), t - (QB - 2))
                add_bank(0, t)
            for b in range(2, OB):
                low_y(KO + b, b)
            for t in range(QB):
                eng.wait_ge(f_sq, t + 1)
                eng.tensor_scalar(f_m0[:, t:t + 1], f_ss[:, t:t + 1], 1.0 / D, EPS, ALU.mult, ALU.add).then_inc(f_m0_ok, 1)
                eng.tensor_tensor(h_res[:, t, 0:HALF], h_res[:, t, 0:HALF], w_fin[:, 0:HALF], ALU.mult).then_inc(hw_ok, 1)
            with eng.Fori(KO // OB + 1, 2 * KO // OB) as g:
                for b in range(OB):
                    low_y(OB * g + b, b)

            def finish(t):
                eng.wait_ge(f_rs_ok, t + 1)
                eng.scalar_tensor_tensor(h_res[:, t, HALF:D], h_res[:, t, HALF:D], f_rs[:, t:t + 1], w_fin[:, HALF:D], ALU.mult, ALU.mult).then_inc(f_ok, 1)

            add_bank(1, 0)
            for t in range(QB):
                if t + 1 < QB:
                    add_bank(1, t + 1)
                eng.wait_ge(f_sq, QB + t + 1)
                eng.wait_ge(f_m0_ok, t + 1)
                eng.scalar_tensor_tensor(f_ms[:, t:t + 1], f_ss[:, QB + t:QB + t + 1], 1.0 / D, f_m0[:, t:t + 1], ALU.mult, ALU.add).then_inc(f_ms_ok, 1)
                if t > 0:
                    finish(t - 1)
            finish(QB - 1)

        @block.tensor
        def _(eng):
            def turn(dst, src, n=P):
                return eng.transpose(dst, src, ident[0:n, 0:n])

            eng.wait_ge(consts, 8)
            def project(dst, m, cols, wh, wl, ks=range(KD)):
                terms = [(wh, u_hi), (wh, u_lo), (wl, u_hi)]
                for k in ks:
                    for n, (w, u) in enumerate(terms):
                        ins = eng.matmul(dst, w[:, k, 0:m], u[:, k, cols], start=(k == 0 and n == 0), stop=(k == KD - 1 and n == 2))
                return ins

            def multiply(n, b, t, first, last):
                terms = [(y_hi, wo_hi), (y_hi, wo_lo), (y_lo, wo_hi)]
                for m, (y, w) in enumerate(terms):
                    ins = eng.matmul(ps[:, t, :], y[:, b, t * P:(t + 1) * P], w[:, b, :], start=(first and m == 0),
                                     stop=(last and m == 2), skip_group_check=True)
                return ins

            def out_tile(n, b, half, first, banks=range(QB)):
                eng.wait_ge(y_lo_ok, n + 2)
                eng.wait_ge(wo_lo_ok, n + 2)
                for t in banks:
                    if first and half == 1:
                        eng.wait_ge(h_ok, t + 1)
                    ins = multiply(n, b, t, first, False)
                if banks[-1] == QB - 1:
                    ins.then_inc(out_k, 1)

            def iteration(i, steps):
                for step, a, d in steps:
                    it = i + d
                    if step == "project":
                        p, h = a
                        t, tc = tile_of(p)
                        if (tc, h) == (0, 0):
                            eng.wait_ge(w_lo_ok, it * NT + t + 3)
                            if t in SHARED:
                                eng.wait_ge(w_lo2_ok, it * len(SHARED) + SHARED.index(t) + 1)
                        if steps is AHEAD and h == 0:
                            eng.wait_ge(u_lo_ok, tiles_of(tc))
                            eng.wait_ge(u_lo2_ok, tiles_of(tc))
                        if h == 0:
                            eng.wait_ge(bank_free[p % 2], it * (PPI // 2) + p // 2 + 1)
                        ins = project(pb[p % 2][:, 0:PW], P, slice(tc * PW, (tc + 1) * PW), w_hi[:, t % 2], w_lo[:, t % 2],
                                      range(h * KD // 2, (h + 1) * KD // 2))
                        if h == 1:
                            ins.then_inc(piece_done, 1)
                    elif step == "x_turn":
                        n = META if a == 0 else P
                        eng.wait_ge(x_n, a + 1)
                        if a >= 2:
                            eng.wait_ge(u_prod, a - 1)
                        for k in range(KD):
                            ins = turn(u_ps[a % 2][:, k * P:k * P + n], x_buf[a % XB][0:n, k * P:(k + 1) * P], n)
                        ins.then_inc(x_tr, 1)
                    elif step == "dt_piece":
                        if a == 0:
                            eng.wait_ge(wd_lo_ok, 1)
                        if a == 1:
                            eng.wait_ge(lam_ok, 1)
                        if a == 2:
                            eng.wait_ge(dt_row_ok, 1)
                        eng.wait_ge(u_lo_ok, tiles_of(a))
                        eng.wait_ge(u_lo2_ok, tiles_of(a))
                        project(dt_ps[a][0:SH, 0:PW], SH, slice(a * PW, (a + 1) * PW), wd_hi, wd_lo).then_inc(dt_pe, 1)
                    elif step == "dt":
                        eng.wait_ge(dt_row_ok, PIECES)
                        for c in range(CH):
                            ins = turn(dt_ps[0][:, c * SH:(c + 1) * SH], dt_rows[:, c * P:(c + 1) * P], SH)
                        ins.then_inc(dt_tr, 1)
                    elif step == "parameters":
                        eng.wait_ge(rows_in, 96)
                        turn(o_ps[:, 0:R_END], rows[0:R_END, :], R_END).then_inc(par_tr, 1)
                    elif step == "lambda_out":
                        eng.wait_ge(lam_row, 1)
                        eng.matmul(o_ps[:, 0:1], ones[0:1, :], lam_s[0:1, 5:6], start=True, stop=True).then_inc(lam_pe, 1)
                    elif step == "dt_cum":
                        eng.wait_ge(adt_ok, 1)
                        eng.wait_ge(lam_ok, 1)
                        eng.matmul(o_ps[:, 0:CH * SH], tri[:, :], sp[:, 4, :], start=True, stop=True)
                        eng.matmul(o_ps[:, CH * SH:2 * CH * SH], ones[:, :], sp[:, 4, :], start=True, stop=True).then_inc(cum_pe, 1)
                    elif step == "dt_row":
                        eng.wait_ge(acum_ok, 1)
                        eng.wait_ge(stat_x, 1)
                        for c in range(CH):
                            ins = turn(ps[0:SH, 5 + c // 4, (c % 4) * P:(c % 4 + 1) * P], stat[:, 1, c, :])
                        ins.then_inc(acum_tr, 1)
                    elif step == "turn_v":
                        for b in range(2):
                            eng.wait_ge(bank_free[b], it * (PPI // 2) + (PIECES * (TV + 1) + 1 - b) // 2 + 1)
                        eng.wait_ge(ys_ok, it * QB + 1)
                        eng.wait_ge(state_ok, it * (CH - 1) + 1)
                        eng.wait_ge(y_gated, it * QB + 1)
                        for n in range(QB):
                            turn(t_ps[n // 4][:, (n % 4) * P:(n % 4 + 1) * P], v_t[:, META + n * P:META + (n + 1) * P])
                        turn(o_ps[0:META, 0:P], v_t[:, 0:META]).then_inc(v_tr, 1)
                    elif step == "scores":
                        s, m = a
                        n = it * 2 * QB + 2 * s + m
                        if (s, m) == (0, 0):
                            for b in range(2):
                                eng.wait_ge(bank_free[b], it * (PPI // 2) + PIECES * (TK + 1) // 2 + 1)
                            eng.wait_ge(x_free, it * CH + 1)
                            eng.wait_ge(y_gated, it * QB + 1)
                        eng.wait_ge(exp_ok, n + 1)
                        qa, qb = token_cols(s + 1)
                        q = q_map[m][:, qa:qb]
                        for at in range(0, (s + 1) * P, 512):
                            w = min(512, (s + 1) * P - at)
                            last = at + w == (s + 1) * P
                            eng.matmul(s_ps[:, at:at + w], q, k_t[:, META + at:META + at + w], start=True, stop=not last)
                            if last:
                                eng.matmul(s_ps[:, s * P:(s + 1) * P], ident_b[:, :], mask_b[:, :], start=False, stop=True)
                        eng.matmul(s_ps[:, (s + 1) * P:(s + 1) * P + META], q, k_t[:, 0:META], start=True, stop=True).then_inc(s_done, 1)
                    elif step == "turn":
                        eng.wait_ge(mix_ok, it * QB + a + 2)
                        if a == 0:
                            eng.wait_ge(v_meta_ok, it + 1)
                            eng.wait_ge(v_blk_ok, it + 1)
                        eng.wait_ge(a_t_ok, it * QB + a + 1)
                        eng.wait_ge(a_m_ok, it * QB + a + 1)
                        eng.wait_ge(attn_ok, it * QB + a + 1)
                        for n in range(a + 1):
                            turn(t_ps[n // 4][:, (n % 4) * P:(n % 4 + 1) * P], prob[0][:, n * P:(n + 1) * P])
                        turn(o_ps[0:META, 0:P], prob[0][:, (a + 1) * P:(a + 1) * P + META]).then_inc(a_tr, 1)
                    elif step == "values":
                        eng.wait_ge(a_t_ok, it * QB + a + 2)
                        eng.wait_ge(a_m_ok, it * QB + a + 2)
                        for n in range(a + 1):
                            eng.matmul(o_ps[:, P:2 * P], a_t[:, n, :], v_blk[:, n, :], start=(n == 0), stop=False)
                        eng.matmul(o_ps[:, P:2 * P], a_meta[:, :], v_meta, start=False, stop=True).then_inc(o_done, 1)
                    elif step == "attn_out":
                        eng.wait_ge(o_n_ok, it * QB + a + 1)
                        turn(o_ps[:, 2 * P:3 * P], o_n).then_inc(o_tr, 1)
                    elif step == "chunk":
                        n = META if a == 0 else P
                        ca, cb = token_cols(a)
                        b = a % 2
                        if a == 0:
                            eng.wait_ge(conv_ok, it * 4 + 4 + 1)
                            eng.wait_ge(exp_ok, it * 2 * QB + 2 * QB + 1)
                        if a >= 2:
                            eng.wait_ge(x_free, it * CH + a)
                        for t in range(2):
                            turn(x_ps[b][0:n, t * P:(t + 1) * P], xs[:, t, ca:cb])
                        ins = turn(x_ps[b][0:n, 2 * P:3 * P], b_t[:, ca:cb])
                        if a > 0:
                            ins = eng.matmul(x_ps[b][:, 3 * P:4 * P], b_t[:, ca:cb], c_t[:, ca:cb], start=True, stop=True)
                        ins.then_inc(x_done, 1)
                    elif step == "z":
                        p = PZ + a - 1
                        ca, cb = token_cols(a)
                        if a == 1:
                            eng.wait_ge(w_lo_ok, it * NT + TZ1 + 3)
                            eng.wait_ge(w_lo2_ok, it * len(SHARED) + SHARED.index(TZ1) + 1)
                        eng.wait_ge(bank_free[p % 2], it * (PPI // 2) + p // 2 + 1)
                        terms = [(u_hi, w_hi), (u_hi, w_lo), (u_lo, w_hi)]
                        for k in range(KD):
                            for n, (u, w) in enumerate(terms):
                                ins = eng.matmul(pb[p % 2][:, 0:GW], u[:, k, ca:cb], w[:, :, k, :], start=(k == 0 and n == 0), stop=(k == KD - 1 and n == 2))
                        ins.then_inc(piece_done, 1)
                    elif step == "scan":
                        n = META if a == 0 else P
                        ca, cb = token_cols(a)
                        b = a % 2
                        if a == 0:
                            eng.wait_ge(attn_ok, it * QB + QB + 1)
                        if a > 0:
                            eng.wait_ge(y_gated, it * QB + max(a - 2, 0) + 1)
                            eng.wait_ge(g_ok, it * QB + a + 1)
                            for r in range(R):
                                eng.matmul(y_ps[b][:, r * HD:(r + 1) * HD], lmat[:, b, r, :], xdt[:, b, r * HD:(r + 1) * HD], start=True, stop=True)
                            eng.wait_ge(state_ok, it * (CH - 1) + a + 1)
                            ins = eng.matmul(y_ps[b][:, GW:2 * GW], c_t[:, ca:cb], state[:, :], start=True, stop=True)
                        if a < CH - 1:
                            eng.wait_ge(xdd_ok, it * (CH - 1) + a + 2)
                            eng.wait_ge(x_free, it * CH + a + 2)
                            ins = eng.matmul(st_ps[:, 0:GW], b_n[0:n, b, :], xdd[0:n, b, :], start=True, stop=True)
                        ins.then_inc(scan_done, 1)
                    elif step == "out_begin":
                        for b in range(2):
                            eng.wait_ge(bank_free[b], HEADS * PPI // 2 + 1)
                        eng.wait_ge(x_free, HEADS * CH + 1)
                        for b in range(2):
                            out_tile(b, b, 0, b == 0, range(QB // 2))
                    elif step == "ssm_out":
                        eng.wait_ge(y_n_ok, it * QB + a)
                        eng.wait_ge(ys_ok, it * QB + a)
                        turn(yt_ps[:, 0:P], y_n[:, a % 2, 0:P])
                        turn(yt_ps[:, P:2 * P], y_n[:, a % 2, P:2 * P]).then_inc(y_tr, 1)

            iteration(-1, AHEAD)
            eng.wait_ge(acum_row, 1)
            with eng.Fori(0, HEADS - 1) as i:
                iteration(i, BODY)
            iteration(HEADS - 1, LAST)

            eng.wait_ge(y_gated, HEADS * QB + 1)
            eng.wait_ge(ys_ok, HEADS * QB + 1)
            for half in range(2):
                for b in range(OB):
                    out_tile(half * KO + b, b, half, b == 0, range(QB // 2 if half == 0 and b < 2 else 0, QB))
                with eng.Fori(1, KO // OB - 1) as g:
                    for b in range(OB):
                        out_tile(half * KO + OB * g + b, b, half, False)
                at = (half + 1) * KO - OB
                for b in range(OB - 2):
                    out_tile(at + b, b, half, False)
                eng.wait_ge(y_lo_ok, at + OB + 1)
                eng.wait_ge(wo_lo_ok, at + OB + 1)
                for t in range(QB):
                    for b in range(OB - 2, OB):
                        ins = multiply(at + b, b, t, False, b == OB - 1)
                    ins.then_inc(out_bank, 1)


_INS = ["x", "meta_tokens", "norm_w", "w_in", "w_out", "attn_lambda", "attn_norm_w", "sconv_w", "ssm_conv_w",
        "ssm_conv_b", "ssm_a_log", "ssm_dt_bias", "ssm_d", "ssm_norm_w", "final_norm_w"]


def kernel(**inputs):
    import concourse.bacc as bacc
    from concourse.bass_utils import run_bass_kernel_spmd

    nc = bacc.Bacc("TRN2", target_bir_lowering=False, num_devices=1)
    arrays, args = {}, []
    for name in _INS:
        a = np.ascontiguousarray(inputs[name])
        arrays[f"in_{name}"] = a
        args.append(nc.dram_tensor(f"in_{name}", a.shape, mybir.dt.from_np(a.dtype), kind="ExternalInput").ap())
    args.append(nc.dram_tensor("out_0", (1, T, D), F32, kind="ExternalOutput").ap())
    args.append(nc.dram_tensor("y_scratch", (2 * D, T), F32, kind="Internal").ap())
    args.append(nc.dram_tensor("acum_scratch", (SH, CH * P), F32, kind="Internal").ap())
    build(nc, *args)
    r = run_bass_kernel_spmd(nc, [arrays], core_ids=[0])
    return r.results[0]["out_0"]
```
